# Optimizing a Trainium2 kernel written in Bass

```python
import math
import jax, jax.numpy as jnp
from jax import lax
import numpy as np

D_MODEL = 1024
BATCH = 1
SEQ = 256
DEPTH = 2

CTX_LEN = 256
GRID_W = 64
N_HEADS = 8
HEAD_DIM = 64
ATT_W = N_HEADS * HEAD_DIM
WIN_ROWS = 8
WIN_COLS = 16
HY_W = 512
HY_ORDER = 2
HY_SHORT = 3
HY_EMB = 33
HY_BANDS = (HY_EMB - 1) // 2
HY_FILT = 64
HY_DECAY_TARGET = 1e-2
HY_FAST_PCT = 0.3
HY_SLOW_PCT = 1.5
HY_MAX_DECAY = math.log(HY_DECAY_TARGET) / HY_FAST_PCT
HY_MIN_DECAY = math.log(HY_DECAY_TARGET) / HY_SLOW_PCT
HY_DECAY_SHIFT = 0.05
PROJ_W = 3 * ATT_W + 3 * HY_W + 2 * D_MODEL
D_FF = 2816
N_EXPERTS = 8
TOP_K = 2
N_DENSE = (DEPTH + 1) // 2
N_MOE = DEPTH // 2
N_MOD = 6
EPS = 1e-6

kernel_name = "hybrid_na_hyena_moe_dit_block"

def rmsnorm(x, g):
    xf = x.astype(jnp.float32)
    y = xf * lax.rsqrt(jnp.mean(xf * xf, axis=-1, keepdims=True) + EPS)
    return (y * g.astype(jnp.float32)).astype(x.dtype)

def modulate(h, shift, scale):
    return h * (1.0 + scale) + shift

def split_proj(p):
    idx = [ATT_W, 2 * ATT_W, 3 * ATT_W, 3 * ATT_W + 3 * HY_W, 3 * ATT_W + 3 * HY_W + D_MODEL]
    return jnp.split(p, idx, axis=-1)

def heads(t):
    return t.reshape(*t.shape[:-1], N_HEADS, HEAD_DIM)

def neighbourhood_attention(q, k, v, k_ctx, v_ctx, rpb):
    B, L, H, Dh = q.shape
    rows = L // GRID_W
    kr = min(WIN_ROWS, rows)
    qg = q.reshape(B, rows, GRID_W, H, Dh) * (Dh ** -0.5)
    kg = k.reshape(B, rows, GRID_W, H, Dh)
    vg = v.reshape(B, rows, GRID_W, H, Dh)
    r = jnp.arange(rows)
    row_idx = jnp.clip(r - kr // 2, 0, rows - kr)[:, None] + jnp.arange(kr)[None, :]
    k_blk = jnp.take(kg, row_idx, axis=1)
    v_blk = jnp.take(vg, row_idx, axis=1)
    col = jnp.arange(GRID_W)
    c0 = jnp.clip(col - WIN_COLS // 2, 0, GRID_W - WIN_COLS)
    valid = (col[None, :] >= c0[:, None]) & (col[None, :] < c0[:, None] + WIN_COLS)
    dr = row_idx - r[:, None] + (WIN_ROWS - 1)
    dc = jnp.clip(col[None, :] - col[:, None] + (WIN_COLS - 1), 0, 2 * WIN_COLS - 2)
    bias = rpb[:, dr[:, None, :, None], dc[None, :, None, :]]
    s_loc = jnp.einsum('brqhd,brikhd->bhrqik', qg, k_blk).astype(jnp.float32)
    s_loc = jnp.where(valid[:, None, :], s_loc + bias.astype(jnp.float32), -jnp.inf)
    s_loc = s_loc.reshape(B, H, rows, GRID_W, kr * GRID_W)
    s_ctx = jnp.einsum('brqhd,bchd->bhrqc', qg, k_ctx).astype(jnp.float32)
    p = jax.nn.softmax(jnp.concatenate([s_loc, s_ctx], axis=-1), axis=-1).astype(q.dtype)
    p_loc = p[..., :kr * GRID_W].reshape(B, H, rows, GRID_W, kr, GRID_W)
    p_ctx = p[..., kr * GRID_W:]
    o = (jnp.einsum('bhrqik,brikhd->brqhd', p_loc, v_blk)
         + jnp.einsum('bhrqc,bchd->brqhd', p_ctx, v_ctx))
    return o.reshape(B, L, H * Dh)

def context_attention(q, k, v):
    B, C, H, Dh = q.shape
    s = jnp.einsum('bqhd,bkhd->bhqk', q * (Dh ** -0.5), k).astype(jnp.float32)
    p = jax.nn.softmax(s, axis=-1).astype(q.dtype)
    return jnp.einsum('bhqk,bkhd->bqhd', p, v).reshape(B, C, H * Dh)

def short_conv(u, w, b):
    L = u.shape[1]
    pad = HY_SHORT // 2
    up = jnp.pad(u, ((0, 0), (pad, HY_SHORT - 1 - pad), (0, 0)))
    return sum(up[:, j:j + L] * w[j] for j in range(HY_SHORT)) + b

def implicit_filters(L, w1, b1, w2, b2, w3, freq):
    f32 = jnp.float32
    pos = jnp.arange(L, dtype=f32)
    t = pos / max(L - 1, 1)
    bands = jnp.linspace(1e-4, HY_BANDS - 1, HY_BANDS, dtype=f32)
    ang = (2.0 * math.pi / L) * pos[:, None] * bands[None, :]
    z = jnp.concatenate([t[:, None], jnp.cos(ang), -jnp.sin(ang)], axis=-1)
    a = jnp.sin(freq[0].astype(f32) * (z @ w1.astype(f32) + b1.astype(f32)))
    a = jnp.sin(freq[1].astype(f32) * (a @ w2.astype(f32) + b2.astype(f32)))
    h = a @ w3.astype(f32)
    dist = jnp.abs(pos - L // 2) * (2.0 / L)
    rates = jnp.abs(jnp.linspace(HY_MIN_DECAY, HY_MAX_DECAY, HY_ORDER * HY_W, dtype=f32))
    h = h * (jnp.exp(-dist[:, None] * rates[None, :]) + HY_DECAY_SHIFT)
    return h.reshape(L, HY_ORDER, HY_W).transpose(1, 0, 2)

def fft_long_conv(u, h, bias):
    L = u.shape[1]
    uf = u.astype(jnp.float32)
    spec = jnp.fft.rfft(uf, n=2 * L, axis=1) * jnp.fft.rfft(h, n=2 * L, axis=0)[None]
    y = jnp.fft.irfft(spec, n=2 * L, axis=1)[:, L // 2:L // 2 + L]
    return (y + uf * bias.astype(jnp.float32)).astype(u.dtype)

def hyena(u, conv_w, conv_b, w1, b1, w2, b2, w3, freq, bias):
    L = u.shape[1]
    u = short_conv(u, conv_w, conv_b)
    v, x1, x2 = jnp.split(u, 3, axis=-1)
    h = implicit_filters(L, w1, b1, w2, b2, w3, freq)
    z = x1 * fft_long_conv(v, h[0], bias[0])
    return x2 * fft_long_conv(z, h[1], bias[1])

def merge(o_att, o_hy, ga, gb, w_pa, w_pb, w_o):
    return (jax.nn.sigmoid(ga) * (o_att @ w_pa) + jax.nn.sigmoid(gb) * (o_hy @ w_pb)) @ w_o

def swiglu(h, w1, w3, w2):
    return (jax.nn.silu(h @ w1) * (h @ w3)) @ w2

def channel_mixer(h, l, ffn_w1, ffn_w3, ffn_w2, moe_router, moe_w1, moe_w3, moe_w2):
    i = l // 2
    if l % 2 == 0:
        return swiglu(h, ffn_w1[i], ffn_w3[i], ffn_w2[i])
    logits = (h @ moe_router[i]).astype(jnp.float32)
    top_val, top_idx = lax.top_k(logits, TOP_K)
    gate = jax.nn.softmax(top_val, axis=-1)
    weight = jnp.einsum('...k,...ke->...e', gate,
                        jax.nn.one_hot(top_idx, N_EXPERTS, dtype=jnp.float32)).astype(h.dtype)
    out = jnp.zeros_like(h)
    for e in range(N_EXPERTS):
        out = out + weight[..., e:e + 1] * swiglu(h, moe_w1[i, e], moe_w3[i, e], moe_w2[i, e])
    return out

def setup_inputs(seed: int = 0) -> dict:
    key = jax.random.key(seed)
    ks = jax.random.split(key, 32)
    f32 = jnp.float32

    def nrm(k, shape, s):
        return s * jax.random.normal(k, shape, f32)

    D = D_MODEL
    return {
        'x': nrm(ks[0], (BATCH, SEQ, D), 1.0),
        'c': nrm(ks[1], (BATCH, D), 1.0),
        'ctx': nrm(ks[2], (BATCH, CTX_LEN, D), 1.0),
        'c_ctx': nrm(ks[3], (D,), 1.0),
        'w_mod': nrm(ks[4], (DEPTH, D, N_MOD * D), 0.5 * D ** -0.5),
        'b_mod': nrm(ks[5], (DEPTH, N_MOD * D), 0.02),
        'norm1_g': 1.0 + nrm(ks[6], (DEPTH, D), 0.02),
        'norm2_g': 1.0 + nrm(ks[7], (DEPTH, D), 0.02),
        'w_in': nrm(ks[8], (DEPTH, D, PROJ_W), D ** -0.5),
        'rpb': nrm(ks[9], (DEPTH, N_HEADS, 2 * WIN_ROWS - 1, 2 * WIN_COLS - 1), 0.1),
        'hy_conv_w': nrm(ks[10], (DEPTH, HY_SHORT, 3 * HY_W), HY_SHORT ** -0.5),
        'hy_conv_b': nrm(ks[11], (DEPTH, 3 * HY_W), 0.02),
        'hy_w1': nrm(ks[12], (DEPTH, HY_EMB, HY_FILT), HY_EMB ** -0.5),
        'hy_b1': nrm(ks[13], (DEPTH, HY_FILT), 0.1),
        'hy_w2': nrm(ks[14], (DEPTH, HY_FILT, HY_FILT), HY_FILT ** -0.5),
        'hy_b2': nrm(ks[15], (DEPTH, HY_FILT), 0.1),
        'hy_w3': nrm(ks[16], (DEPTH, HY_FILT, HY_ORDER * HY_W), 0.05 * HY_FILT ** -0.5),
        'hy_freq': 1.0 + nrm(ks[17], (DEPTH, 2, HY_FILT), 0.02),
        'hy_bias': nrm(ks[18], (DEPTH, HY_ORDER, HY_W), 0.5),
        'w_pa': nrm(ks[19], (DEPTH, ATT_W, D), ATT_W ** -0.5),
        'w_pb': nrm(ks[20], (DEPTH, HY_W, D), HY_W ** -0.5),
        'w_o': nrm(ks[21], (DEPTH, D, D), D ** -0.5),
        'ffn_w1': nrm(ks[22], (N_DENSE, D, D_FF), D ** -0.5),
        'ffn_w3': nrm(ks[23], (N_DENSE, D, D_FF), D ** -0.5),
        'ffn_w2': nrm(ks[24], (N_DENSE, D_FF, D), D_FF ** -0.5),
        'moe_router': nrm(ks[25], (N_MOE, D, N_EXPERTS), D ** -0.5),
        'moe_w1': nrm(ks[26], (N_MOE, N_EXPERTS, D, D_FF), D ** -0.5),
        'moe_w3': nrm(ks[27], (N_MOE, N_EXPERTS, D, D_FF), D ** -0.5),
        'moe_w2': nrm(ks[28], (N_MOE, N_EXPERTS, D_FF, D), D_FF ** -0.5),
        'final_g': 1.0 + nrm(ks[29], (D,), 0.02),
    }

def reference(x, c, ctx, c_ctx, w_mod, b_mod, norm1_g, norm2_g, w_in, rpb, hy_conv_w, hy_conv_b,
              hy_w1, hy_b1, hy_w2, hy_b2, hy_w3, hy_freq, hy_bias, w_pa, w_pb, w_o,
              ffn_w1, ffn_w3, ffn_w2, moe_router, moe_w1, moe_w3, moe_w2, final_g):
    s_lat = jax.nn.silu(c)[:, None, :]
    s_ctx = jax.nn.silu(c_ctx)[None, None, :]
    xl, xc = x, ctx
    for l in range(DEPTH):
        last = l == DEPTH - 1
        mod_l = jnp.split(s_lat @ w_mod[l] + b_mod[l], N_MOD, axis=-1)
        mod_c = jnp.split(s_ctx @ w_mod[l] + b_mod[l], N_MOD, axis=-1)
        hy_l = (hy_conv_w[l], hy_conv_b[l], hy_w1[l], hy_b1[l], hy_w2[l], hy_b2[l], hy_w3[l],
                hy_freq[l], hy_bias[l])

        hc = modulate(rmsnorm(xc, norm1_g[l]), mod_c[0], mod_c[1])
        if last:
            k_c, v_c = jnp.split(hc @ w_in[l, :, ATT_W:3 * ATT_W], 2, axis=-1)
        else:
            q_c, k_c, v_c, u_c, ga_c, gb_c = split_proj(hc @ w_in[l])
            mix_c = merge(context_attention(heads(q_c), heads(k_c), heads(v_c)), hyena(u_c, *hy_l),
                          ga_c, gb_c, w_pa[l], w_pb[l], w_o[l])

        hl = modulate(rmsnorm(xl, norm1_g[l]), mod_l[0], mod_l[1])
        q_l, k_l, v_l, u_l, ga_l, gb_l = split_proj(hl @ w_in[l])
        o_att = neighbourhood_attention(heads(q_l), heads(k_l), heads(v_l), heads(k_c), heads(v_c), rpb[l])
        o_hy = hyena(u_l, *hy_l)
        xl = xl + mod_l[2] * merge(o_att, o_hy, ga_l, gb_l, w_pa[l], w_pb[l], w_o[l])

        hl = modulate(rmsnorm(xl, norm2_g[l]), mod_l[3], mod_l[4])
        xl = xl + mod_l[5] * channel_mixer(hl, l, ffn_w1, ffn_w3, ffn_w2, moe_router, moe_w1, moe_w3, moe_w2)
        if not last:
            xc = xc + mod_c[2] * mix_c
            hc = modulate(rmsnorm(xc, norm2_g[l]), mod_c[3], mod_c[4])
            xc = xc + mod_c[5] * channel_mixer(hc, l, ffn_w1, ffn_w3, ffn_w2, moe_router, moe_w1, moe_w3, moe_w2)
    return rmsnorm(xl, final_g)


_drawn_inputs = setup_inputs


def setup_inputs(seed=0):
    import zlib

    import numpy as np

    out = dict(_drawn_inputs(seed))
    spreads = {}
    factors = {'norm1_g': 6.966,
     'norm2_g': 15.917,
     'rpb': 48.185,
     'hy_conv_b': 8.0,
     'hy_b1': 3.435,
     'hy_b2': 2.899,
     'hy_freq': 8.0,
     'final_g': 8.87}
    for name, (base, spread) in spreads.items():
        noise = np.random.default_rng([zlib.crc32(name.encode()), seed]).standard_normal(out[name].shape)
        drawn = base * np.exp(spread * noise) if base else spread * noise
        out[name] = __import__('jax').numpy.asarray(drawn.astype(out[name].dtype))
    for name, factor in factors.items():
        out[name] = (out[name] * factor).astype(out[name].dtype)
    return out
```

```python
import math
from contextlib import ExitStack

import numpy as np
import concourse.bass as bass
from concourse import mybir

F32 = mybir.dt.float32
R32 = mybir.dt.float32r
U32 = mybir.dt.uint32
ALU = mybir.AluOpType
ACT = mybir.ActivationFunctionType
AX = mybir.AxisListType.X

P = 128
D = 1024
DK = D // P
L = 256
TOK = 2 * L
PROJ = 5120
ATT_W, HY_W = 512, 512
OFF_U, OFF_GA, OFF_GB = 1536, 3072, 4096
HEADS, HD = 8, 64
GRID, WIN = 64, 16
RPB_R, RPB_C = 15, 31
FF = 2816
FK = FF // P
NE = 8
BLK = 256
NB = FF // BLK
NFFT = 384
BINS = 96
EPS = 1e-6
SCALE = HD ** -0.5
NEG = -1e30
MAGIC = 1.5 * 2.0 ** 23
TWO_PI_PARTS = (6.28125, 0.0019350051879882812, 3.0199157663446036e-07)
PI_CLIP = 3.1415925
TAPB = (0, 1, 5, 6)
N_SMALL, N_FILT = 11, 9

MOD_U, U_U, QKV_U, MERGE_U, WO_U, UP_U, DOWN_U = 24, 6, 6, 12, 4, 22, 16
SHIFT1, SCALE1, GATE1, SHIFT2, SCALE2, GATE2 = range(6)


def unit_bases():
    base, n = [{}, {}], 0
    for l in range(2):
        stages = [("mod", MOD_U), ("u", U_U), ("qkv", QKV_U), ("merge", MERGE_U), ("wo", WO_U)]
        if l == 0:
            stages += [("up", UP_U), ("down", DOWN_U)]
        for name, count in stages:
            base[l][name] = n
            n += count
    return base, n


def build(nc, t, out):
    base, n_units = unit_bases()
    top = ExitStack()
    with top:
        def sem(name):
            return top.enter_context(nc.semaphore(name))

        def sb(stack, name, shape, dt=F32):
            return stack.enter_context(nc.sbuf_tensor(name, shape, dt))

        X = sb(top, "x_residual", [P, DK, TOK])
        ident = sb(top, "ident", [P, P])
        flip = sb(top, "flip", [P, P])
        ones = sb(top, "ones", [P, P])
        eps = sb(top, "eps", [P, 1])
        cvec = sb(top, "cvec", [P, DK, 2])
        svec = sb(top, "svec", [P, DK, 2])
        SH = sb(top, "silu_c_hi", [P, DK, 2], R32)
        SL = sb(top, "silu_c_lo", [P, DK, 2], R32)
        bmod = sb(top, "b_mod", [P, 2, 48])
        g1 = sb(top, "norm1_g", [P, 2, DK])
        g2 = sb(top, "norm2_g", [P, 2, DK])
        gf = sb(top, "final_g", [P, DK])
        cw = sb(top, "conv_w", [P, 2, 3, 12])
        cb = sb(top, "conv_b", [P, 2, 12])
        hyb = sb(top, "hyena_bias", [P, 2, 2, 4])
        mod = sb(top, "modulation", [P, 48, 2])
        na1 = sb(top, "norm1_scale", [P, DK, 2])
        na2 = sb(top, "norm2_scale", [P, DK, 2])
        rs = sb(top, "rms", [P, TOK])
        sq = sb(top, "squares", [P, 2, TOK])
        router = sb(top, "router", [P, DK, NE])
        RTH = sb(top, "router_hi", [P, DK, NE], R32)
        RTL = sb(top, "router_lo", [P, DK, NE], R32)

        PS = top.enter_context(nc.psum_tensor("psum", [P, 8, 512], F32))

        st = ExitStack()
        raw = sb(st, "raw_units", [P, 2, 2048])
        WH = sb(st, "units_hi", [P, 2, 2048], R32)
        WL = sb(st, "units_lo", [P, 2, 2048], R32)
        HH = sb(st, "h_hi", [P, DK, TOK], R32)
        HL = sb(st, "h_lo", [P, DK, TOK], R32)
        mix = ExitStack()
        OHH = sb(mix, "hyena_out_hi", [P, 4, TOK], R32)
        OHL = sb(mix, "hyena_out_lo", [P, 4, TOK], R32)
        hy = ExitStack()
        spec = sb(hy, "filter_spectra", [BINS, 2, 5, HY_W])
        dftf = sb(hy, "dft_forward", [P, 2, 4 * BINS])
        dftk = sb(hy, "dft_filter", [P, 2, 5 * BINS])
        dfti = sb(hy, "dft_inverse", [BINS, 4, L])
        U = sb(hy, "hyena_u", [P, 12, TOK])
        fl = ExitStack()
        posT = sb(fl, "positions", [33, L])
        decay = sb(fl, "decay", [P, 2, 2, HY_W])
        fw1 = sb(fl, "filter_w1", [33, 64])
        fw2 = sb(fl, "filter_w2", [64, 64])
        fw3 = sb(fl, "filter_w3", [64, 2, HY_W])
        fb = sb(fl, "filter_vectors", [64, 4])
        arg = sb(fl, "sine_argument", [64, 2, L])
        turns = sb(fl, "sine_turns", [64, L])
        act1 = sb(fl, "filter_act", [64, 2, L])
        taps = sb(fl, "filter_taps", [P, 2, HY_W])
        fl.close()
        cv = ExitStack()
        VT = sb(cv, "tokens_major", [P, 2, HY_W])
        Y = sb(cv, "product_spectrum", [BINS, 4, HY_W])
        pt = sb(cv, "product_terms", [BINS, 2, HY_W])
        zt = sb(cv, "conv_sum", [P, 4, L])
        cv.close()
        hy.close()
        OAH = sb(mix, "att_out_hi", [P, 4, TOK], R32)
        OAL = sb(mix, "att_out_lo", [P, 4, TOK], R32)
        at = ExitStack()
        QK = sb(at, "qk", [P, 8, TOK])
        V = sb(at, "v", [P, 4, ATT_W])
        bias = sb(at, "att_bias", [P, HEADS, 6 * GRID])
        mask = sb(at, "att_mask", [P, 6 * GRID])
        S = sb(at, "scores", [P, 2, TOK])
        nmax = sb(at, "neg_max", [P, 32])
        psums = sb(at, "prob_sums", [P, 32])
        rsum = sb(at, "recip_sums", [P, 32])
        PT = sb(at, "probs_T", [P, 2, TOK])
        OT = sb(at, "att_tokens_major", [P, 4, ATT_W])
        at.close()
        mg = ExitStack()
        MH = sb(mg, "merged_hi", [P, DK, TOK], R32)
        ML = sb(mg, "merged_lo", [P, DK, TOK], R32)
        sga = sb(mg, "sig_a", [P, 2, TOK])
        sgb = sb(mg, "sig_b", [P, 2, TOK])
        mg.close()
        mix.close()
        ff = ExitStack()
        MDH = sb(ff, "mid_hi", [P, FK, TOK], R32)
        MDL = sb(ff, "mid_lo", [P, FK, TOK], R32)
        sff = sb(ff, "silu_ff", [P, 2, TOK])
        ff.close()
        st.close()
        mo = ExitStack()
        eraw = sb(mo, "expert_raw", [P, 6, 2048])
        EH = sb(mo, "expert_hi", [P, 3, 2048], R32)
        EL = sb(mo, "expert_lo", [P, 3, 2048], R32)
        RH = sb(mo, "moe_h_hi", [P, DK, L], R32)
        RL = sb(mo, "moe_h_lo", [P, DK, L], R32)
        mo_h = sb(mo, "moe_h", [P, DK, L])
        mo_ht = sb(mo, "moe_h_tokens", [P, 2, D])
        sel = sb(mo, "select", [P, 2, NE, P])
        selw = sb(mo, "select_weighted", [P, 2, NE, P])
        selT = sb(mo, "scatter", [P, NE, L])
        GH = sb(mo, "gathered_hi", [P, DK, P], R32)
        GL = sb(mo, "gathered_lo", [P, DK, P], R32)
        sil = sb(mo, "silu_block", [P, BLK])
        mid = sb(mo, "mid_block", [P, BLK])
        TH = sb(mo, "midT_hi", [P, 2, P], R32)
        TL = sb(mo, "midT_lo", [P, 2, P], R32)
        yexp = sb(mo, "expert_out", [P, D])
        logits = sb(mo, "logits", [P, 2, NE])
        tv = sb(mo, "top_values", [P, 2, 8])
        ti = sb(mo, "top_index", [P, 2, 8], U32)
        tif = sb(mo, "top_index_f", [P, 2, 8])
        gt = sb(mo, "top_gates", [P, 2, 4])
        oh = sb(mo, "one_hot", [P, 2, 4, NE])
        msk = sb(mo, "chosen", [P, 2, NE])
        wex = sb(mo, "expert_weight", [P, 2, NE])
        rank = sb(mo, "rank", [P, 2, NE])
        tri = sb(mo, "before", [P, P])
        iot = sb(mo, "iota", [P, L])
        mo.close()

        consts_in = sem("consts_in")
        x_in = sem("x_in")
        filt_in = sem("filt_in")
        bias_in = sem("bias_in")
        raw_in = [sem("raw_in0"), sem("raw_in1")]
        hi_done = sem("hi_done")
        lo_done = sem("lo_done")
        unit_done = sem("unit_done")
        evac = sem("evac")
        dve_chain = sem("dve_chain")
        act_chain = sem("act_chain")
        s_ready = sem("s_ready")
        sl_ready = sem("sl_ready")
        mod_ready = sem("mod_ready")
        setup_done = sem("setup_done")
        f_pe, f_dv, f_ac = sem("f_pe"), sem("f_dv"), sem("f_ac")
        n_sq, n_pe, n_rt = sem("n_sq"), sem("n_pe"), sem("n_rt")
        n_t, n_hi, n_lo = sem("n_t"), sem("n_hi"), sem("n_lo")
        c_ac = sem("c_ac")
        y_t, y_vt, y_d, y_y, y_i, y_z = (sem("y_" + s) for s in ("t", "vt", "d", "y", "i", "z"))
        y_hi, y_lo = sem("y_hi"), sem("y_lo")
        a_s, a_sc, a_ex, a_t, a_pt, a_o = (sem("a_" + s) for s in ("s", "sc", "ex", "t", "pt", "o"))
        a_on, a_ot, a_hi, a_lo = (sem("a_" + s) for s in ("on", "ot", "hi", "lo"))
        a_flip, a_bias = sem("a_flip"), sem("a_bias")
        m_sig, m_sum, m_hi, m_lo = (sem("m_" + s) for s in ("sig", "sum", "hi", "lo"))
        up_silu, up_mid, up_hi, up_lo = (sem("up_" + s) for s in ("silu", "mid", "hi", "lo"))
        out_done = sem("out_done")
        o_ready = sem("o_ready")
        r_split, r_pe, r_mask, r_rank, r_ev, h_tr, h_ev = (sem("r_" + s) for s in
            ("split", "pe", "mask", "rank", "ev", "htr", "hev"))
        p_sel, p_tr, p_selT = sem("p_sel"), sem("p_tr"), sem("p_selT")
        e_in = [sem(f"e_in{n}") for n in range(6)]
        e_hi = [sem(f"e_hi{n}") for n in range(3)]
        e_lo = [sem(f"e_lo{n}") for n in range(3)]
        e_use = [sem(f"e_use{n}") for n in range(3)]
        e_silu, e_mid, e_tr, e_th, e_tl = (sem("e_" + s) for s in ("silu", "mid", "tr", "th", "tl"))
        g_pe, g_hi, g_lo, y_ev, sc_pe, sc_ev = (sem("g_" + s) for s in
            ("pe", "hi", "lo", "yev", "scpe", "scev"))

        evb, n = [{}, {}], 0
        for l in range(2):
            n += 2
            for name, count in (("u", U_U), ("qkv", QKV_U), ("merge", 0), ("wo", WO_U)) + \
                    ((("up", 0), ("down", DK)) if l == 0 else ()):
                evb[l][name] = n
                n += count

        norm_c0 = [0, 0, 0, L, L]
        items_before = [0, 16, 32, 48, 56]

        block = top.enter_context(nc.Block())

        @block.sync
        def _(sp):
            def load(u, s, dst, src):
                sp.dma_start(dst, src).then_inc(raw_in[s], 16)

            def free(u):
                if not isinstance(u, int) or u >= 2:
                    sp.wait_ge(lo_done, u - 1)

            def std(w, col):
                return w[:, bass.ds(col, BLK)].rearrange("(k p) c -> p k c", p=P)

            def raw_std(s):
                return raw[:, s, :].rearrange("p (k c) -> p k c", k=DK)

            for l in range(2):
                b = base[l]
                for s in range(2):
                    free(b["mod"] + s)
                    load(0, s, raw_std(s), std(t["w_mod"][l], BLK * s))
                with sp.Fori(1, MOD_U // 2) as i:
                    for s in range(2):
                        free(b["mod"] + 2 * i + s)
                        load(0, s, raw_std(s), std(t["w_mod"][l], (2 * i + s) * BLK))
                with sp.Fori(0, U_U // 2) as i:
                    for s in range(2):
                        free(b["u"] + 2 * i + s)
                        load(0, s, raw_std(s), std(t["w_in"][l], OFF_U + (2 * i + s) * BLK))
                with sp.Fori(0, QKV_U // 2) as i:
                    for s in range(2):
                        free(b["qkv"] + 2 * i + s)
                        load(0, s, raw_std(s), std(t["w_in"][l], (2 * i + s) * BLK))
                with sp.Fori(0, 2) as i:
                    for n in range(6):
                        free(b["merge"] + 6 * i + n)
                        pair, kind = n // 3, n % 3
                        col = (2 * i + pair) * BLK
                        w = t["w_opab"][l] if kind == 2 else t["w_in"][l]
                        load(0, n % 2, raw_std(n % 2), std(w, (OFF_GA, OFF_GB, D)[kind] + col))
                with sp.Fori(0, WO_U // 2) as i:
                    for s in range(2):
                        free(b["wo"] + 2 * i + s)
                        load(0, s, raw_std(s), std(t["w_opab"][l], (2 * i + s) * BLK))
                if l == 0:
                    with sp.Fori(0, NB) as i:
                        for s, w in enumerate(("ffn_w1", "ffn_w3")):
                            free(b["up"] + 2 * i + s)
                            load(0, s, raw_std(s), std(t[w], i * BLK))
                    with sp.Fori(0, DK) as i:
                        for s in range(2):
                            free(b["down"] + 2 * i + s)
                            load(0, s, raw[:, s, 0:11 * P].rearrange("p (k c) -> p k c", k=11),
                                 t["ffn_w2"][s * 11 * P:(s + 1) * 11 * P, bass.ds(i * P, P)]
                                 .rearrange("(k p) c -> p k c", p=P))
            sp.wait_ge(lo_done, n_units)
            sp.wait_ge(unit_done, n_units)
            for g in range(2):
                with sp.Fori(0, NE) as e:
                    for b in range(NB):
                        for kind in range(3):
                            B = g * NE * NB + e * NB + b
                            sp.wait_ge(e_lo[kind], B + 1 - (b > 0))
                            slot = 2 * kind + b % 2
                            dst = eraw[:, slot, :]
                            if kind < 2:
                                w = t["moe_w1"] if kind == 0 else t["moe_w3"]
                                src = w[bass.ds(e * D, D), b * BLK:(b + 1) * BLK].rearrange("(k p) c -> p k c", p=P)
                                dst = dst.rearrange("p (k c) -> p k c", k=DK)
                            else:
                                src = t["moe_w2"][bass.ds(e * FF + b * BLK, BLK), :].rearrange("(k p) c -> p k c", p=P)
                                dst = dst.rearrange("p (k c) -> p k c", k=2)
                            sp.dma_start(dst, src).then_inc(e_in[slot], 16)
            sp.wait_ge(o_ready, DK)
            sp.dma_start(out.rearrange("(k p) t -> p k t", p=P), X[:, :, L:TOK]).then_inc(out_done, 16)
            sp.wait_ge(out_done, 16)

        @block.gpsimd
        def _(pool):
            def load(dst, src, s):
                pool.dma_start(dst, src).then_inc(s, 16)
            small = [(cvec[:], t["cc"]), (ident[:], t["ident"]), (flip[:], t["flip"]), (bmod[:], t["b_mod"]),
                     (g1[:], t["norm1_g"]), (g2[:], t["norm2_g"]), (gf[:], t["final_g"]),
                     (cw[:], t["hy_conv_w"]), (cb[:], t["hy_conv_b"]), (hyb[:], t["hy_bias"]),
                     (router[:], t["moe_router"])]
            assert len(small) == N_SMALL
            for dst, src in small:
                load(dst, src, consts_in)
            load(X[:, :, 0:L], t["ctxT"].rearrange("(k p) t -> p k t", p=P), x_in)
            load(X[:, :, L:TOK], t["xT"].rearrange("(k p) t -> p k t", p=P), x_in)
            for l in range(2):
                if l == 1:
                    pool.wait_ge(unit_done, base[1]["mod"])
                    pool.wait_ge(evac, evb[0]["down"] + DK)
                filt = [(dftf[:], t["dftf"]), (dftk[:], t["dftk"]), (dfti[:], t["dfti"]), (posT[:], t["posT"]),
                        (decay[:], t["decay"]), (fw1[:], t["hy_w1"][l]), (fw2[:], t["hy_w2"][l]),
                        (fw3[:], t["hy_w3"][l].rearrange("f (o c) -> f o c", o=2)), (fb[:], t["fvec"][l])]
                assert len(filt) == N_FILT
                for dst, src in filt:
                    load(dst, src, filt_in)
                pool.wait_ge(y_z, (4 if l == 0 else 6))
                pool.wait_ge(y_lo, (2 if l == 0 else 3))
                load(mask[:], t["mask"], bias_in)
                rp = t["rpb"]
                for h in range(HEADS):
                    for half in range(2):
                        first = ((l * HEADS + h) * RPB_R + 5 - half) * RPB_C + WIN - GRID
                        src = bass.AP(rp.tensor, first, [[1, GRID], [RPB_C, 6], [1, GRID]])
                        load(bias[half * GRID:(half + 1) * GRID, h, :].rearrange("p (r c) -> p r c", r=6), src, bias_in)
            pool.wait_ge(unit_done, n_units)
            load(tri[:], t["tri"], bias_in)
            load(iot[:], t["iota"], bias_in)

        @block.scalar
        def _(act):
            A = nc.scalar.activation

            def hi(u, s, half):
                act.wait_ge(raw_in[s], 16 * half + 16)
                if not isinstance(u, int) or u >= 2:
                    act.wait_ge(unit_done, u - 1)
                A(WH[:, s, :], raw[:, s, :], ACT.Copy).then_inc(hi_done, 1)

            def ahead(b, n, s):
                u = b + n + 2
                half = (u - s) // 2 if isinstance(u, int) else None
                hi(u, s, half)

            def ahead_loop(b, i, stride, n):
                u0 = b + n + 2
                hi(u0 + stride * i, n % 2, u0 // 2 + (stride // 2) * i)

            def norm_roots(q):
                c0 = norm_c0[q]
                if q == 0:
                    act.wait_ge(x_in, 32)
                elif q < 4:
                    act.wait_ge(evac, (None, evb[0]["wo"] + WO_U, evb[0]["down"] + DK, evb[1]["wo"] + WO_U)[q])
                else:
                    act.wait_ge(sc_ev, 1 + 8 * NE)
                for k in range(DK):
                    if 8 * q + k >= 2:
                        act.wait_ge(n_pe, 8 * q + k - 1)
                    if q and k < 2:
                        act.wait_ge(n_lo, items_before[q])
                    A(sq[:, k % 2, c0:TOK], X[:, k, c0:TOK], ACT.Square).then_inc(n_sq, 1)
                act.wait_ge(n_pe, 8 * q + 8)
                A(rs[:, c0:TOK], PS[:, 7, c0:TOK], ACT.Sqrt, bias=eps[:, 0:1], scale=1.0 / D).then_inc(n_rt, 1)

            def norm_hi(q, shift, hh):
                streams = range(1 if q == 3 else 0, 2)
                it = items_before[q]
                for k in range(DK):
                    for s in streams:
                        act.wait_ge(n_t, it + 1)
                        dst = hh[:, k, 0:L] if q == 3 else hh[:, k, s * L:(s + 1) * L]
                        A(dst, sq[:, it % 2, 0:L], ACT.Identity,
                          bias=mod[:, shift * DK + k, s:s + 1]).then_inc(n_hi, 1)
                        if q == 3:
                            A(mo_h[:, k, :], sq[:, it % 2, 0:L], ACT.Identity,
                              bias=mod[:, shift * DK + k, s:s + 1]).then_inc(n_hi, 1)
                        it += 1

            act.wait_ge(consts_in, 16 * N_SMALL)
            act.wait_ge(setup_done, 2)
            A(svec[:], cvec[:], ACT.Silu).then_inc(act_chain, 1)
            act.wait_ge(act_chain, 1)
            A(SH[:], svec[:], ACT.Copy).then_inc(s_ready, 1)
            A(RTH[:], router[:], ACT.Copy).then_inc(r_split, 1)
            cb_seen = 0
            conv_items = 0
            att_n = att_q = 0
            for l in range(2):
                b = base[l]
                c0 = 0 if l == 0 else L
                for j in range(2):
                    act.wait_ge(f_dv, 4 * l + j + 1)
                    A(act1[:, j, :], arg[:, j, :], ACT.Sin).then_inc(f_ac, 1)
                for o in range(2):
                    act.wait_ge(f_pe, 5 * l + 4 + o)
                    for g in range(5):
                        last = A(spec[:, o, g, :], PS[0:BINS, g, :], ACT.Copy)
                    last.then_inc(f_ac, 1)
                if l == 0:
                    hi(0, 0, 0)
                    hi(1, 1, 0)
                    for n in range(2):
                        hi(2 + n, n, 1)
                    with act.Fori(1, MOD_U // 2) as i:
                        for n in range(2):
                            ahead_loop(b["mod"], i, 2, n)
                else:
                    with act.Fori(0, MOD_U // 2) as i:
                        for n in range(2):
                            ahead_loop(b["mod"], i, 2, n)
                norm_roots(2 * l)
                norm_hi(2 * l, SHIFT1, HH)
                with act.Fori(0, U_U // 2) as i:
                    for n in range(2):
                        ahead_loop(b["u"], i, 2, n)
                        act.wait_ge(unit_done, b["u"] + 2 * i + n + 1)
                        for j in range(2):
                            m = 4 * i + 2 * n + j
                            A(U[:, m, c0:TOK], PS[:, 2 * n + j, c0:TOK], ACT.Identity,
                              bias=cb[:, l, bass.ds(m, 1)], scale=cw[:, l, 1, bass.ds(m, 1)]).then_inc(c_ac, 1)
                for o in range(2):
                    for s in range(1 if l else 0, 2):
                        n = conv_items
                        act.wait_ge(y_t, n + 1)
                        if n:
                            act.wait_ge(y_d, n)
                        for c in range(2):
                            last = A(VT[:, c, :], PS[:, 4 + c, :], ACT.Copy)
                        last.then_inc(y_vt, 1)
                        if o == 1:
                            act.wait_ge(y_z, n + 1)
                            A(OHH[:, :, s * L:(s + 1) * L], zt[:, :, :], ACT.Copy).then_inc(y_hi, 1)
                        conv_items += 1
                with act.Fori(0, QKV_U // 2) as i:
                    for n in range(2):
                        ahead_loop(b["qkv"], i, 2, n)
                def probs_out(n, width):
                    act.wait_ge(a_t, n + 1)
                    if n >= 2:
                        act.wait_ge(a_o, n - 1)
                    A(PT[:, n % 2, 0:width], PS[:, 2 + n % 2, 0:width], ACT.Copy).then_inc(a_pt, 1)
                for qc in range(0 if l == 0 else 2, 4):
                    width = TOK if qc >= 2 else L
                    for h in range(HEADS):
                        n = att_n
                        act.wait_ge(a_sc, n + 1)
                        A(S[:, n % 2, 0:width], S[:, n % 2, 0:width], ACT.Exp, bias=nmax[:, n % 32:n % 32 + 1],
                          accum_out=psums[:, n % 32:n % 32 + 1]).then_inc(a_ex, 1)
                        if h:
                            probs_out(n - 1, width)
                        att_n += 1
                    probs_out(att_n - 1, width)
                    act.wait_ge(a_ot, att_q + 1)
                    A(OAH[:, :, qc * P:(qc + 1) * P], PS[:, 6 + qc % 2, :].rearrange("p (c q) -> p c q", c=4),
                      ACT.Copy).then_inc(a_hi, 1)
                    att_q += 1
                mb = 4 * l
                if l == 0:
                    act.nop().then_inc(m_sig, 1)
                with act.Fori(0, 2) as i:
                    for n in range(6):
                        pair, kind = n // 3, n % 3
                        ahead_loop(b["merge"], i, 6, n)
                        act.wait_ge(unit_done, b["merge"] + 6 * i + n + 1)
                        if kind < 2:
                            act.wait_ge(m_lo, mb + 2 * i + pair + 1)
                            dst = sga if kind == 0 else sgb
                            A(dst[:, :, c0:TOK], PS[:, 2 * kind:2 * kind + 2, c0:TOK], ACT.Sigmoid).then_inc(m_sig, 1)
                        else:
                            act.wait_ge(m_sum, mb + 2 * i + pair + 2)
                            A(MH[:, bass.ds(2 * (2 * i + pair), 2), c0:TOK], sga[:, :, c0:TOK], ACT.Copy).then_inc(m_hi, 1)
                for n in range(WO_U):
                    if l == 0 or n < 2:
                        hi(b["wo"] + n + 2, n % 2, b["wo"] // 2 + (n + 2) // 2)
                norm_roots(2 * l + 1)
                if l == 0:
                    norm_hi(1, SHIFT2, HH)
                    act.nop().then_inc(up_silu, 1)
                    with act.Fori(0, NB) as i:
                        ahead_loop(b["up"], i, 2, 0)
                        act.wait_ge(unit_done, b["up"] + 2 * i + 1)
                        act.wait_ge(up_lo, i + 1)
                        A(sff[:, :, :], PS[:, 0:2, :], ACT.Silu).then_inc(up_silu, 1)
                        ahead_loop(b["up"], i, 2, 1)
                        act.wait_ge(up_mid, i + 2)
                        A(MDH[:, bass.ds(2 * i, 2), :], sff[:, :, :], ACT.Copy).then_inc(up_hi, 1)
                    with act.Fori(0, DK) as i:
                        for n in range(2):
                            ahead_loop(b["down"], i, 2, n)
                else:
                    act.wait_ge(unit_done, n_units)
                    norm_hi(3, SHIFT2, RH)
            for c in range(2):
                act.wait_ge(r_mask, c + 1)
                A(gt[:, c, 1:2], gt[:, c, 0:1], ACT.Exp).then_inc(r_ev, 1)
            for c in range(2):
                for hf in range(2):
                    act.wait_ge(h_tr, 2 * c + hf + 1)
                    A(mo_ht[:, c, hf * 512:(hf + 1) * 512], PS[:, 2 * c + hf, :], ACT.Copy).then_inc(h_ev, 1)
            for g in range(2):
                for q in range(4):
                    act.wait_ge(p_tr, 4 * g + q + 1)
                    A(selT[:, 2 * q:2 * q + 2, :], PS[:, q, :].rearrange("p (e t) -> p e t", e=2), ACT.Copy).then_inc(p_selT, 1)
                with act.Fori(0, NE) as e:
                    B0 = g * NE * NB + e * NB
                    E0 = g * NE + e

                    def ehi(kind, b):
                        slot = 2 * kind + b % 2
                        per = 6 if b % 2 == 0 else 5
                        act.wait_ge(e_in[slot], 16 * (per * (g * NE) + b // 2 + 1) + (16 * per) * e)
                        act.wait_ge(e_use[kind], B0 + b + 1)
                        A(EH[:, kind, :], eraw[:, slot, :], ACT.Copy).then_inc(e_hi[kind], 1)

                    for q in range(2):
                        act.wait_ge(g_pe, 2 * E0 + q + 1)
                        A(GH[:, 4 * q:4 * q + 4, :], PS[:, 5 + q, :].rearrange("p (k j) -> p k j", k=4), ACT.Copy).then_inc(g_hi, 1)
                    ehi(0, 0)
                    ehi(1, 0)
                    for b in range(NB + 1):
                        if b < NB:
                            act.wait_ge(e_use[0], B0 + b + 2)
                            act.wait_ge(e_mid, B0 + b + 1)
                            A(sil[:], PS[:, 0, 0:BLK], ACT.Silu).then_inc(e_silu, 1)
                        if b + 1 < NB:
                            ehi(0, b + 1)
                        if b:
                            act.wait_ge(e_tr, B0 + b)
                            act.wait_ge(e_use[2], B0 + b)
                            A(TH[:], PS[:, 2, 0:2 * P].rearrange("p (k j) -> p k j", k=2), ACT.Copy).then_inc(e_th, 1)
                        if b + 1 < NB:
                            ehi(1, b + 1)
                        if b < NB:
                            ehi(2, b)
                    act.wait_ge(e_use[2], B0 + NB + 1)
                    act.wait_ge(sc_pe, 4 * E0 + 1)
                    A(yexp[:], PS[:, 3:5, :].rearrange("p a b -> p (a b)"), ACT.Copy).then_inc(y_ev, 1)
            norm_roots(4)

        @block.vector
        def _(dve):
            V_ = nc.vector
            TT, TS, STT = V_.tensor_tensor, V_.tensor_scalar, V_.scalar_tensor_tensor
            chain = Chain(dve, dve_chain)
            link = chain.link

            def lo(u, s):
                dve.wait_ge(hi_done, u + 1)
                TT(WL[:, s, :], raw[:, s, :], WH[:, s, :].bitcast(F32), ALU.subtract).then_inc(lo_done, 1)

            def norm_lo(q, shift, scale, hh, hl):
                c0 = norm_c0[q]
                streams = range(1 if q == 3 else 0, 2)
                dve.wait_ge(n_rt, q + 1)
                link(V_.reciprocal(rs[:, c0:TOK], rs[:, c0:TOK]))
                todo = [(k, s) for k in range(DK) for s in streams]
                first = items_before[q]

                def low(j):
                    k, s = todo[j]
                    it = first + j
                    dve.wait_ge(n_hi, it + 1 if q < 3 else first + 2 * (j + 1))
                    dst = slice(0, L) if q == 3 else slice(s * L, (s + 1) * L)
                    STT(hl[:, k, dst], sq[:, it % 2, 0:L], mod[:, shift * DK + k, s:s + 1],
                        hh[:, k, dst].bitcast(F32), ALU.add, ALU.subtract).then_inc(n_lo, 1)

                for j, (k, s) in enumerate(todo):
                    it = first + j
                    if j >= 2:
                        dve.wait_ge(n_lo, it - 1)
                    STT(sq[:, it % 2, 0:L], X[:, k, s * L:(s + 1) * L], scale[:, k, s:s + 1],
                        rs[:, s * L:(s + 1) * L], ALU.mult, ALU.mult).then_inc(n_t, 1)
                    if j:
                        low(j - 1)
                low(len(todo) - 1)

            V_.memset(ones[:], 1.0).then_inc(setup_done, 1)
            V_.memset(eps[:], EPS).then_inc(setup_done, 1)
            dve.wait_ge(s_ready, 1)
            TT(SL[:], svec[:], SH[:].bitcast(F32), ALU.subtract).then_inc(sl_ready, 1)
            dve.wait_ge(r_split, 1)
            TT(RTL[:], router[:], RTH[:].bitcast(F32), ALU.subtract).then_inc(r_split, 1)
            dve.wait_ge(x_in, 32)
            conv_items = conv_c = 0
            att_n = att_q = 0
            for l in range(2):
                b = base[l]
                c0 = 0 if l == 0 else L
                ns = 2 - l
                dve.wait_ge(filt_in, 16 * N_FILT * (l + 1))
                for j in range(2):
                    dve.wait_ge(f_pe, 5 * l + j + 1)
                    a = arg[:, j, :]
                    link(TS(a, PS[0:64, 7, 0:L], fb[:, 2 * j:2 * j + 1], fb[:, 2 * j + 1:2 * j + 2], ALU.add, ALU.mult))
                    link(TS(turns[:], a, 1.0 / (2 * math.pi), MAGIC, ALU.mult, ALU.add))
                    link(TS(turns[:], turns[:], MAGIC, None, ALU.subtract))
                    for c in TWO_PI_PARTS:
                        link(STT(a, turns[:], -c, a, ALU.mult, ALU.add))
                    TS(a, a, PI_CLIP, -PI_CLIP, ALU.min, ALU.max).then_inc(f_dv, 1)
                dve.wait_ge(f_pe, 5 * l + 3)
                for o in range(2):
                    if o:
                        dve.wait_ge(f_pe, 5 * l + 4)
                    for pc in range(2):
                        last = TT(taps[:, pc, :], PS[:, TAPB[2 * o + pc], :], decay[:, pc, o, :], ALU.mult)
                    last.then_inc(f_dv, 1)
                if l == 0:
                    for n in range(4):
                        lo(n, n % 2)
                    with dve.Fori(1, MOD_U // 2) as i:
                        for n in range(2):
                            lo(b["mod"] + 2 * i + n + 2, n)
                else:
                    with dve.Fori(0, MOD_U // 2) as i:
                        for n in range(2):
                            lo(b["mod"] + 2 * i + n + 2, n)
                dve.wait_ge(unit_done, b["mod"] + MOD_U)
                dve.wait_ge(consts_in, 16 * N_SMALL)
                mps = PS[:, 0, 0:96].rearrange("p (m s) -> p m s", s=2)
                for s in range(2):
                    last = TT(mod[:, :, s], mps[:, :, s], bmod[:, l, :], ALU.add)
                    last.then_inc(evac, 1)
                dve.wait_ge(evac, (evb[l]["u"]))
                for s in range(2):
                    link(STT(na1[:, :, s], mod[:, SCALE1 * DK:(SCALE1 + 1) * DK, s], 1.0, g1[:, l, :], ALU.add, ALU.mult))
                    link(STT(na2[:, :, s], mod[:, SCALE2 * DK:(SCALE2 + 1) * DK, s], 1.0, g2[:, l, :], ALU.add, ALU.mult))
                norm_lo(2 * l, SHIFT1, na1, HH, HL)
                Ust = U[:, :, :].rearrange("p m (s t) -> p m s t", s=2)
                with dve.Fori(0, U_U // 2) as i:
                    chain.enter(i, 4, U_U // 2)
                    for n in range(2):
                        lo(b["u"] + 2 * i + n + 2, n)
                        for j in range(2):
                            m = 4 * i + 2 * n + j
                            dve.wait_ge(c_ac, 12 * l + 1 + m)
                            pv = PS[:, 2 * n + j, :].rearrange("p (s t) -> p s t", s=2)
                            row = U[:, bass.ds(m, 1), :].rearrange("p m (s t) -> p (m s) t", s=2)
                            sl = slice(l, 2)
                            link(STT(row[:, sl, 1:L], pv[:, sl, 0:L - 1], cw[:, l, 0, bass.ds(m, 1)],
                                     row[:, sl, 1:L], ALU.mult, ALU.add))
                            last = STT(row[:, sl, 0:L - 1], pv[:, sl, 1:L], cw[:, l, 2, bass.ds(m, 1)],
                                       row[:, sl, 0:L - 1], ALU.mult, ALU.add)
                        last.then_inc(evac, 1)
                    chain.exit()
                dve.wait_ge(evac, evb[l]["qkv"])
                for o in range(2):
                    for s in range(l, 2):
                        n = conv_items
                        dve.wait_ge(y_d, n + 1)
                        if n:
                            dve.wait_ge(y_i, n)
                        F = spec[:, o]
                        for j in range(2):
                            are, aim = PS[0:BINS, j, :], PS[0:BINS, 2 + j, :]
                            fre, fim, fren = F[:, j], F[:, 2 + j], (F[:, 4] if j == 0 else F[:, 1])
                            TT(Y[:, j, :], are, fre, ALU.mult)
                            TT(pt[:, 0, :], aim, fim, ALU.mult)
                            TT(Y[:, 2 + j, :], are, fim, ALU.mult)
                            link(TT(pt[:, 1, :], aim, fren, ALU.mult))
                            TT(Y[:, j, :], Y[:, j, :], pt[:, 0, :], ALU.subtract)
                            last = TT(Y[:, 2 + j, :], Y[:, 2 + j, :], pt[:, 1, :], ALU.add)
                            link(last) if j == 0 else last.then_inc(y_y, 1)
                        dve.wait_ge(y_i, n + 1)
                        if conv_c:
                            dve.wait_ge(y_lo, conv_c)
                        cols = slice(s * L, (s + 1) * L)
                        for c in range(4):
                            last = STT(zt[:, c, :], U[:, c, cols], hyb[:, l, o, c:c + 1], PS[:, 6 + c // 2, (c % 2) * L:(c % 2 + 1) * L],
                                       ALU.mult, ALU.add)
                        link(last)
                        dst = zt[:, :, :] if o else U[:, 0:4, cols]
                        TT(dst, zt[:, :, :], U[:, 4 + 4 * o:8 + 4 * o, cols], ALU.mult).then_inc(y_z, 1)
                        if o:
                            dve.wait_ge(y_hi, conv_c + 1)
                            TT(OHL[:, :, cols], zt[:, :, :], OHH[:, :, cols].bitcast(F32), ALU.subtract).then_inc(y_lo, 1)
                            conv_c += 1
                        conv_items += 1
                for n in range(QKV_U):
                    lo(b["qkv"] + n + 2, n % 2)
                    dve.wait_ge(unit_done, b["qkv"] + n + 1)
                    if n == 0:
                        dve.wait_ge(y_lo, conv_c)
                    if n < 4:
                        last = V_.tensor_copy(QK[:, 2 * n:2 * n + 2, :], PS[:, 2 * (n % 2):2 * (n % 2) + 2, :])
                    else:
                        src = PS[:, 2 * (n % 2):2 * (n % 2) + 2, :].rearrange("p a (b c) -> p (a b) c", b=2)
                        last = V_.tensor_copy(V[:, :, (n - 4) * BLK:(n - 3) * BLK], src)
                    last.then_inc(evac, 1)
                dve.wait_ge(bias_in, 16 * 17 * (l + 1))
                for h in range(HEADS):
                    dve.wait_ge(a_flip, HEADS * l + h + 1)
                    TT(bias[:, h, :], PS[:, 4 + h % 4, 0:6 * GRID], mask[:, :], ALU.add).then_inc(a_bias, 1)
                dve.wait_ge(a_bias, HEADS * (l + 1))
                for qc in range(2 * l, 4):
                    width = TOK if qc >= 2 else L
                    n0 = att_n
                    for h in range(HEADS):
                        n = att_n
                        dve.wait_ge(a_s, n + 1)
                        if n >= 2:
                            dve.wait_ge(a_t, n - 1)
                        last = TS(S[:, n % 2, 0:L], PS[:, n % 2, 0:L], SCALE, None, ALU.mult)
                        if qc >= 2:
                            bs = bias[:, h, (3 - qc) * P:(3 - qc) * P + L]
                            last = STT(S[:, n % 2, L:TOK], PS[:, n % 2, L:TOK], SCALE, bs, ALU.mult, ALU.add)
                        link(last)
                        V_.tensor_reduce(nmax[:, n % 32:n % 32 + 1], S[:, n % 2, 0:width], AX, ALU.max,
                                         negate=True).then_inc(a_sc, 1)
                        att_n += 1
                    dve.wait_ge(a_ex, att_n)
                    r0 = n0 % 32
                    link(V_.reciprocal(rsum[:, r0:r0 + HEADS], psums[:, r0:r0 + HEADS]))
                    dve.wait_ge(a_o, att_n)
                    src = PS[:, 4 + qc % 2, :].rearrange("p (h d) -> p h d", h=HEADS)
                    TT(OT[:, qc, :].rearrange("p (h d) -> p h d", h=HEADS), src,
                       rsum[:, r0:r0 + HEADS].unsqueeze(2).to_broadcast([P, HEADS, HD]), ALU.mult).then_inc(a_on, 1)
                    dve.wait_ge(a_hi, att_q + 1)
                    TT(OAL[:, :, qc * P:(qc + 1) * P], PS[:, 6 + qc % 2, :].rearrange("p (c q) -> p c q", c=4),
                       OAH[:, :, qc * P:(qc + 1) * P].bitcast(F32), ALU.subtract).then_inc(a_lo, 1)
                    att_q += 1
                if l == 0:
                    for s_ in (m_sum, m_lo):
                        dve.nop().then_inc(s_, 1)
                with dve.Fori(0, 2) as i:
                    chain.enter(i, 2, 2)
                    for n in range(6):
                        pair, kind = n // 3, n % 3
                        lo(b["merge"] + 6 * i + n + 2, n % 2)
                        if kind == 2:
                            q = 4 * l + 2 * i + pair
                            dve.wait_ge(unit_done, b["merge"] + 6 * i + n + 1)
                            dve.wait_ge(m_sig, 2 * q + 3)
                            TT(sga[:, :, c0:TOK], sga[:, :, c0:TOK], PS[:, 4:6, c0:TOK], ALU.mult)
                            link(TT(sgb[:, :, c0:TOK], sgb[:, :, c0:TOK], PS[:, 6:8, c0:TOK], ALU.mult))
                            TT(sga[:, :, c0:TOK], sga[:, :, c0:TOK], sgb[:, :, c0:TOK], ALU.add).then_inc(m_sum, 1)
                            dve.wait_ge(m_hi, q + 1)
                            mm = bass.ds(2 * (2 * i + pair), 2)
                            TT(ML[:, mm, c0:TOK], sga[:, :, c0:TOK], MH[:, mm, c0:TOK].bitcast(F32), ALU.subtract).then_inc(m_lo, 1)
                    chain.exit()
                for n in range(WO_U):
                    if l == 0 or n < 2:
                        lo(b["wo"] + n + 2, n % 2)
                    dve.wait_ge(unit_done, b["wo"] + n + 1)
                    for j in range(2):
                        for s in range(l, 2):
                            m = 2 * n + j
                            cols = slice(s * L, (s + 1) * L)
                            last = STT(X[:, m, cols], PS[:, 2 * (n % 2) + j, cols], mod[:, GATE1 * DK + m, s:s + 1],
                                       X[:, m, cols], ALU.mult, ALU.add)
                    last.then_inc(evac, 1)
                if l == 0:
                    norm_lo(1, SHIFT2, na2, HH, HL)
                    for s_ in (up_mid, up_lo):
                        dve.nop().then_inc(s_, 1)
                    with dve.Fori(0, NB) as i:
                        lo(b["up"] + 2 * i + 2, 0)
                        lo(b["up"] + 2 * i + 3, 1)
                        dve.wait_ge(up_silu, i + 2)
                        dve.wait_ge(unit_done, b["up"] + 2 * i + 2)
                        TT(sff[:, :, :], sff[:, :, :], PS[:, 2:4, :], ALU.mult).then_inc(up_mid, 1)
                        dve.wait_ge(up_hi, i + 1)
                        TT(MDL[:, bass.ds(2 * i, 2), :], sff[:, :, :], MDH[:, bass.ds(2 * i, 2), :].bitcast(F32),
                           ALU.subtract).then_inc(up_lo, 1)
                    with dve.Fori(0, DK // 2) as i:
                        for mm in range(2):
                            for s in range(2):
                                lo(b["down"] + 4 * i + 2 * mm + s + 2, s)
                            dve.wait_ge(unit_done, b["down"] + 4 * i + 2 * mm + 2)
                            for s in range(2):
                                cols = slice(s * L, (s + 1) * L)
                                xm = X[:, bass.ds(2 * i + mm, 1), cols].rearrange("p m t -> p (m t)")
                                last = STT(xm, PS[:, mm, cols], mod[:, bass.ds(GATE2 * DK + 2 * i + mm, 1), s],
                                           xm, ALU.mult, ALU.add)
                            last.then_inc(evac, 1)
                else:
                    norm_lo(3, SHIFT2, na2, RH, RL)
            for c in range(2):
                dve.wait_ge(r_pe, c + 1)
                link(V_.tensor_copy(logits[:, c, :], PS[:, c, 0:NE]))
                link(V_.max(tv[:, c, :], logits[:, c, :]))
                link(V_.max_index(ti[:, c, :], tv[:, c, :], logits[:, c, :]))
                V_.tensor_copy(tif[:, c, :], ti[:, c, :])
                TT(gt[:, c, 0:1], tv[:, c, 1:2], tv[:, c, 0:1], ALU.subtract).then_inc(r_mask, 1)
            dve.wait_ge(bias_in, 16 * 36)
            for c in range(2):
                dve.wait_ge(r_ev, c + 1)
                link(TS(gt[:, c, 2:3], gt[:, c, 1:2], 1.0, None, ALU.add))
                link(V_.reciprocal(gt[:, c, 2:3], gt[:, c, 2:3]))
                link(TT(gt[:, c, 3:4], gt[:, c, 1:2], gt[:, c, 2:3], ALU.mult))
                for j in range(2):
                    link(TS(oh[:, c, j, :], iot[:, 0:NE], tif[:, c, j:j + 1], None, ALU.is_equal))
                    link(TS(oh[:, c, 2 + j, :], oh[:, c, j, :], gt[:, c, 2 + j:3 + j], None, ALU.mult))
                link(TT(wex[:, c, :], oh[:, c, 2, :], oh[:, c, 3, :], ALU.add))
                TT(msk[:, c, :], oh[:, c, 0, :], oh[:, c, 1, :], ALU.add).then_inc(r_mask, 1)
            dve.wait_ge(r_mask, 4)
            dve.wait_ge(r_rank, 1)
            for c in range(2):
                link(TS(rank[:, c, :], msk[:, c, :], -1000.0, 1000.0, ALU.mult, ALU.add))
                link(TT(rank[:, c, :], rank[:, c, :], PS[:, 4 + c, 0:NE], ALU.add))
            for k in range(3):
                dve.nop().then_inc(e_lo[k], 1)
            dve.nop().then_inc(e_mid, 1)
            dve.nop().then_inc(sc_ev, 1)
            for g in range(2):
                if g:
                    dve.wait_ge(sc_pe, 1 + 4 * NE)
                    dve.wait_ge(g_pe, 2 * NE)
                for e in range(NE):
                    for c in range(2):
                        TS(sel[:, c, e, :], iot[:, g * P:(g + 1) * P], rank[:, c, e:e + 1], None, ALU.is_equal)
                        last = TS(selw[:, c, e, :], iot[:, g * P:(g + 1) * P], rank[:, c, e:e + 1],
                                  wex[:, c, e:e + 1], ALU.is_equal, ALU.mult)
                    last.then_inc(p_sel, 1)
                with dve.Fori(0, NE) as e:
                    B0 = g * NE * NB + e * NB
                    E0 = g * NE + e

                    def elo(kind, b):
                        dve.wait_ge(e_hi[kind], B0 + b + 1)
                        TT(EL[:, kind, :], eraw[:, 2 * kind + b % 2, :], EH[:, kind, :].bitcast(F32),
                           ALU.subtract).then_inc(e_lo[kind], 1)

                    for q in range(2):
                        dve.wait_ge(g_hi, 2 * E0 + q + 1)
                        TT(GL[:, 4 * q:4 * q + 4, :], PS[:, 5 + q, :].rearrange("p (k j) -> p k j", k=4),
                           GH[:, 4 * q:4 * q + 4, :].bitcast(F32), ALU.subtract).then_inc(g_lo, 1)
                    elo(0, 0)
                    elo(1, 0)
                    for b in range(NB + 1):
                        if b + 1 < NB:
                            elo(0, b + 1)
                        if b:
                            dve.wait_ge(e_th, B0 + b)
                            TT(TL[:], PS[:, 2, 0:2 * P].rearrange("p (k j) -> p k j", k=2), TH[:].bitcast(F32),
                               ALU.subtract).then_inc(e_tl, 1)
                        if b < NB:
                            dve.wait_ge(e_silu, B0 + b + 1)
                            dve.wait_ge(e_use[1], B0 + b + 2)
                            TT(mid[:], sil[:], PS[:, 1, 0:BLK], ALU.mult).then_inc(e_mid, 1)
                        if b + 1 < NB:
                            elo(1, b + 1)
                        if b < NB:
                            elo(2, b)
                    for r in range(4):
                        dve.wait_ge(sc_pe, 4 * E0 + r + 2)
                        for j in range(2):
                            f = 2 * r + j
                            last = STT(X[:, f, L:TOK], PS[:, 5 + r % 2, j * L:(j + 1) * L], mod[:, GATE2 * DK + f, 1:2],
                                       X[:, f, L:TOK], ALU.mult, ALU.add)
                        last.then_inc(sc_ev, 1)
            dve.wait_ge(n_rt, 5)
            link(V_.reciprocal(rs[:, L:TOK], rs[:, L:TOK]))
            for k in range(DK):
                STT(X[:, k, L:TOK], X[:, k, L:TOK], gf[:, k:k + 1], rs[:, L:TOK], ALU.mult, ALU.mult).then_inc(o_ready, 1)

        @block.tensor
        def _(pe):
            MM, TR = nc.tensor.matmul, nc.tensor.transpose

            def mm3(o, wh, wl, xh, xl, first, last):
                MM(o, wh, xh, start=first, stop=False)
                MM(o, wh, xl, start=False, stop=False)
                return MM(o, wl, xh, start=False, stop=last)

            def ready(u):
                pe.wait_ge(lo_done, u + 1)

            def cols(s, k, j):
                a = k * BLK + j * P
                return slice(a, a + P)

            def features(s, banks, c0, xh, xl, ks=range(DK), wk=None):
                for j in range(2):
                    for n, k in enumerate(ks):
                        w = n if wk is None else wk + n
                        last = mm3(PS[:, banks + j, c0:TOK], WH[:, s, cols(s, w, j)], WL[:, s, cols(s, w, j)],
                                   xh[:, k, c0:TOK], xl[:, k, c0:TOK], n == 0, n == len(ks) - 1)
                return last

            def norm_sums(q):
                c0 = norm_c0[q]
                for k in range(DK):
                    pe.wait_ge(n_sq, 8 * q + k + 1)
                    MM(PS[:, 7, c0:TOK], ones[:], sq[:, k % 2, c0:TOK], start=k == 0, stop=k == DK - 1).then_inc(n_pe, 1)

            pe.wait_ge(setup_done, 2)
            conv_items = 0
            att_n = att_q = 0
            for l in range(2):
                b = base[l]
                c0 = 0 if l == 0 else L
                pe.wait_ge(filt_in, 16 * N_FILT * (l + 1))
                MM(PS[0:64, 7, 0:L], fw1[:], posT[:], start=True, stop=True).then_inc(f_pe, 1)
                pe.wait_ge(f_ac, 4 * l + 1)
                MM(PS[0:64, 7, 0:L], fw2[:], act1[:, 0, :], start=True, stop=True).then_inc(f_pe, 1)
                pe.wait_ge(f_ac, 4 * l + 2)
                for o in range(2):
                    for pc in range(2):
                        last = MM(PS[:, TAPB[2 * o + pc], :], act1[:, 1, pc * P:(pc + 1) * P], fw3[:, o, :], start=True, stop=True)
                last.then_inc(f_pe, 1)
                for o in range(2):
                    pe.wait_ge(f_dv, 4 * l + 3 + o)
                    if o:
                        pe.wait_ge(f_ac, 4 * l + 3)
                    for g in range(5):
                        for c in range(2):
                            last = MM(PS[0:BINS, g, :], dftk[:, c, g * BINS:(g + 1) * BINS], taps[:, c, :], start=c == 0, stop=c == 1)
                    last.then_inc(f_pe, 1)
                pe.wait_ge(sl_ready, 1)
                pe.wait_ge(f_ac, 4 * l + 4)
                with pe.Fori(0, MOD_U // 2) as i:
                    for n in range(2):
                        ready(b["mod"] + 2 * i + n)
                        for j in range(2):
                            for k in range(DK):
                                last = mm3(PS[:, 0, bass.ds(8 * i + 4 * n + 2 * j, 2)], WH[:, n, cols(n, k, j)], WL[:, n, cols(n, k, j)],
                                           SH[:, k, :], SL[:, k, :], k == 0, k == DK - 1)
                        last.then_inc(unit_done, 1)
                norm_sums(2 * l)
                pe.wait_ge(n_lo, items_before[2 * l] + 16)
                with pe.Fori(0, U_U // 2) as i:
                    for n in range(2):
                        ready(b["u"] + 2 * i + n)
                        pe.wait_ge(evac, evb[l]["u"] + 2 * i + n - 1)
                        features(n, 2 * n, c0, HH, HL).then_inc(unit_done, 1)
                pe.wait_ge(evac, evb[l]["qkv"])
                for o in range(2):
                    for s in range(l, 2):
                        n = conv_items
                        if o:
                            pe.wait_ge(y_z, n - (2 - l) + 1)
                        if n:
                            pe.wait_ge(y_vt, n)
                        for c in range(2):
                            for ch in range(4):
                                last = TR(PS[:, 4 + c, ch * P:(ch + 1) * P], U[:, ch, s * L + c * P:s * L + (c + 1) * P], ident[:])
                        last.then_inc(y_t, 1)
                        pe.wait_ge(y_vt, n + 1)
                        if n:
                            pe.wait_ge(y_y, n)
                        for g in range(4):
                            for c in range(2):
                                last = MM(PS[0:BINS, g, :], dftf[:, c, g * BINS:(g + 1) * BINS], VT[:, c, :], start=c == 0, stop=c == 1)
                        last.then_inc(y_d, 1)
                        pe.wait_ge(y_y, n + 1)
                        if n:
                            pe.wait_ge(y_z, n)
                        for ch in range(4):
                            for g in range(4):
                                last = MM(PS[:, 6 + ch // 2, (ch % 2) * L:(ch % 2 + 1) * L], Y[:, g, ch * P:(ch + 1) * P], dfti[:, g, :],
                                          start=g == 0, stop=g == 3)
                        last.then_inc(y_i, 1)
                        conv_items += 1
                for n in range(QKV_U):
                    ready(b["qkv"] + n)
                    pe.wait_ge(evac, evb[l]["qkv"] + n - 1)
                    if n == 0:
                        pe.wait_ge(y_z, conv_items)
                    if n < 4:
                        last = features(n % 2, 2 * (n % 2), 0, HH, HL)
                    else:
                        for tc in range(4):
                            o = PS[:, 2 * (n % 2) + tc // 2, (tc % 2) * BLK:(tc % 2 + 1) * BLK]
                            for k in range(DK):
                                w = slice(k * BLK, (k + 1) * BLK)
                                x_ = slice(tc * P, (tc + 1) * P)
                                MM(o, HH[:, k, x_], WH[:, n % 2, w], start=k == 0, stop=False)
                                MM(o, HL[:, k, x_], WH[:, n % 2, w], start=False, stop=False)
                                last = MM(o, HH[:, k, x_], WL[:, n % 2, w], start=False, stop=k == DK - 1)
                    last.then_inc(unit_done, 1)
                pe.wait_ge(bias_in, 16 * 17 * (l + 1))
                for h in range(HEADS):
                    if h >= 4:
                        pe.wait_ge(a_bias, HEADS * l + h - 3)
                    MM(PS[:, 4 + h % 4, 0:6 * GRID], flip[:], bias[:, h, :], start=True, stop=True).then_inc(a_flip, 1)
                pe.wait_ge(evac, evb[l]["merge"])
                pe.wait_ge(a_bias, HEADS * (l + 1))

                def scores(n, qc, h):
                    r = slice(HD * (h % 2), HD * (h % 2) + HD)
                    width = TOK if qc >= 2 else L
                    if n >= 2:
                        pe.wait_ge(a_sc, n - 1)
                    MM(PS[:, n % 2, 0:width], QK[r, h // 2, qc * P:(qc + 1) * P], QK[r, 4 + h // 2, 0:width],
                       start=True, stop=True).then_inc(a_s, 1)

                def turn(n, qc):
                    pe.wait_ge(a_ex, n + 1)
                    if n >= 2:
                        pe.wait_ge(a_pt, n - 1)
                    for kc in range(4 if qc >= 2 else 2):
                        last = TR(PS[:, 2 + n % 2, kc * P:(kc + 1) * P], S[:, n % 2, kc * P:(kc + 1) * P], ident[:])
                    last.then_inc(a_t, 1)

                def attend(n, qc, h):
                    pe.wait_ge(a_pt, n + 1)
                    nk = 4 if qc >= 2 else 2
                    for kc in range(nk):
                        last = MM(PS[:, 4 + qc % 2, h * HD:(h + 1) * HD], PT[:, n % 2, kc * P:(kc + 1) * P],
                                  V[:, kc, h * HD:(h + 1) * HD], start=kc == 0, stop=kc == nk - 1)
                    last.then_inc(a_o, 1)

                for qc in range(2 * l, 4):
                    n0 = att_n
                    for h in range(HEADS + 2):
                        if h < HEADS:
                            scores(n0 + h, qc, h)
                        if 1 <= h <= HEADS:
                            turn(n0 + h - 1, qc)
                        if h >= 2:
                            attend(n0 + h - 2, qc, h - 2)
                    att_n += HEADS
                    pe.wait_ge(a_on, att_q + 1)
                    for c in range(4):
                        last = TR(PS[:, 6 + qc % 2, c * P:(c + 1) * P], OT[:, qc, c * P:(c + 1) * P], ident[:])
                    last.then_inc(a_ot, 1)
                    att_q += 1
                pe.wait_ge(a_lo, att_q)
                with pe.Fori(0, 2) as i:
                    for n in range(6):
                        pair, kind = n // 3, n % 3
                        ready(b["merge"] + 6 * i + n)
                        if kind == 0:
                            pe.wait_ge(m_sig, 2 * (4 * l + 2 * i + pair) + 1)
                        if kind == 2:
                            pe.wait_ge(m_sum, 4 * l + 2 * i + pair + 1)
                        if kind < 2:
                            last = features(n % 2, 2 * kind, c0, HH, HL)
                        else:
                            features(n % 2, 4, c0, OAH, OAL, range(4), 0)
                            last = features(n % 2, 6, c0, OHH, OHL, range(4), 4)
                        last.then_inc(unit_done, 1)
                pe.wait_ge(m_lo, 4 * l + 5)
                for n in range(WO_U):
                    ready(b["wo"] + n)
                    pe.wait_ge(evac, evb[l]["wo"] + n - 1)
                    features(n % 2, 2 * (n % 2), c0, MH, ML).then_inc(unit_done, 1)
                norm_sums(2 * l + 1)
                if l == 0:
                    pe.wait_ge(n_lo, items_before[1] + 16)
                    with pe.Fori(0, NB) as i:
                        ready(b["up"] + 2 * i)
                        pe.wait_ge(up_silu, i + 1)
                        features(0, 0, 0, HH, HL).then_inc(unit_done, 1)
                        ready(b["up"] + 2 * i + 1)
                        pe.wait_ge(up_mid, i + 1)
                        features(1, 2, 0, HH, HL).then_inc(unit_done, 1)
                    pe.wait_ge(up_lo, NB + 1)
                    with pe.Fori(0, DK // 2) as i:
                        for mm in range(2):
                            pe.wait_ge(evac, evb[l]["down"] + 2 * i + mm - 1)
                            for s in range(2):
                                ready(b["down"] + 4 * i + 2 * mm + s)
                                for n in range(11):
                                    w = slice(n * P, (n + 1) * P)
                                    k = 11 * s + n
                                    last = mm3(PS[:, mm, :], WH[:, s, w], WL[:, s, w], MDH[:, k, :], MDL[:, k, :],
                                               k == 0, k == FK - 1)
                                last.then_inc(unit_done, 1)
            pe.wait_ge(n_lo, 56)
            pe.wait_ge(r_split, 2)
            for c in range(2):
                x_ = slice(c * P, (c + 1) * P)
                for k in range(DK):
                    MM(PS[:, c, 0:NE], RH[:, k, x_], RTH[:, k, :], start=k == 0, stop=False)
                    MM(PS[:, c, 0:NE], RL[:, k, x_], RTH[:, k, :], start=False, stop=False)
                    last = MM(PS[:, c, 0:NE], RH[:, k, x_], RTL[:, k, :], start=False, stop=k == DK - 1)
                last.then_inc(r_pe, 1)
            pe.wait_ge(r_mask, 4)
            MM(PS[:, 4, 0:NE], tri[:], msk[:, 0, :], start=True, stop=True)
            MM(PS[:, 5, 0:NE], tri[:], msk[:, 1, :], start=True, stop=False)
            MM(PS[:, 5, 0:NE], ones[:], msk[:, 0, :], start=False, stop=True).then_inc(r_rank, 1)
            for c in range(2):
                for hf in range(2):
                    for k in range(4):
                        last = TR(PS[:, 2 * c + hf, k * P:(k + 1) * P], mo_h[:, 4 * hf + k, c * P:(c + 1) * P], ident[:])
                    last.then_inc(h_tr, 1)
            pe.wait_ge(h_ev, 4)
            for g in range(2):
                if g:
                    pe.wait_ge(sc_ev, 1 + 4 * NE)
                for q in range(4):
                    pe.wait_ge(p_sel, NE * g + 2 * q + 2)
                    for j in range(2):
                        for c in range(2):
                            last = TR(PS[:, q, j * L + c * P:j * L + (c + 1) * P], selw[:, c, 2 * q + j, :], ident[:])
                    last.then_inc(p_tr, 1)
                pe.wait_ge(p_selT, 4 * g + 4)
                if g == 0:
                    for k in range(3):
                        pe.nop().then_inc(e_use[k], 1)
                    pe.nop().then_inc(sc_pe, 1)
                with pe.Fori(0, NE) as e:
                    B0 = g * NE * NB + e * NB
                    E0 = g * NE + e
                    pe.wait_ge(sc_ev, 4 * E0 + 1)
                    for q in range(2):
                        for k in range(4):
                            for c in range(2):
                                last = MM(PS[:, 5 + q, k * P:(k + 1) * P], mo_ht[:, c, (4 * q + k) * P:(4 * q + k + 1) * P],
                                          sel[:, c, bass.ds(e, 1), :].rearrange("p e j -> p (e j)"), start=c == 0, stop=c == 1)
                        last.then_inc(g_pe, 1)
                    pe.wait_ge(g_lo, 2 * E0 + 2)

                    def up(kind, b):
                        pe.wait_ge(e_lo[kind], B0 + b + 2)
                        for k in range(DK):
                            w = slice(k * BLK, (k + 1) * BLK)
                            o = PS[:, kind, 0:BLK]
                            MM(o, GH[:, k, :], EH[:, kind, w], start=k == 0, stop=False)
                            MM(o, GH[:, k, :], EL[:, kind, w], start=False, stop=False)
                            last = MM(o, GL[:, k, :], EH[:, kind, w], start=False, stop=k == DK - 1)
                        last.then_inc(e_use[kind], 1)

                    def turn_mid(b):
                        pe.wait_ge(e_mid, B0 + b + 2)
                        for k in range(2):
                            last = TR(PS[:, 2, k * P:(k + 1) * P], mid[:, k * P:(k + 1) * P], ident[:])
                        last.then_inc(e_tr, 1)

                    def down(b):
                        pe.wait_ge(e_tl, B0 + b + 1)
                        pe.wait_ge(e_lo[2], B0 + b + 2)
                        for hf in range(2):
                            for k in range(2):
                                w = slice(k * D + hf * 512, k * D + (hf + 1) * 512)
                                o = PS[:, 3 + hf, :]
                                MM(o, TH[:, k, :], EH[:, 2, w], start=b == 0 and k == 0, stop=False)
                                MM(o, TH[:, k, :], EL[:, 2, w], start=False, stop=False)
                                last = MM(o, TL[:, k, :], EH[:, 2, w], start=False, stop=b == NB - 1 and k == 1)
                        last.then_inc(e_use[2], 1)

                    for b in range(NB + 1):
                        if b < NB:
                            pe.wait_ge(e_silu, B0 + b) if b else None
                            up(0, b)
                        if b:
                            turn_mid(b - 1)
                        if b < NB:
                            pe.wait_ge(e_mid, B0 + b + 1)
                            up(1, b)
                        if b:
                            down(b - 1)
                    pe.wait_ge(y_ev, E0 + 1)
                    for r in range(4):
                        if r >= 2:
                            pe.wait_ge(sc_ev, 4 * E0 + r)
                        for j in range(2):
                            f = 2 * r + j
                            last = MM(PS[:, 5 + r % 2, j * L:(j + 1) * L], yexp[:, f * P:(f + 1) * P],
                                      selT[:, bass.ds(e, 1), :].rearrange("p e t -> p (e t)"), start=True, stop=True)
                        last.then_inc(sc_pe, 1)
            norm_sums(4)


class Chain:

    def __init__(self, eng, sem):
        self.eng, self.sem, self.n, self.i, self.per = eng, sem, 0, None, 0

    def enter(self, i, per, trips):
        self.i, self.per, self.trips, self.start = i, per, trips, self.n

    def exit(self):
        assert self.n - self.start == self.per, (self.n - self.start, self.per)
        self.i, self.n = None, self.start + self.per * self.trips

    def link(self, ins):
        ins.then_inc(self.sem, 1)
        self.n += 1
        self.eng.wait_ge(self.sem, self.n if self.i is None else self.n + self.per * self.i)


def tables():
    pos = np.arange(L, dtype=np.float32)
    bands = np.linspace(1e-4, 15.0, 16, dtype=np.float32)
    ang = (np.float32(2.0 * math.pi / L) * pos[:, None] * bands[None, :]).astype(np.float32)
    feats = np.concatenate([(pos / (L - 1))[:, None], np.cos(ang), -np.sin(ang)], axis=-1)
    dist = np.abs(pos - L // 2) * np.float32(2.0 / L)
    rates = np.abs(np.linspace(math.log(1e-2) / 1.5, math.log(1e-2) / 0.3, 2 * HY_W, dtype=np.float32))
    decay = np.exp(-dist[:, None] * rates[None, :]) + 0.05
    j = np.arange(L)[:, None].astype(np.float64)
    k = np.arange(2 * BINS)[None, :]
    w = 2 * np.pi / NFFT
    re, im = np.cos(w * j * k), -np.sin(w * j * k)
    nyq = np.cos(np.pi * j[:, 0])
    imn = im.copy()
    imn[:, 0] = nyq
    ren = re[:, :BINS].copy()
    ren[:, 0] = nyq
    fwd = np.concatenate([re, imn], axis=1)
    fil = np.concatenate([re, im * (k > 0), ren], axis=1)
    n = (np.arange(L) + L // 2)[None, :]
    kk = np.arange(2 * BINS)[:, None]
    ire = np.where(kk == 0, 1.0, 2 * np.cos(w * kk * n)) / NFFT
    iim = np.where(kk == 0, np.cos(np.pi * n), -2 * np.sin(w * kk * n)) / NFFT
    inv = np.concatenate([ire, iim], axis=0).reshape(4, BINS, L)
    c = np.arange(P) % GRID
    start = np.clip(c - WIN // 2, 0, GRID - WIN)[:, None]
    col = np.arange(GRID)[None, :]
    mask = np.where((col >= start) & (col < start + WIN), 0.0, NEG)
    f = np.float32
    chunks = lambda a: np.ascontiguousarray(a.reshape(2, P, -1).transpose(1, 0, 2)).astype(f)
    return {
        "posT": np.ascontiguousarray(feats.T).astype(f),
        "decay": np.ascontiguousarray(decay.reshape(2, P, 2, HY_W).transpose(1, 0, 2, 3)).astype(f),
        "dftf": chunks(fwd), "dftk": chunks(fil),
        "dfti": np.ascontiguousarray(inv.transpose(1, 0, 2)).astype(f),
        "mask": np.tile(mask, (1, 6)).astype(f),
        "ident": np.eye(P, dtype=f),
        "flip": np.kron(np.eye(2), np.eye(GRID)[::-1]).astype(f),
        "tri": np.triu(np.ones((P, P), f), 1),
        "iota": np.tile(np.arange(L, dtype=f), (P, 1)),
    }


def kernel(**inputs):
    import concourse.bacc as bacc
    from concourse.bass_utils import run_bass_kernel_spmd as run

    a = {k: np.asarray(v) for k, v in inputs.items()}

    def features_first(v, lead):
        v = v.reshape(*v.shape[:-1], v.shape[-1] // P, P)
        return np.moveaxis(v, -1, 0)

    arrays = {
        "xT": a["x"][0].T, "ctxT": a["ctx"][0].T,
        "cc": np.moveaxis(features_first(np.stack([a["c_ctx"], a["c"][0]]), 1), 1, 2),
        "w_mod": a["w_mod"], "b_mod": features_first(a["b_mod"], 1),
        "norm1_g": features_first(a["norm1_g"], 1), "norm2_g": features_first(a["norm2_g"], 1),
        "final_g": features_first(a["final_g"], 0),
        "w_in": a["w_in"], "rpb": a["rpb"],
        "hy_conv_w": features_first(a["hy_conv_w"], 2), "hy_conv_b": features_first(a["hy_conv_b"], 1),
        "hy_w1": a["hy_w1"], "hy_w2": a["hy_w2"], "hy_w3": a["hy_w3"],
        "fvec": np.stack([a["hy_b1"], a["hy_freq"][:, 0], a["hy_b2"], a["hy_freq"][:, 1]], axis=-1),
        "hy_bias": features_first(a["hy_bias"], 2),
        "w_opab": np.concatenate([a["w_o"], np.concatenate([a["w_pa"], a["w_pb"]], axis=1)], axis=2),
        "ffn_w1": a["ffn_w1"][0], "ffn_w3": a["ffn_w3"][0], "ffn_w2": a["ffn_w2"][0],
        "moe_router": np.moveaxis(a["moe_router"][0].reshape(DK, P, NE), 1, 0),
        "moe_w1": a["moe_w1"][0].reshape(NE * D, FF), "moe_w3": a["moe_w3"][0].reshape(NE * D, FF),
        "moe_w2": a["moe_w2"][0].reshape(NE * FF, D),
        **tables(),
    }
    arrays = {k: np.ascontiguousarray(v) for k, v in arrays.items()}
    nc = bacc.Bacc("TRN2", target_bir_lowering=False, num_devices=1)
    t = {k: nc.dram_tensor("in_" + k, v.shape, mybir.dt.from_np(v.dtype), kind="ExternalInput").ap() for k, v in arrays.items()}
    out = nc.dram_tensor("out_features", (D, L), F32, kind="ExternalOutput").ap()
    build(nc, t, out)
    r = run(nc, [{"in_" + k: v for k, v in arrays.items()}], core_ids=[0])
    return np.ascontiguousarray(r.results[0]["out_features"].T)[None]
```

```python
import math
from contextlib import ExitStack

import numpy as np
import concourse.bass as bass
from concourse import mybir

F32 = mybir.dt.float32
R32 = mybir.dt.float32r
U32 = mybir.dt.uint32
ALU = mybir.AluOpType
ACT = mybir.ActivationFunctionType
AX = mybir.AxisListType.X

P = 128
D = 1024
DK = D // P
L = 256
TOK = 2 * L
PROJ = 5120
ATT_W, HY_W = 512, 512
OFF_U, OFF_GA, OFF_GB = 1536, 3072, 4096
HEADS, HD = 8, 64
GRID, WIN = 64, 16
RPB_R, RPB_C = 15, 31
FF = 2816
FK = FF // P
NE = 8
BLK = 256
NB = FF // BLK
NFFT = 384
BINS = 96
EPS = 1e-6
SCALE = HD ** -0.5
NEG = -1e30
MAGIC = 1.5 * 2.0 ** 23
TWO_PI_PARTS = (6.28125, 0.0019350051879882812, 3.0199157663446036e-07)
PI_CLIP = 3.1415925
TAPB = (0, 1, 5, 6)
SCB = (7, 0, 1, 2)
N_SMALL, N_FILT = 11, 9

MOD_U, U_U, QKV_U, MERGE_U, WO_U, UP_U, DOWN_U = 24, 6, 6, 12, 4, 22, 16
SHIFT1, SCALE1, GATE1, SHIFT2, SCALE2, GATE2 = range(6)


RAW, SPLIT = 6, 4
ORDER = [(0, 0), (1, 0)] + [u for b in range(1, NB) for u in ((0, b), (1, b), (2, b - 1))] + [(2, NB - 1)]
NU = len(ORDER)
POS = {u: j for j, u in enumerate(ORDER)}


def slot_before(j, slots):
    return j - slots if j >= slots else max(q for q in range(NU) if q % slots == j % slots) - NU


def unit_bases():
    base, n = [{}, {}], 0
    for l in range(2):
        stages = [("mod", MOD_U), ("u", U_U), ("qkv", QKV_U), ("merge", MERGE_U), ("wo", WO_U)]
        if l == 0:
            stages += [("up", UP_U), ("down", DOWN_U)]
        for name, count in stages:
            base[l][name] = n
            n += count
    return base, n


def build(nc, t, out):
    base, n_units = unit_bases()
    top = ExitStack()
    with top:
        def sem(name):
            return top.enter_context(nc.semaphore(name))

        def sb(stack, name, shape, dt=F32):
            return stack.enter_context(nc.sbuf_tensor(name, shape, dt))

        X = sb(top, "x_residual", [P, DK, TOK])
        ident = sb(top, "ident", [P, P])
        flip = sb(top, "flip", [P, P])
        ones = sb(top, "ones", [P, P])
        eps = sb(top, "eps", [P, 1])
        cvec = sb(top, "cvec", [P, DK, 2])
        svec = sb(top, "svec", [P, DK, 2])
        SH = sb(top, "silu_c_hi", [P, DK, P], R32)
        SL = sb(top, "silu_c_lo", [P, DK, P], R32)
        mrow = sb(top, "modulation_rows", [2, 2, BLK])
        bmod = sb(top, "b_mod", [P, 2, 48])
        g1 = sb(top, "norm1_g", [P, 2, DK])
        g2 = sb(top, "norm2_g", [P, 2, DK])
        gf = sb(top, "final_g", [P, DK])
        cw = sb(top, "conv_w", [P, 2, 3, 12])
        cb = sb(top, "conv_b", [P, 2, 12])
        hyb = sb(top, "hyena_bias", [P, 2, 2, 4])
        mod = sb(top, "modulation", [P, 48, 2])
        na1 = sb(top, "norm1_scale", [P, DK, 2])
        na2 = sb(top, "norm2_scale", [P, DK, 2])
        rs = sb(top, "rms", [P, TOK])
        sq = sb(top, "squares", [P, 2, TOK])
        router = sb(top, "router", [P, DK, NE])
        RTH = sb(top, "router_hi", [P, DK, NE], R32)
        RTL = sb(top, "router_lo", [P, DK, NE], R32)

        PS = top.enter_context(nc.psum_tensor("psum", [P, 8, 512], F32))

        st = ExitStack()
        raw = sb(st, "raw_units", [P, 2, 2048])
        WH = sb(st, "units_hi", [P, 2, 2048], R32)
        WL = sb(st, "units_lo", [P, 2, 2048], R32)
        HH = sb(st, "h_hi", [P, DK, TOK], R32)
        HL = sb(st, "h_lo", [P, DK, TOK], R32)
        mix = ExitStack()
        fi = ExitStack()
        decay = sb(fi, "decay", [P, 2, 2, HY_W])
        fw3 = sb(fi, "filter_w3", [64, 2, HY_W])
        taps = sb(fi, "filter_taps", [P, 2, HY_W])
        fi.close()
        OHH = sb(mix, "hyena_out_hi", [P, 4, TOK], R32)
        OHL = sb(mix, "hyena_out_lo", [P, 4, TOK], R32)
        hy = ExitStack()
        spec = sb(hy, "filter_spectra", [BINS, 2, 5, HY_W])
        dftf = sb(hy, "dft_forward", [P, 2, 4 * BINS])
        dftk = sb(hy, "dft_filter", [P, 2, 5 * BINS])
        dfti = sb(hy, "dft_inverse", [BINS, 4, L])
        U = sb(hy, "hyena_u", [P, 12, TOK])
        fl = ExitStack()
        posT = sb(fl, "positions", [33, L])
        fw1 = sb(fl, "filter_w1", [33, 64])
        fw2 = sb(fl, "filter_w2", [64, 64])
        fb = sb(fl, "filter_vectors", [64, 4])
        arg = sb(fl, "sine_argument", [64, 2, L])
        turns = sb(fl, "sine_turns", [64, L])
        act1 = sb(fl, "filter_act", [64, 2, L])
        fl.close()
        cv = ExitStack()
        VT = sb(cv, "tokens_major", [P, 2, HY_W])
        Y = sb(cv, "product_spectrum", [BINS, 4, HY_W])
        pt = sb(cv, "product_terms", [BINS, 2, HY_W])
        zt = sb(cv, "conv_sum", [P, 4, L])
        cv.close()
        hy.close()
        OAH = sb(mix, "att_out_hi", [P, 4, TOK], R32)
        OAL = sb(mix, "att_out_lo", [P, 4, TOK], R32)
        at = ExitStack()
        QK = sb(at, "qk", [P, 8, TOK])
        V = sb(at, "v", [P, 4, ATT_W])
        bias = sb(at, "att_bias", [P, HEADS, 6 * GRID])
        mask = sb(at, "att_mask", [P, 6 * GRID])
        S = sb(at, "scores", [P, 2, TOK])
        nmax = sb(at, "neg_max", [P, 32])
        psums = sb(at, "prob_sums", [P, 32])
        rsum = sb(at, "recip_sums", [P, 32])
        PT = sb(at, "probs_T", [P, 2, TOK])
        OT = sb(at, "att_tokens_major", [P, 4, ATT_W])
        at.close()
        mg = ExitStack()
        MH = sb(mg, "merged_hi", [P, DK, TOK], R32)
        ML = sb(mg, "merged_lo", [P, DK, TOK], R32)
        sga = sb(mg, "sig_a", [P, 2, TOK])
        sgb = sb(mg, "sig_b", [P, 2, TOK])
        mg.close()
        mix.close()
        ff = ExitStack()
        MDH = sb(ff, "mid_hi", [P, FK, TOK], R32)
        MDL = sb(ff, "mid_lo", [P, FK, TOK], R32)
        ff.close()
        st.close()
        mo = ExitStack()
        eraw = sb(mo, "expert_raw", [P, RAW, 2048])
        EH = sb(mo, "expert_hi", [P, SPLIT, 2048], R32)
        EL = sb(mo, "expert_lo", [P, SPLIT, 2048], R32)
        rt = ExitStack()
        RH = sb(rt, "moe_h_hi", [P, DK, L], R32)
        RL = sb(rt, "moe_h_lo", [P, DK, L], R32)
        rt.close()
        selw = sb(mo, "select_weighted", [P, 2, NE, P])
        sel = sb(mo, "select", [P, 2, NE, P])
        mt = ExitStack()
        mo_h = sb(mt, "moe_h", [P, DK, L])
        mt.close()
        GH = sb(mo, "gathered_hi", [P, DK, P], R32)
        GL = sb(mo, "gathered_lo", [P, DK, P], R32)
        mo_ht = sb(mo, "moe_h_tokens", [P, 2, D])
        selT = sb(mo, "scatter", [P, NE, L])
        sil = sb(mo, "silu_block", [P, BLK])
        mid = sb(mo, "mid_block", [P, BLK])
        TH = sb(mo, "midT_hi", [P, 2, P], R32)
        TL = sb(mo, "midT_lo", [P, 2, P], R32)
        yexp = sb(mo, "expert_out", [P, D])
        logits = sb(mo, "logits", [P, 2, NE])
        tv = sb(mo, "top_values", [P, 2, 8])
        ti = sb(mo, "top_index", [P, 2, 8], U32)
        tif = sb(mo, "top_index_f", [P, 2, 8])
        gt = sb(mo, "top_gates", [P, 2, 4])
        oh = sb(mo, "one_hot", [P, 2, 4, NE])
        msk = sb(mo, "chosen", [P, 2, NE])
        wex = sb(mo, "expert_weight", [P, 2, NE])
        over = sb(mo, "overflow", [P, NE])
        overi = sb(mo, "overflow_flag", [P, NE], mybir.dt.int32)
        rank = sb(mo, "rank", [P, 2, NE])
        tri = sb(mo, "before", [P, P])
        iot = sb(mo, "iota", [P, L])
        mo.close()

        consts_in = sem("consts_in")
        x_in = sem("x_in")
        filt_in = sem("filt_in")
        bias_in = sem("bias_in")
        raw_in = [sem("raw_in0"), sem("raw_in1")]
        hi_done = sem("hi_done")
        lo_done = sem("lo_done")
        unit_done = sem("unit_done")
        evac = sem("evac")
        dve_chain = sem("dve_chain")
        act_chain = sem("act_chain")
        s_ready = sem("s_ready")
        sl_ready = sem("sl_ready")
        md_row, md_tr, md_out = (sem("md_" + n_) for n_ in ("row", "turn", "out"))
        setup_done = sem("setup_done")
        f_pe, f_dv, f_ac = sem("f_pe"), sem("f_dv"), sem("f_ac")
        n_sq, n_pe, n_rt = sem("n_sq"), sem("n_pe"), sem("n_rt")
        n_t, n_hi, n_lo = sem("n_t"), sem("n_hi"), sem("n_lo")
        c_ac = sem("c_ac")
        y_t, y_vt, y_d, y_y, y_i, y_z = (sem("y_" + s) for s in ("t", "vt", "d", "y", "i", "z"))
        y_hi, y_lo = sem("y_hi"), sem("y_lo")
        a_s, a_sc, a_ex, a_t, a_pt, a_o = (sem("a_" + s) for s in ("s", "sc", "ex", "t", "pt", "o"))
        a_on, a_ot, a_hi, a_lo = (sem("a_" + s) for s in ("on", "ot", "hi", "lo"))
        a_flip, a_bias = sem("a_flip"), sem("a_bias")
        m_sig, m_sum, m_hi, m_lo = (sem("m_" + s) for s in ("sig", "sum", "hi", "lo"))
        up_silu, up_mid, up_hi, up_lo = (sem("up_" + s) for s in ("silu", "mid", "hi", "lo"))
        out_done = sem("out_done")
        o_ready = sem("o_ready")
        r_split, r_pe, r_mask, r_rank, r_ev, h_tr, h_ev = (sem("r_" + s) for s in
            ("split", "pe", "mask", "rank", "ev", "htr", "hev"))
        flag_ready = sem("flag_ready")
        r_cnt = sem("r_cnt")
        p_sel, p_tr, p_selT = sem("p_sel"), sem("p_tr"), sem("p_selT")
        e_in = [sem(f"e_in{n}") for n in range(RAW)]
        e_hi, e_lo, e_use = sem("e_hi"), sem("e_lo"), sem("e_use")
        e_silu, e_mid, e_tr, e_th, e_tl = (sem("e_" + s) for s in ("silu", "mid", "tr", "th", "tl"))
        g_pe, g_hi, g_lo, y_ev, sc_pe, sc_ev = (sem("g_" + s) for s in
            ("pe", "hi", "lo", "yev", "scpe", "scev"))

        evb, n = [{}, {}], 0
        for l in range(2):
            n += 2 * (l == 0)
            for name, count in (("u", U_U), ("qkv", QKV_U), ("merge", 0), ("wo", WO_U)) + \
                    ((("up", 0), ("down", DK)) if l == 0 else ()):
                evb[l][name] = n
                n += count

        norm_c0 = [0, 0, 0, L, L]
        items_before = [0, 16, 32, 48, 56]

        block = top.enter_context(nc.Block())

        @block.sync
        def _(sp):
            def load(u, s, dst, src):
                sp.dma_start(dst, src).then_inc(raw_in[s], 16)

            def free(u):
                if not isinstance(u, int) or u >= 2:
                    sp.wait_ge(lo_done, u - 1)

            def std(w, col):
                return w[:, bass.ds(col, BLK)].rearrange("(k p) c -> p k c", p=P)

            def raw_std(s):
                return raw[:, s, :].rearrange("p (k c) -> p k c", k=DK)

            for l in range(2):
                b = base[l]
                for s in range(2):
                    free(b["mod"] + s)
                    load(0, s, raw_std(s), std(t["w_mod"][l], BLK * s))
                with sp.Fori(1, MOD_U // 2) as i:
                    for s in range(2):
                        free(b["mod"] + 2 * i + s)
                        load(0, s, raw_std(s), std(t["w_mod"][l], (2 * i + s) * BLK))
                with sp.Fori(0, U_U // 2) as i:
                    for s in range(2):
                        free(b["u"] + 2 * i + s)
                        load(0, s, raw_std(s), std(t["w_in"][l], OFF_U + (2 * i + s) * BLK))
                with sp.Fori(0, QKV_U // 2) as i:
                    for s in range(2):
                        free(b["qkv"] + 2 * i + s)
                        load(0, s, raw_std(s), std(t["w_in"][l], (2 * i + s) * BLK))
                with sp.Fori(0, 2) as i:
                    for n in range(6):
                        free(b["merge"] + 6 * i + n)
                        pair, kind = n // 3, n % 3
                        col = (2 * i + pair) * BLK
                        w = t["w_opab"][l] if kind == 2 else t["w_in"][l]
                        load(0, n % 2, raw_std(n % 2), std(w, (OFF_GA, OFF_GB, D)[kind] + col))
                with sp.Fori(0, WO_U // 2) as i:
                    for s in range(2):
                        free(b["wo"] + 2 * i + s)
                        load(0, s, raw_std(s), std(t["w_opab"][l], (2 * i + s) * BLK))
                if l == 0:
                    with sp.Fori(0, NB) as i:
                        for s, w in enumerate(("ffn_w1", "ffn_w3")):
                            free(b["up"] + 2 * i + s)
                            load(0, s, raw_std(s), std(t[w], i * BLK))
                    with sp.Fori(0, DK) as i:
                        for s in range(2):
                            free(b["down"] + 2 * i + s)
                            load(0, s, raw[:, s, 0:11 * P].rearrange("p (k c) -> p k c", k=11),
                                 t["ffn_w2"][s * 11 * P:(s + 1) * 11 * P, bass.ds(i * P, P)]
                                 .rearrange("(k p) c -> p k c", p=P))
            sp.wait_ge(lo_done, n_units)
            sp.wait_ge(unit_done, n_units)
            def experts(g):
                with sp.Fori(0, NE) as e:
                    E0 = g * NE + e
                    for j, (kind, b) in enumerate(ORDER):
                        sp.wait_ge(e_lo, NU + NU * E0 + slot_before(j, RAW) + 1)
                        dst = eraw[:, j % RAW, :]
                        if kind < 2:
                            w = t["moe_w1"] if kind == 0 else t["moe_w3"]
                            src = w[bass.ds(e * D, D), b * BLK:(b + 1) * BLK].rearrange("(k p) c -> p k c", p=P)
                            dst = dst.rearrange("p (k c) -> p k c", k=DK)
                        else:
                            src = t["moe_w2"][bass.ds(e * FF + b * BLK, BLK), :].rearrange("(k p) c -> p k c", p=P)
                            dst = dst.rearrange("p (k c) -> p k c", k=2)
                        sp.dma_start(dst, src).then_inc(e_in[j % RAW], 16)

            experts(0)
            sp.wait_ge(flag_ready, 1)
            with sp.If(sp.value_load(overi[0:1, 0:1], min_val=0, max_val=1) == 1):
                experts(1)
            sp.wait_ge(o_ready, DK)
            sp.dma_start(out.rearrange("(k p) t -> p k t", p=P), X[:, :, L:TOK]).then_inc(out_done, 16)
            sp.wait_ge(out_done, 16)

        @block.gpsimd
        def _(pool):
            def load(dst, src, s):
                pool.dma_start(dst, src).then_inc(s, 16)
            small = [(cvec[:], t["cc"]), (ident[:], t["ident"]), (flip[:], t["flip"]), (bmod[:], t["b_mod"]),
                     (g1[:], t["norm1_g"]), (g2[:], t["norm2_g"]), (gf[:], t["final_g"]),
                     (cw[:], t["hy_conv_w"]), (cb[:], t["hy_conv_b"]), (hyb[:], t["hy_bias"]),
                     (router[:], t["moe_router"])]
            assert len(small) == N_SMALL
            for dst, src in small:
                load(dst, src, consts_in)
            load(X[:, :, 0:L], t["ctxT"].rearrange("(k p) t -> p k t", p=P), x_in)
            load(X[:, :, L:TOK], t["xT"].rearrange("(k p) t -> p k t", p=P), x_in)
            for l in range(2):
                if l == 1:
                    pool.wait_ge(unit_done, base[1]["mod"])
                    pool.wait_ge(evac, evb[0]["down"] + DK)
                filt = [(dftf[:], t["dftf"]), (dftk[:], t["dftk"]), (dfti[:], t["dfti"]), (posT[:], t["posT"]),
                        (decay[:], t["decay"]), (fw1[:], t["hy_w1"][l]), (fw2[:], t["hy_w2"][l]),
                        (fw3[:], t["hy_w3"][l].rearrange("f (o c) -> f o c", o=2)), (fb[:], t["fvec"][l])]
                assert len(filt) == N_FILT
                for dst, src in filt:
                    load(dst, src, filt_in)
                pool.wait_ge(y_z, (4 if l == 0 else 6))
                pool.wait_ge(y_lo, (2 if l == 0 else 3))
                load(mask[:], t["mask"], bias_in)
                rp = t["rpb"]
                for h in range(HEADS):
                    for half in range(2):
                        first = ((l * HEADS + h) * RPB_R + 5 - half) * RPB_C + WIN - GRID
                        src = bass.AP(rp.tensor, first, [[1, GRID], [RPB_C, 6], [1, GRID]])
                        load(bias[half * GRID:(half + 1) * GRID, h, :].rearrange("p (r c) -> p r c", r=6), src, bias_in)
            pool.wait_ge(unit_done, n_units)
            load(tri[:], t["tri"], bias_in)
            load(iot[:], t["iota"], bias_in)

        @block.scalar
        def _(act):
            A = nc.scalar.activation

            def hi(u, s, half):
                act.wait_ge(raw_in[s], 16 * half + 16)
                if not isinstance(u, int) or u >= 2:
                    act.wait_ge(unit_done, u - 1)
                A(WH[:, s, :], raw[:, s, :], ACT.Copy).then_inc(hi_done, 1)

            def ahead(b, n, s):
                u = b + n + 2
                half = (u - s) // 2 if isinstance(u, int) else None
                hi(u, s, half)

            def ahead_loop(b, i, stride, n):
                u0 = b + n + 2
                hi(u0 + stride * i, n % 2, u0 // 2 + (stride // 2) * i)

            def norm_roots(q):
                c0 = norm_c0[q]
                if q == 0:
                    act.wait_ge(x_in, 32)
                elif q < 4:
                    act.wait_ge(evac, (None, evb[0]["wo"] + WO_U, evb[0]["down"] + DK, evb[1]["wo"] + WO_U)[q])
                for k in range(DK):
                    if 8 * q + k >= 2:
                        act.wait_ge(n_pe, 8 * q + k - 1)
                    if q and k < 2:
                        act.wait_ge(n_lo, items_before[q])
                    A(sq[:, k % 2, c0:TOK], X[:, k, c0:TOK], ACT.Square).then_inc(n_sq, 1)
                act.wait_ge(n_pe, 8 * q + 8)
                A(rs[:, c0:TOK], PS[:, 7, c0:TOK], ACT.Sqrt, bias=eps[:, 0:1], scale=1.0 / D).then_inc(n_rt, 1)

            def norm_hi(q, shift, hh):
                streams = range(1 if q == 3 else 0, 2)
                it = items_before[q]
                for k in range(DK):
                    for s in streams:
                        act.wait_ge(n_t, it + 1)
                        dst = hh[:, k, 0:L] if q == 3 else hh[:, k, s * L:(s + 1) * L]
                        A(dst, sq[:, it % 2, 0:L], ACT.Identity,
                          bias=mod[:, shift * DK + k, s:s + 1]).then_inc(n_hi, 1)
                        if q == 3:
                            A(mo_h[:, k, :], sq[:, it % 2, 0:L], ACT.Identity,
                              bias=mod[:, shift * DK + k, s:s + 1]).then_inc(n_hi, 1)
                        it += 1

            act.wait_ge(consts_in, 16 * N_SMALL)
            act.wait_ge(setup_done, 4)
            A(svec[:], cvec[:], ACT.Silu).then_inc(act_chain, 1)
            act.wait_ge(act_chain, 1)
            A(SH[:, :, 0:2], svec[:], ACT.Copy).then_inc(s_ready, 1)
            A(RTH[:], router[:], ACT.Copy).then_inc(r_split, 1)
            cb_seen = 0
            conv_items = 0
            att_n = att_q = 0
            for l in range(2):
                b = base[l]
                c0 = 0 if l == 0 else L
                for j in range(2):
                    act.wait_ge(f_dv, 4 * l + j + 1)
                    A(act1[:, j, :], arg[:, j, :], ACT.Sin).then_inc(f_ac, 1)
                for o in range(2):
                    act.wait_ge(f_pe, 5 * l + 4 + o)
                    for g in range(5):
                        last = A(spec[:, o, g, :], PS[0:BINS, g, :], ACT.Copy)
                    last.then_inc(f_ac, 1)
                def mod_row(i, n):
                    act.wait_ge(unit_done, b["mod"] + 2 * i + n + 1)
                    act.wait_ge(md_tr, MOD_U * l + 2 * i + n + 1)
                    A(mrow[:, n, :], PS[0:2, n, 0:BLK], ACT.Copy).then_inc(md_row, 1)

                if l == 0:
                    hi(0, 0, 0)
                    hi(1, 1, 0)
                    for n in range(2):
                        hi(2 + n, n, 1)
                        mod_row(0, n)
                with act.Fori(1 - l, MOD_U // 2) as i:
                    for n in range(2):
                        ahead_loop(b["mod"], i, 2, n)
                        mod_row(i, n)
                norm_roots(2 * l)
                norm_hi(2 * l, SHIFT1, HH)
                with act.Fori(0, U_U // 2) as i:
                    for n in range(2):
                        ahead_loop(b["u"], i, 2, n)
                        act.wait_ge(unit_done, b["u"] + 2 * i + n + 1)
                        for j in range(2):
                            m = 4 * i + 2 * n + j
                            A(U[:, m, c0:TOK], PS[:, 2 * n + j, c0:TOK], ACT.Identity,
                              bias=cb[:, l, bass.ds(m, 1)], scale=cw[:, l, 1, bass.ds(m, 1)]).then_inc(c_ac, 1)
                for o in range(2):
                    for s in range(1 if l else 0, 2):
                        n = conv_items
                        act.wait_ge(y_t, n + 1)
                        if n:
                            act.wait_ge(y_d, n)
                        for c in range(2):
                            last = A(VT[:, c, :], PS[:, 4 + c, :], ACT.Copy)
                        last.then_inc(y_vt, 1)
                        if o == 1:
                            act.wait_ge(y_z, n + 1)
                            A(OHH[:, :, s * L:(s + 1) * L], zt[:, :, :], ACT.Copy).then_inc(y_hi, 1)
                        conv_items += 1
                with act.Fori(0, QKV_U // 2) as i:
                    for n in range(2):
                        ahead_loop(b["qkv"], i, 2, n)
                def probs_out(n, width):
                    act.wait_ge(a_t, n + 1)
                    if n >= 2:
                        act.wait_ge(a_o, n - 1)
                    A(PT[:, n % 2, 0:width], PS[:, 2 + n % 2, 0:width], ACT.Copy).then_inc(a_pt, 1)
                for qc in range(0 if l == 0 else 2, 4):
                    width = TOK if qc >= 2 else L
                    for h in range(HEADS):
                        n = att_n
                        act.wait_ge(a_sc, n + 1)
                        A(S[:, n % 2, 0:width], S[:, n % 2, 0:width], ACT.Exp, bias=nmax[:, n % 32:n % 32 + 1],
                          accum_out=psums[:, n % 32:n % 32 + 1]).then_inc(a_ex, 1)
                        if h:
                            probs_out(n - 1, width)
                        att_n += 1
                    probs_out(att_n - 1, width)
                    act.wait_ge(a_ot, att_q + 1)
                    A(OAH[:, :, qc * P:(qc + 1) * P], PS[:, 6 + qc % 2, :].rearrange("p (c q) -> p c q", c=4),
                      ACT.Copy).then_inc(a_hi, 1)
                    att_q += 1
                mb = 4 * l
                if l == 0:
                    act.nop().then_inc(m_sig, 1)
                with act.Fori(0, 2) as i:
                    for n in range(6):
                        pair, kind = n // 3, n % 3
                        ahead_loop(b["merge"], i, 6, n)
                        act.wait_ge(unit_done, b["merge"] + 6 * i + n + 1)
                        if kind < 2:
                            act.wait_ge(m_lo, mb + 2 * i + pair + 1)
                            dst = sga if kind == 0 else sgb
                            A(dst[:, :, c0:TOK], PS[:, 2 * kind:2 * kind + 2, c0:TOK], ACT.Sigmoid).then_inc(m_sig, 1)
                        else:
                            act.wait_ge(m_sum, mb + 2 * i + pair + 2)
                            A(MH[:, bass.ds(2 * (2 * i + pair), 2), c0:TOK], sga[:, :, c0:TOK], ACT.Copy).then_inc(m_hi, 1)
                for n in range(WO_U):
                    if l == 0 or n < 2:
                        hi(b["wo"] + n + 2, n % 2, b["wo"] // 2 + (n + 2) // 2)
                norm_roots(2 * l + 1)
                if l == 0:
                    norm_hi(1, SHIFT2, HH)
                    act.nop().then_inc(up_silu, 1)
                    with act.Fori(0, NB) as i:
                        ahead_loop(b["up"], i, 2, 0)
                        act.wait_ge(unit_done, b["up"] + 2 * i + 1)
                        act.wait_ge(up_lo, i + 1)
                        A(sq[:, :, :], PS[:, 0:2, :], ACT.Silu).then_inc(up_silu, 1)
                        ahead_loop(b["up"], i, 2, 1)
                        act.wait_ge(up_mid, i + 2)
                        A(MDH[:, bass.ds(2 * i, 2), :], sq[:, :, :], ACT.Copy).then_inc(up_hi, 1)
                    with act.Fori(0, DK) as i:
                        for n in range(2):
                            ahead_loop(b["down"], i, 2, n)
                else:
                    act.wait_ge(unit_done, n_units)
                    norm_hi(3, SHIFT2, RH)
            for c in range(2):
                act.wait_ge(r_mask, c + 1)
                A(gt[:, c, 1:2], gt[:, c, 0:1], ACT.Exp).then_inc(r_ev, 1)
            for c in range(2):
                for hf in range(2):
                    act.wait_ge(h_tr, 2 * c + hf + 1)
                    A(mo_ht[:, c, hf * 512:(hf + 1) * 512], PS[:, 2 * c + hf, :], ACT.Copy).then_inc(h_ev, 1)
            def experts(g):
                for q in range(4):
                    act.wait_ge(p_tr, 4 * g + q + 1)
                    A(selT[:, 2 * q:2 * q + 2, :], PS[:, q, :].rearrange("p (e t) -> p e t", e=2), ACT.Copy).then_inc(p_selT, 1)

                def gathered(E0):
                    for q in range(2):
                        act.wait_ge(g_pe, 2 * E0 + q + 1)
                        A(GH[:, 4 * q:4 * q + 4, :], PS[:, 5 + q, :].rearrange("p (k j) -> p k j", k=4), ACT.Copy).then_inc(g_hi, 1)

                def ehi(E0, j):
                    r = j % RAW
                    loads = len(range(r, NU, RAW))
                    act.wait_ge(e_in[r], 16 * loads * E0 + 16 * (j // RAW + 1))
                    act.wait_ge(e_use, NU + NU * E0 + slot_before(j, SPLIT) + 1)
                    A(EH[:, j % SPLIT, :], eraw[:, r, :], ACT.Copy).then_inc(e_hi, 1)

                def turned(E0, b):
                    act.wait_ge(e_tr, NB * E0 + b + 1)
                    if b:
                        act.wait_ge(e_use, NU + NU * E0 + POS[(2, b - 1)] + 1)
                    A(TH[:], PS[:, 2, 0:2 * P].rearrange("p (k j) -> p k j", k=2), ACT.Copy).then_inc(e_th, 1)

                def expert(e, last):
                    E0 = g * NE + e
                    for j, (kind, b) in enumerate(ORDER):
                        if kind == 0:
                            act.wait_ge(e_use, NU + NU * E0 + j + 1)
                            act.wait_ge(e_mid, NB * E0 + b + 1)
                            A(sil[:], PS[:, 0, 0:BLK], ACT.Silu).then_inc(e_silu, 1)
                            if b:
                                turned(E0, b - 1)
                        if j + SPLIT < NU:
                            ehi(E0, j + SPLIT)
                        if j == NU - 2:
                            turned(E0, NB - 1)
                    if not last:
                        for j in range(SPLIT - 2):
                            ehi(E0 + 1, j)
                    act.wait_ge(e_use, NU + NU * E0 + NU)
                    act.wait_ge(sc_pe, 4 * E0 + 4)
                    A(yexp[:, 0:512], PS[:, 3, :], ACT.Copy).then_inc(y_ev, 1)
                    if not last:
                        gathered(E0 + 1)
                        for j in range(SPLIT - 2, SPLIT):
                            ehi(E0 + 1, j)

                for j in range(SPLIT):
                    ehi(g * NE, j)
                gathered(g * NE)
                with act.Fori(0, NE - 1) as e:
                    expert(e, False)
                expert(NE - 1, True)
                act.wait_ge(sc_ev, 4 + 4 * NE * (g + 1))

            experts(0)
            act.wait_ge(flag_ready, 1)
            with act.If(act.value_load(overi[0:1, 0:1], min_val=0, max_val=1) == 1):
                experts(1)
            norm_roots(4)

        @block.vector
        def _(dve):
            V_ = nc.vector
            TT, TS, STT = V_.tensor_tensor, V_.tensor_scalar, V_.scalar_tensor_tensor
            chain = Chain(dve, dve_chain)
            link = chain.link

            def lo(u, s):
                dve.wait_ge(hi_done, u + 1)
                TT(WL[:, s, :], raw[:, s, :], WH[:, s, :].bitcast(F32), ALU.subtract).then_inc(lo_done, 1)

            def norm_lo(q, shift, scale, hh, hl):
                c0 = norm_c0[q]
                streams = range(1 if q == 3 else 0, 2)
                dve.wait_ge(n_rt, q + 1)
                link(V_.reciprocal(rs[:, c0:TOK], rs[:, c0:TOK]))
                todo = [(k, s) for k in range(DK) for s in streams]
                first = items_before[q]

                def low(j):
                    k, s = todo[j]
                    it = first + j
                    dve.wait_ge(n_hi, it + 1 if q < 3 else first + 2 * (j + 1))
                    dst = slice(0, L) if q == 3 else slice(s * L, (s + 1) * L)
                    STT(hl[:, k, dst], sq[:, it % 2, 0:L], mod[:, shift * DK + k, s:s + 1],
                        hh[:, k, dst].bitcast(F32), ALU.add, ALU.subtract).then_inc(n_lo, 1)

                for j, (k, s) in enumerate(todo):
                    it = first + j
                    if j >= 2:
                        dve.wait_ge(n_lo, it - 1)
                    STT(sq[:, it % 2, 0:L], X[:, k, s * L:(s + 1) * L], scale[:, k, s:s + 1],
                        rs[:, s * L:(s + 1) * L], ALU.mult, ALU.mult).then_inc(n_t, 1)
                    if j:
                        low(j - 1)
                low(len(todo) - 1)

            V_.memset(ones[:], 1.0).then_inc(setup_done, 1)
            V_.memset(eps[:], EPS).then_inc(setup_done, 1)
            V_.memset(SH[:].bitcast(F32), 0.0).then_inc(setup_done, 1)
            V_.memset(SL[:].bitcast(F32), 0.0).then_inc(setup_done, 1)
            dve.sem_inc(md_out, 2)
            dve.sem_inc(evac, 2)
            dve.wait_ge(setup_done, 4)
            dve.wait_ge(s_ready, 1)
            TT(SL[:, :, 0:2], svec[:], SH[:, :, 0:2].bitcast(F32), ALU.subtract).then_inc(sl_ready, 1)
            dve.wait_ge(r_split, 1)
            TT(RTL[:], router[:], RTH[:].bitcast(F32), ALU.subtract).then_inc(r_split, 1)
            dve.wait_ge(x_in, 32)
            conv_items = conv_c = 0
            att_n = att_q = 0
            for l in range(2):
                b = base[l]
                c0 = 0 if l == 0 else L
                ns = 2 - l
                dve.wait_ge(filt_in, 16 * N_FILT * (l + 1))
                for j in range(2):
                    dve.wait_ge(f_pe, 5 * l + j + 1)
                    a = arg[:, j, :]
                    link(TS(a, PS[0:64, 7, 0:L], fb[:, 2 * j:2 * j + 1], fb[:, 2 * j + 1:2 * j + 2], ALU.add, ALU.mult))
                    link(TS(turns[:], a, 1.0 / (2 * math.pi), MAGIC, ALU.mult, ALU.add))
                    link(TS(turns[:], turns[:], MAGIC, None, ALU.subtract))
                    for c in TWO_PI_PARTS:
                        link(STT(a, turns[:], -c, a, ALU.mult, ALU.add))
                    TS(a, a, PI_CLIP, -PI_CLIP, ALU.min, ALU.max).then_inc(f_dv, 1)
                dve.wait_ge(f_pe, 5 * l + 3)
                for o in range(2):
                    if o:
                        dve.wait_ge(f_pe, 5 * l + 4)
                    for pc in range(2):
                        last = TT(taps[:, pc, :], PS[:, TAPB[2 * o + pc], :], decay[:, pc, o, :], ALU.mult)
                    last.then_inc(f_dv, 1)
                def mod_out(i, n):
                    dve.wait_ge(md_tr, MOD_U * l + 2 * i + n + 3)
                    m = bass.ds(4 * i + 2 * n, 2)
                    TT(mod[:, m, :], PS[:, 2 + n, 0:4].rearrange("p (m s) -> p m s", s=2),
                       bmod[:, l, m].unsqueeze(2).to_broadcast([P, 2, 2]), ALU.add).then_inc(md_out, 1)

                if l == 0:
                    dve.wait_ge(consts_in, 16 * N_SMALL)
                    for n in range(4):
                        lo(n, n % 2)
                        if n >= 2:
                            mod_out(0, n - 2)
                with dve.Fori(1 - l, MOD_U // 2) as i:
                    for n in range(2):
                        lo(b["mod"] + 2 * i + n + 2, n)
                        mod_out(i, n)
                dve.wait_ge(md_out, 2 + MOD_U * (l + 1))
                for s in range(2):
                    link(STT(na1[:, :, s], mod[:, SCALE1 * DK:(SCALE1 + 1) * DK, s], 1.0, g1[:, l, :], ALU.add, ALU.mult))
                    link(STT(na2[:, :, s], mod[:, SCALE2 * DK:(SCALE2 + 1) * DK, s], 1.0, g2[:, l, :], ALU.add, ALU.mult))
                norm_lo(2 * l, SHIFT1, na1, HH, HL)
                Ust = U[:, :, :].rearrange("p m (s t) -> p m s t", s=2)
                with dve.Fori(0, U_U // 2) as i:
                    chain.enter(i, 4, U_U // 2)
                    for n in range(2):
                        lo(b["u"] + 2 * i + n + 2, n)
                        for j in range(2):
                            m = 4 * i + 2 * n + j
                            dve.wait_ge(c_ac, 12 * l + 1 + m)
                            pv = PS[:, 2 * n + j, :].rearrange("p (s t) -> p s t", s=2)
                            row = U[:, bass.ds(m, 1), :].rearrange("p m (s t) -> p (m s) t", s=2)
                            sl = slice(l, 2)
                            link(STT(row[:, sl, 1:L], pv[:, sl, 0:L - 1], cw[:, l, 0, bass.ds(m, 1)],
                                     row[:, sl, 1:L], ALU.mult, ALU.add))
                            last = STT(row[:, sl, 0:L - 1], pv[:, sl, 1:L], cw[:, l, 2, bass.ds(m, 1)],
                                       row[:, sl, 0:L - 1], ALU.mult, ALU.add)
                        last.then_inc(evac, 1)
                    chain.exit()
                dve.wait_ge(evac, evb[l]["qkv"])
                for o in range(2):
                    for s in range(l, 2):
                        n = conv_items
                        dve.wait_ge(y_d, n + 1)
                        if n:
                            dve.wait_ge(y_i, n)
                        F = spec[:, o]
                        for j in range(2):
                            are, aim = PS[0:BINS, j, :], PS[0:BINS, 2 + j, :]
                            fre, fim, fren = F[:, j], F[:, 2 + j], (F[:, 4] if j == 0 else F[:, 1])
                            TT(Y[:, j, :], are, fre, ALU.mult)
                            TT(pt[:, 0, :], aim, fim, ALU.mult)
                            TT(Y[:, 2 + j, :], are, fim, ALU.mult)
                            link(TT(pt[:, 1, :], aim, fren, ALU.mult))
                            TT(Y[:, j, :], Y[:, j, :], pt[:, 0, :], ALU.subtract)
                            last = TT(Y[:, 2 + j, :], Y[:, 2 + j, :], pt[:, 1, :], ALU.add)
                            link(last) if j == 0 else last.then_inc(y_y, 1)
                        dve.wait_ge(y_i, n + 1)
                        if conv_c:
                            dve.wait_ge(y_lo, conv_c)
                        cols = slice(s * L, (s + 1) * L)
                        for c in range(4):
                            last = STT(zt[:, c, :], U[:, c, cols], hyb[:, l, o, c:c + 1], PS[:, 6 + c // 2, (c % 2) * L:(c % 2 + 1) * L],
                                       ALU.mult, ALU.add)
                        link(last)
                        dst = zt[:, :, :] if o else U[:, 0:4, cols]
                        TT(dst, zt[:, :, :], U[:, 4 + 4 * o:8 + 4 * o, cols], ALU.mult).then_inc(y_z, 1)
                        if o:
                            dve.wait_ge(y_hi, conv_c + 1)
                            TT(OHL[:, :, cols], zt[:, :, :], OHH[:, :, cols].bitcast(F32), ALU.subtract).then_inc(y_lo, 1)
                            conv_c += 1
                        conv_items += 1
                for n in range(QKV_U):
                    lo(b["qkv"] + n + 2, n % 2)
                    dve.wait_ge(unit_done, b["qkv"] + n + 1)
                    if n == 0:
                        dve.wait_ge(y_lo, conv_c)
                    if n < 4:
                        last = V_.tensor_copy(QK[:, 2 * n:2 * n + 2, :], PS[:, 2 * (n % 2):2 * (n % 2) + 2, :])
                    else:
                        src = PS[:, 2 * (n % 2):2 * (n % 2) + 2, :].rearrange("p a (b c) -> p (a b) c", b=2)
                        last = V_.tensor_copy(V[:, :, (n - 4) * BLK:(n - 3) * BLK], src)
                    last.then_inc(evac, 1)
                dve.wait_ge(bias_in, 16 * 17 * (l + 1))
                for h in range(HEADS):
                    dve.wait_ge(a_flip, HEADS * l + h + 1)
                    TT(bias[:, h, :], PS[:, 4 + h % 4, 0:6 * GRID], mask[:, :], ALU.add).then_inc(a_bias, 1)
                dve.wait_ge(a_bias, HEADS * (l + 1))
                for qc in range(2 * l, 4):
                    width = TOK if qc >= 2 else L
                    n0 = att_n
                    for h in range(HEADS):
                        n = att_n
                        dve.wait_ge(a_s, n + 1)
                        if n >= 2:
                            dve.wait_ge(a_t, n - 1)
                        last = TS(S[:, n % 2, 0:L], PS[:, n % 2, 0:L], SCALE, None, ALU.mult)
                        if qc >= 2:
                            bs = bias[:, h, (3 - qc) * P:(3 - qc) * P + L]
                            last = STT(S[:, n % 2, L:TOK], PS[:, n % 2, L:TOK], SCALE, bs, ALU.mult, ALU.add)
                        link(last)
                        V_.tensor_reduce(nmax[:, n % 32:n % 32 + 1], S[:, n % 2, 0:width], AX, ALU.max,
                                         negate=True).then_inc(a_sc, 1)
                        att_n += 1
                    dve.wait_ge(a_ex, att_n)
                    r0 = n0 % 32
                    link(V_.reciprocal(rsum[:, r0:r0 + HEADS], psums[:, r0:r0 + HEADS]))
                    dve.wait_ge(a_o, att_n)
                    src = PS[:, 4 + qc % 2, :].rearrange("p (h d) -> p h d", h=HEADS)
                    TT(OT[:, qc, :].rearrange("p (h d) -> p h d", h=HEADS), src,
                       rsum[:, r0:r0 + HEADS].unsqueeze(2).to_broadcast([P, HEADS, HD]), ALU.mult).then_inc(a_on, 1)
                    dve.wait_ge(a_hi, att_q + 1)
                    TT(OAL[:, :, qc * P:(qc + 1) * P], PS[:, 6 + qc % 2, :].rearrange("p (c q) -> p c q", c=4),
                       OAH[:, :, qc * P:(qc + 1) * P].bitcast(F32), ALU.subtract).then_inc(a_lo, 1)
                    att_q += 1
                if l == 0:
                    for s_ in (m_sum, m_lo):
                        dve.nop().then_inc(s_, 1)
                with dve.Fori(0, 2) as i:
                    chain.enter(i, 2, 2)
                    for n in range(6):
                        pair, kind = n // 3, n % 3
                        lo(b["merge"] + 6 * i + n + 2, n % 2)
                        if kind == 2:
                            q = 4 * l + 2 * i + pair
                            dve.wait_ge(unit_done, b["merge"] + 6 * i + n + 1)
                            dve.wait_ge(m_sig, 2 * q + 3)
                            TT(sga[:, :, c0:TOK], sga[:, :, c0:TOK], PS[:, 4:6, c0:TOK], ALU.mult)
                            link(TT(sgb[:, :, c0:TOK], sgb[:, :, c0:TOK], PS[:, 6:8, c0:TOK], ALU.mult))
                            TT(sga[:, :, c0:TOK], sga[:, :, c0:TOK], sgb[:, :, c0:TOK], ALU.add).then_inc(m_sum, 1)
                            dve.wait_ge(m_hi, q + 1)
                            mm = bass.ds(2 * (2 * i + pair), 2)
                            TT(ML[:, mm, c0:TOK], sga[:, :, c0:TOK], MH[:, mm, c0:TOK].bitcast(F32), ALU.subtract).then_inc(m_lo, 1)
                    chain.exit()
                for n in range(WO_U):
                    if l == 0 or n < 2:
                        lo(b["wo"] + n + 2, n % 2)
                    dve.wait_ge(unit_done, b["wo"] + n + 1)
                    for j in range(2):
                        for s in range(l, 2):
                            m = 2 * n + j
                            cols = slice(s * L, (s + 1) * L)
                            last = STT(X[:, m, cols], PS[:, 2 * (n % 2) + j, cols], mod[:, GATE1 * DK + m, s:s + 1],
                                       X[:, m, cols], ALU.mult, ALU.add)
                    last.then_inc(evac, 1)
                if l == 0:
                    norm_lo(1, SHIFT2, na2, HH, HL)
                    for s_ in (up_mid, up_lo):
                        dve.nop().then_inc(s_, 1)
                    with dve.Fori(0, NB) as i:
                        lo(b["up"] + 2 * i + 2, 0)
                        lo(b["up"] + 2 * i + 3, 1)
                        dve.wait_ge(up_silu, i + 2)
                        dve.wait_ge(unit_done, b["up"] + 2 * i + 2)
                        TT(sq[:, :, :], sq[:, :, :], PS[:, 2:4, :], ALU.mult).then_inc(up_mid, 1)
                        dve.wait_ge(up_hi, i + 1)
                        TT(MDL[:, bass.ds(2 * i, 2), :], sq[:, :, :], MDH[:, bass.ds(2 * i, 2), :].bitcast(F32),
                           ALU.subtract).then_inc(up_lo, 1)
                    with dve.Fori(0, DK // 2) as i:
                        for mm in range(2):
                            for s in range(2):
                                lo(b["down"] + 4 * i + 2 * mm + s + 2, s)
                            dve.wait_ge(unit_done, b["down"] + 4 * i + 2 * mm + 2)
                            for s in range(2):
                                cols = slice(s * L, (s + 1) * L)
                                xm = X[:, bass.ds(2 * i + mm, 1), cols].rearrange("p m t -> p (m t)")
                                last = STT(xm, PS[:, mm, cols], mod[:, bass.ds(GATE2 * DK + 2 * i + mm, 1), s],
                                           xm, ALU.mult, ALU.add)
                            last.then_inc(evac, 1)
                else:
                    norm_lo(3, SHIFT2, na2, RH, RL)
            for c in range(2):
                dve.wait_ge(r_pe, c + 1)
                link(V_.tensor_copy(logits[:, c, :], PS[:, c, 0:NE]))
                link(V_.max(tv[:, c, :], logits[:, c, :]))
                link(V_.max_index(ti[:, c, :], tv[:, c, :], logits[:, c, :]))
                V_.tensor_copy(tif[:, c, :], ti[:, c, :])
                TT(gt[:, c, 0:1], tv[:, c, 1:2], tv[:, c, 0:1], ALU.subtract).then_inc(r_mask, 1)
            dve.wait_ge(bias_in, 16 * 36)
            for c in range(2):
                dve.wait_ge(r_ev, c + 1)
                link(TS(gt[:, c, 2:3], gt[:, c, 1:2], 1.0, None, ALU.add))
                link(V_.reciprocal(gt[:, c, 2:3], gt[:, c, 2:3]))
                link(TT(gt[:, c, 3:4], gt[:, c, 1:2], gt[:, c, 2:3], ALU.mult))
                for j in range(2):
                    link(TS(oh[:, c, j, :], iot[:, 0:NE], tif[:, c, j:j + 1], None, ALU.is_equal))
                    link(TS(oh[:, c, 2 + j, :], oh[:, c, j, :], gt[:, c, 2 + j:3 + j], None, ALU.mult))
                link(TT(wex[:, c, :], oh[:, c, 2, :], oh[:, c, 3, :], ALU.add))
                TT(msk[:, c, :], oh[:, c, 0, :], oh[:, c, 1, :], ALU.add).then_inc(r_mask, 1)
            dve.wait_ge(r_mask, 4)
            dve.wait_ge(r_rank, 1)
            for c in range(2):
                link(TS(rank[:, c, :], msk[:, c, :], -1000.0, 1000.0, ALU.mult, ALU.add))
                link(TT(rank[:, c, :], rank[:, c, :], PS[:, 4 + c, 0:NE], ALU.add))
            V_.tensor_reduce(over[:, 0:1], PS[:, 6, 0:NE], AX, ALU.max).then_inc(r_cnt, 1)
            dve.wait_ge(r_cnt, 1)
            TS(overi[:, 0:1], over[:, 0:1], P + 0.5, None, ALU.is_gt).then_inc(flag_ready, 1)
            dve.wait_ge(flag_ready, 1)
            dve.sem_inc(e_lo, NU)
            dve.sem_inc(e_mid, 1)
            dve.sem_inc(sc_ev, 4)

            def experts(g):
                if g:
                    dve.wait_ge(sc_pe, 4 + 4 * NE)
                    dve.wait_ge(g_pe, 2 * NE)
                for e in range(NE):
                    for c in range(2):
                        TS(sel[:, c, e, :], iot[:, g * P:(g + 1) * P], rank[:, c, e:e + 1], None, ALU.is_equal)
                        last = TS(selw[:, c, e, :], iot[:, g * P:(g + 1) * P], rank[:, c, e:e + 1],
                                  wex[:, c, e:e + 1], ALU.is_equal, ALU.mult)
                    last.then_inc(p_sel, 1)

                def gathered(E0):
                    for q in range(2):
                        dve.wait_ge(g_hi, 2 * E0 + q + 1)
                        TT(GL[:, 4 * q:4 * q + 4, :], PS[:, 5 + q, :].rearrange("p (k j) -> p k j", k=4),
                           GH[:, 4 * q:4 * q + 4, :].bitcast(F32), ALU.subtract).then_inc(g_lo, 1)

                def elo(E0, j):
                    dve.wait_ge(e_hi, NU * E0 + j + 1)
                    TT(EL[:, j % SPLIT, :], eraw[:, j % RAW, :], EH[:, j % SPLIT, :].bitcast(F32),
                       ALU.subtract).then_inc(e_lo, 1)

                def turned(E0, b):
                    dve.wait_ge(e_th, NB * E0 + b + 1)
                    TT(TL[:], PS[:, 2, 0:2 * P].rearrange("p (k j) -> p k j", k=2), TH[:].bitcast(F32),
                       ALU.subtract).then_inc(e_tl, 1)

                def expert(e, last):
                    E0 = g * NE + e
                    for j, (kind, b) in enumerate(ORDER):
                        if kind == 0 and b:
                            turned(E0, b - 1)
                        if kind == 1:
                            dve.wait_ge(e_silu, NB * E0 + b + 1)
                            dve.wait_ge(e_use, NU + NU * E0 + j + 1)
                            TT(mid[:], sil[:], PS[:, 1, 0:BLK], ALU.mult).then_inc(e_mid, 1)
                        if j + SPLIT < NU:
                            elo(E0, j + SPLIT)
                        if j == NU - 2:
                            turned(E0, NB - 1)
                    if not last:
                        for j in range(SPLIT - 2):
                            elo(E0 + 1, j)
                    dve.wait_ge(e_use, NU + NU * E0 + NU)
                    dve.wait_ge(sc_pe, 4 * E0 + 4)
                    V_.tensor_copy(yexp[:, 512:D], PS[:, 4, :]).then_inc(y_ev, 1)
                    if not last:
                        gathered(E0 + 1)
                    for r in range(4):
                        dve.wait_ge(sc_pe, 4 * E0 + r + 5)
                        for j in range(2):
                            f = 2 * r + j
                            ins = STT(X[:, f, L:TOK], PS[:, SCB[r], j * L:(j + 1) * L], mod[:, GATE2 * DK + f, 1:2],
                                      X[:, f, L:TOK], ALU.mult, ALU.add)
                        ins.then_inc(sc_ev, 1)
                    if not last:
                        for j in range(SPLIT - 2, SPLIT):
                            elo(E0 + 1, j)

                for j in range(SPLIT):
                    elo(g * NE, j)
                gathered(g * NE)
                with dve.Fori(0, NE - 1) as e:
                    expert(e, False)
                expert(NE - 1, True)

            experts(0)
            with dve.If(dve.value_load(overi[0:1, 0:1], min_val=0, max_val=1) == 1):
                experts(1)
            dve.wait_ge(n_rt, 5)
            link(V_.reciprocal(rs[:, L:TOK], rs[:, L:TOK]))
            for k in range(DK):
                STT(X[:, k, L:TOK], X[:, k, L:TOK], gf[:, k:k + 1], rs[:, L:TOK], ALU.mult, ALU.mult).then_inc(o_ready, 1)

        @block.tensor
        def _(pe):
            MM, TR = nc.tensor.matmul, nc.tensor.transpose

            def mm3(o, wh, wl, xh, xl, first, last):
                MM(o, wh, xh, start=first, stop=False)
                MM(o, wh, xl, start=False, stop=False)
                return MM(o, wl, xh, start=False, stop=last)

            def ready(u):
                pe.wait_ge(lo_done, u + 1)

            def cols(s, k, j):
                a = k * BLK + j * P
                return slice(a, a + P)

            def features(s, banks, c0, xh, xl, ks=range(DK), wk=None):
                for j in range(2):
                    for n, k in enumerate(ks):
                        w = n if wk is None else wk + n
                        last = mm3(PS[:, banks + j, c0:TOK], WH[:, s, cols(s, w, j)], WL[:, s, cols(s, w, j)],
                                   xh[:, k, c0:TOK], xl[:, k, c0:TOK], n == 0, n == len(ks) - 1)
                return last

            def norm_sums(q):
                c0 = norm_c0[q]
                for k in range(DK):
                    pe.wait_ge(n_sq, 8 * q + k + 1)
                    MM(PS[:, 7, c0:TOK], ones[:], sq[:, k % 2, c0:TOK], start=k == 0, stop=k == DK - 1).then_inc(n_pe, 1)

            pe.wait_ge(setup_done, 4)
            conv_items = 0
            att_n = att_q = 0
            for l in range(2):
                b = base[l]
                c0 = 0 if l == 0 else L
                pe.wait_ge(filt_in, 16 * N_FILT * (l + 1))
                MM(PS[0:64, 7, 0:L], fw1[:], posT[:], start=True, stop=True).then_inc(f_pe, 1)
                pe.wait_ge(f_ac, 4 * l + 1)
                MM(PS[0:64, 7, 0:L], fw2[:], act1[:, 0, :], start=True, stop=True).then_inc(f_pe, 1)
                pe.wait_ge(f_ac, 4 * l + 2)
                for o in range(2):
                    for pc in range(2):
                        last = MM(PS[:, TAPB[2 * o + pc], :], act1[:, 1, pc * P:(pc + 1) * P], fw3[:, o, :], start=True, stop=True)
                last.then_inc(f_pe, 1)
                for o in range(2):
                    pe.wait_ge(f_dv, 4 * l + 3 + o)
                    if o:
                        pe.wait_ge(f_ac, 4 * l + 3)
                    for g in range(5):
                        for c in range(2):
                            last = MM(PS[0:BINS, g, :], dftk[:, c, g * BINS:(g + 1) * BINS], taps[:, c, :], start=c == 0, stop=c == 1)
                    last.then_inc(f_pe, 1)
                pe.wait_ge(sl_ready, 1)
                pe.wait_ge(f_ac, 4 * l + 4)

                def mod_unit(u, n):
                    ready(b["mod"] + u)
                    for k in range(DK):
                        w = slice(k * BLK, (k + 1) * BLK)
                        MM(PS[:, n, 0:BLK], SH[:, k, :], WH[:, n, w], start=k == 0, stop=False)
                        MM(PS[:, n, 0:BLK], SL[:, k, :], WH[:, n, w], start=False, stop=False)
                        last = MM(PS[:, n, 0:BLK], SH[:, k, :], WL[:, n, w], start=False, stop=k == DK - 1)
                    last.then_inc(unit_done, 1)

                def mod_turn(u, n):
                    pe.wait_ge(md_row, MOD_U * l + u + 1)
                    pe.wait_ge(md_out, MOD_U * l + u + 1)
                    for j in range(2):
                        last = MM(PS[:, 2 + n, 2 * j:2 * j + 2], mrow[:, n, j * P:(j + 1) * P], ident[0:2, 0:2],
                                  start=True, stop=True)
                    last.then_inc(md_tr, 1)

                if l == 0:
                    pe.sem_inc(md_tr, 2)
                mod_unit(0, 0)
                with pe.Fori(0, MOD_U // 2 - 1) as i:
                    mod_unit(2 * i + 1, 1)
                    mod_turn(2 * i, 0)
                    mod_unit(2 * i + 2, 0)
                    mod_turn(2 * i + 1, 1)
                mod_unit(MOD_U - 1, 1)
                for n in range(2):
                    mod_turn(MOD_U - 2 + n, n)
                norm_sums(2 * l)
                pe.wait_ge(n_lo, items_before[2 * l] + 16)
                with pe.Fori(0, U_U // 2) as i:
                    for n in range(2):
                        ready(b["u"] + 2 * i + n)
                        pe.wait_ge(evac, evb[l]["u"] + 2 * i + n - 1)
                        features(n, 2 * n, c0, HH, HL).then_inc(unit_done, 1)
                pe.wait_ge(evac, evb[l]["qkv"])
                for o in range(2):
                    for s in range(l, 2):
                        n = conv_items
                        if o:
                            pe.wait_ge(y_z, n - (2 - l) + 1)
                        if n:
                            pe.wait_ge(y_vt, n)
                        for c in range(2):
                            for ch in range(4):
                                last = TR(PS[:, 4 + c, ch * P:(ch + 1) * P], U[:, ch, s * L + c * P:s * L + (c + 1) * P], ident[:])
                        last.then_inc(y_t, 1)
                        pe.wait_ge(y_vt, n + 1)
                        if n:
                            pe.wait_ge(y_y, n)
                        for g in range(4):
                            for c in range(2):
                                last = MM(PS[0:BINS, g, :], dftf[:, c, g * BINS:(g + 1) * BINS], VT[:, c, :], start=c == 0, stop=c == 1)
                        last.then_inc(y_d, 1)
                        pe.wait_ge(y_y, n + 1)
                        if n:
                            pe.wait_ge(y_z, n)
                        for ch in range(4):
                            for g in range(4):
                                last = MM(PS[:, 6 + ch // 2, (ch % 2) * L:(ch % 2 + 1) * L], Y[:, g, ch * P:(ch + 1) * P], dfti[:, g, :],
                                          start=g == 0, stop=g == 3)
                        last.then_inc(y_i, 1)
                        conv_items += 1
                for n in range(QKV_U):
                    ready(b["qkv"] + n)
                    pe.wait_ge(evac, evb[l]["qkv"] + n - 1)
                    if n == 0:
                        pe.wait_ge(y_z, conv_items)
                    if n < 4:
                        last = features(n % 2, 2 * (n % 2), 0, HH, HL)
                    else:
                        for tc in range(4):
                            o = PS[:, 2 * (n % 2) + tc // 2, (tc % 2) * BLK:(tc % 2 + 1) * BLK]
                            for k in range(DK):
                                w = slice(k * BLK, (k + 1) * BLK)
                                x_ = slice(tc * P, (tc + 1) * P)
                                MM(o, HH[:, k, x_], WH[:, n % 2, w], start=k == 0, stop=False)
                                MM(o, HL[:, k, x_], WH[:, n % 2, w], start=False, stop=False)
                                last = MM(o, HH[:, k, x_], WL[:, n % 2, w], start=False, stop=k == DK - 1)
                    last.then_inc(unit_done, 1)
                pe.wait_ge(bias_in, 16 * 17 * (l + 1))
                for h in range(HEADS):
                    if h >= 4:
                        pe.wait_ge(a_bias, HEADS * l + h - 3)
                    MM(PS[:, 4 + h % 4, 0:6 * GRID], flip[:], bias[:, h, :], start=True, stop=True).then_inc(a_flip, 1)
                pe.wait_ge(evac, evb[l]["merge"])
                pe.wait_ge(a_bias, HEADS * (l + 1))

                def scores(n, qc, h):
                    r = slice(HD * (h % 2), HD * (h % 2) + HD)
                    width = TOK if qc >= 2 else L
                    if n >= 2:
                        pe.wait_ge(a_sc, n - 1)
                    MM(PS[:, n % 2, 0:width], QK[r, h // 2, qc * P:(qc + 1) * P], QK[r, 4 + h // 2, 0:width],
                       start=True, stop=True).then_inc(a_s, 1)

                def turn(n, qc):
                    pe.wait_ge(a_ex, n + 1)
                    if n >= 2:
                        pe.wait_ge(a_pt, n - 1)
                    for kc in range(4 if qc >= 2 else 2):
                        last = TR(PS[:, 2 + n % 2, kc * P:(kc + 1) * P], S[:, n % 2, kc * P:(kc + 1) * P], ident[:])
                    last.then_inc(a_t, 1)

                def attend(n, qc, h):
                    pe.wait_ge(a_pt, n + 1)
                    nk = 4 if qc >= 2 else 2
                    for kc in range(nk):
                        last = MM(PS[:, 4 + qc % 2, h * HD:(h + 1) * HD], PT[:, n % 2, kc * P:(kc + 1) * P],
                                  V[:, kc, h * HD:(h + 1) * HD], start=kc == 0, stop=kc == nk - 1)
                    last.then_inc(a_o, 1)

                for qc in range(2 * l, 4):
                    n0 = att_n
                    for h in range(HEADS + 2):
                        if h < HEADS:
                            scores(n0 + h, qc, h)
                        if 1 <= h <= HEADS:
                            turn(n0 + h - 1, qc)
                        if h >= 2:
                            attend(n0 + h - 2, qc, h - 2)
                    att_n += HEADS
                    pe.wait_ge(a_on, att_q + 1)
                    for c in range(4):
                        last = TR(PS[:, 6 + qc % 2, c * P:(c + 1) * P], OT[:, qc, c * P:(c + 1) * P], ident[:])
                    last.then_inc(a_ot, 1)
                    att_q += 1
                pe.wait_ge(a_lo, att_q)
                with pe.Fori(0, 2) as i:
                    for n in range(6):
                        pair, kind = n // 3, n % 3
                        ready(b["merge"] + 6 * i + n)
                        if kind == 0:
                            pe.wait_ge(m_sig, 2 * (4 * l + 2 * i + pair) + 1)
                        if kind == 2:
                            pe.wait_ge(m_sum, 4 * l + 2 * i + pair + 1)
                        if kind < 2:
                            last = features(n % 2, 2 * kind, c0, HH, HL)
                        else:
                            features(n % 2, 4, c0, OAH, OAL, range(4), 0)
                            last = features(n % 2, 6, c0, OHH, OHL, range(4), 4)
                        last.then_inc(unit_done, 1)
                pe.wait_ge(m_lo, 4 * l + 5)
                for n in range(WO_U):
                    ready(b["wo"] + n)
                    pe.wait_ge(evac, evb[l]["wo"] + n - 1)
                    features(n % 2, 2 * (n % 2), c0, MH, ML).then_inc(unit_done, 1)
                norm_sums(2 * l + 1)
                if l == 0:
                    pe.wait_ge(n_lo, items_before[1] + 16)
                    with pe.Fori(0, NB) as i:
                        ready(b["up"] + 2 * i)
                        pe.wait_ge(up_silu, i + 1)
                        features(0, 0, 0, HH, HL).then_inc(unit_done, 1)
                        ready(b["up"] + 2 * i + 1)
                        pe.wait_ge(up_mid, i + 1)
                        features(1, 2, 0, HH, HL).then_inc(unit_done, 1)
                    pe.wait_ge(up_lo, NB + 1)
                    with pe.Fori(0, DK // 2) as i:
                        for mm in range(2):
                            pe.wait_ge(evac, evb[l]["down"] + 2 * i + mm - 1)
                            for s in range(2):
                                ready(b["down"] + 4 * i + 2 * mm + s)
                                for n in range(11):
                                    w = slice(n * P, (n + 1) * P)
                                    k = 11 * s + n
                                    last = mm3(PS[:, mm, :], WH[:, s, w], WL[:, s, w], MDH[:, k, :], MDL[:, k, :],
                                               k == 0, k == FK - 1)
                                last.then_inc(unit_done, 1)
            pe.wait_ge(n_lo, 56)
            pe.wait_ge(r_split, 2)
            for c in range(2):
                x_ = slice(c * P, (c + 1) * P)
                for k in range(DK):
                    MM(PS[:, c, 0:NE], RH[:, k, x_], RTH[:, k, :], start=k == 0, stop=False)
                    MM(PS[:, c, 0:NE], RL[:, k, x_], RTH[:, k, :], start=False, stop=False)
                    last = MM(PS[:, c, 0:NE], RH[:, k, x_], RTL[:, k, :], start=False, stop=k == DK - 1)
                last.then_inc(r_pe, 1)
            pe.wait_ge(r_mask, 4)
            MM(PS[:, 4, 0:NE], tri[:], msk[:, 0, :], start=True, stop=True)
            MM(PS[:, 5, 0:NE], tri[:], msk[:, 1, :], start=True, stop=False)
            MM(PS[:, 5, 0:NE], ones[:], msk[:, 0, :], start=False, stop=True)
            MM(PS[:, 6, 0:NE], ones[:], msk[:, 0, :], start=True, stop=False)
            MM(PS[:, 6, 0:NE], ones[:], msk[:, 1, :], start=False, stop=True).then_inc(r_rank, 1)
            for c in range(2):
                for hf in range(2):
                    for k in range(4):
                        last = TR(PS[:, 2 * c + hf, k * P:(k + 1) * P], mo_h[:, 4 * hf + k, c * P:(c + 1) * P], ident[:])
                    last.then_inc(h_tr, 1)
            pe.wait_ge(h_ev, 4)

            def experts(g):
                if g:
                    pe.wait_ge(sc_ev, 4 + 4 * NE)
                for q in range(4):
                    pe.wait_ge(p_sel, NE * g + 2 * q + 2)
                    for j in range(2):
                        for c in range(2):
                            last = TR(PS[:, q, j * L + c * P:j * L + (c + 1) * P], selw[:, c, 2 * q + j, :], ident[:])
                    last.then_inc(p_tr, 1)
                pe.wait_ge(p_selT, 4 * g + 4)
                if g == 0:
                    pe.sem_inc(e_use, NU)
                    pe.sem_inc(sc_pe, 4)

                def gather(e):
                    for q in range(2):
                        for k in range(4):
                            for c in range(2):
                                ins = MM(PS[:, 5 + q, k * P:(k + 1) * P], mo_ht[:, c, (4 * q + k) * P:(4 * q + k + 1) * P],
                                         of_expert(sel[:, c], e), start=c == 0, stop=c == 1)
                        ins.then_inc(g_pe, 1)

                def of_expert(ap, e):
                    return ap[:, e, :] if isinstance(e, int) else ap[:, bass.ds(e, 1), :].rearrange("p e j -> p (e j)")

                def up(E0, kind, b):
                    j = POS[(kind, b)]
                    pe.wait_ge(e_lo, NU + NU * E0 + j + 1)
                    for k in range(DK):
                        w = slice(k * BLK, (k + 1) * BLK)
                        o = PS[:, kind, 0:BLK]
                        MM(o, GH[:, k, :], EH[:, j % SPLIT, w], start=k == 0, stop=False)
                        MM(o, GH[:, k, :], EL[:, j % SPLIT, w], start=False, stop=False)
                        ins = MM(o, GL[:, k, :], EH[:, j % SPLIT, w], start=False, stop=k == DK - 1)
                    ins.then_inc(e_use, 1)

                def turn_mid(E0, b):
                    pe.wait_ge(e_mid, NB * E0 + b + 2)
                    for k in range(2):
                        ins = TR(PS[:, 2, k * P:(k + 1) * P], mid[:, k * P:(k + 1) * P], ident[:])
                    ins.then_inc(e_tr, 1)

                def down(E0, b):
                    j = POS[(2, b)]
                    pe.wait_ge(e_tl, NB * E0 + b + 1)
                    pe.wait_ge(e_lo, NU + NU * E0 + j + 1)
                    for hf in range(2):
                        for k in range(2):
                            w = slice(k * D + hf * 512, k * D + (hf + 1) * 512)
                            o = PS[:, 3 + hf, :]
                            MM(o, TH[:, k, :], EH[:, j % SPLIT, w], start=b == 0 and k == 0, stop=False)
                            MM(o, TH[:, k, :], EL[:, j % SPLIT, w], start=False, stop=False)
                            ins = MM(o, TL[:, k, :], EH[:, j % SPLIT, w], start=False, stop=b == NB - 1 and k == 1)
                    ins.then_inc(e_use, 1)

                def expert(e, last):
                    E0 = g * NE + e
                    pe.wait_ge(g_lo, 2 * E0 + 2)
                    for b in range(NB):
                        if b:
                            pe.wait_ge(e_silu, NB * E0 + b)
                        else:
                            pe.wait_ge(sc_ev, 4 * E0 + 2)
                        up(E0, 0, b)
                        if b == 0:
                            pe.wait_ge(sc_ev, 4 * E0 + 4)
                        else:
                            turn_mid(E0, b - 1)
                            pe.wait_ge(e_mid, NB * E0 + b + 1)
                        up(E0, 1, b)
                        if b:
                            down(E0, b - 1)
                    turn_mid(E0, NB - 1)
                    down(E0, NB - 1)
                    if not last:
                        gather(e + 1)
                    pe.wait_ge(y_ev, 2 * E0 + 2)
                    for r in range(4):
                        for j in range(2):
                            f = 2 * r + j
                            ins = MM(PS[:, SCB[r], j * L:(j + 1) * L], yexp[:, f * P:(f + 1) * P],
                                     of_expert(selT, e), start=True, stop=True)
                        ins.then_inc(sc_pe, 1)

                pe.wait_ge(sc_ev, 4)
                gather(0)
                with pe.Fori(0, NE - 1) as e:
                    expert(e, False)
                expert(NE - 1, True)

            experts(0)
            pe.wait_ge(flag_ready, 1)
            with pe.If(pe.value_load(overi[0:1, 0:1], min_val=0, max_val=1) == 1):
                experts(1)
            norm_sums(4)


class Chain:

    def __init__(self, eng, sem):
        self.eng, self.sem, self.n, self.i, self.per = eng, sem, 0, None, 0

    def enter(self, i, per, trips):
        self.i, self.per, self.trips, self.start = i, per, trips, self.n

    def exit(self):
        assert self.n - self.start == self.per, (self.n - self.start, self.per)
        self.i, self.n = None, self.start + self.per * self.trips

    def link(self, ins):
        ins.then_inc(self.sem, 1)
        self.n += 1
        self.eng.wait_ge(self.sem, self.n if self.i is None else self.n + self.per * self.i)


def tables():
    pos = np.arange(L, dtype=np.float32)
    bands = np.linspace(1e-4, 15.0, 16, dtype=np.float32)
    ang = (np.float32(2.0 * math.pi / L) * pos[:, None] * bands[None, :]).astype(np.float32)
    feats = np.concatenate([(pos / (L - 1))[:, None], np.cos(ang), -np.sin(ang)], axis=-1)
    dist = np.abs(pos - L // 2) * np.float32(2.0 / L)
    rates = np.abs(np.linspace(math.log(1e-2) / 1.5, math.log(1e-2) / 0.3, 2 * HY_W, dtype=np.float32))
    decay = np.exp(-dist[:, None] * rates[None, :]) + 0.05
    j = np.arange(L)[:, None].astype(np.float64)
    k = np.arange(2 * BINS)[None, :]
    w = 2 * np.pi / NFFT
    re, im = np.cos(w * j * k), -np.sin(w * j * k)
    nyq = np.cos(np.pi * j[:, 0])
    imn = im.copy()
    imn[:, 0] = nyq
    ren = re[:, :BINS].copy()
    ren[:, 0] = nyq
    fwd = np.concatenate([re, imn], axis=1)
    fil = np.concatenate([re, im * (k > 0), ren], axis=1)
    n = (np.arange(L) + L // 2)[None, :]
    kk = np.arange(2 * BINS)[:, None]
    ire = np.where(kk == 0, 1.0, 2 * np.cos(w * kk * n)) / NFFT
    iim = np.where(kk == 0, np.cos(np.pi * n), -2 * np.sin(w * kk * n)) / NFFT
    inv = np.concatenate([ire, iim], axis=0).reshape(4, BINS, L)
    c = np.arange(P) % GRID
    start = np.clip(c - WIN // 2, 0, GRID - WIN)[:, None]
    col = np.arange(GRID)[None, :]
    mask = np.where((col >= start) & (col < start + WIN), 0.0, NEG)
    f = np.float32
    chunks = lambda a: np.ascontiguousarray(a.reshape(2, P, -1).transpose(1, 0, 2)).astype(f)
    return {
        "posT": np.ascontiguousarray(feats.T).astype(f),
        "decay": np.ascontiguousarray(decay.reshape(2, P, 2, HY_W).transpose(1, 0, 2, 3)).astype(f),
        "dftf": chunks(fwd), "dftk": chunks(fil),
        "dfti": np.ascontiguousarray(inv.transpose(1, 0, 2)).astype(f),
        "mask": np.tile(mask, (1, 6)).astype(f),
        "ident": np.eye(P, dtype=f),
        "flip": np.kron(np.eye(2), np.eye(GRID)[::-1]).astype(f),
        "tri": np.triu(np.ones((P, P), f), 1),
        "iota": np.tile(np.arange(L, dtype=f), (P, 1)),
    }


def kernel(**inputs):
    import concourse.bacc as bacc
    from concourse.bass_utils import run_bass_kernel_spmd as run

    a = {k: np.asarray(v) for k, v in inputs.items()}

    def features_first(v, lead):
        v = v.reshape(*v.shape[:-1], v.shape[-1] // P, P)
        return np.moveaxis(v, -1, 0)

    arrays = {
        "xT": a["x"][0].T, "ctxT": a["ctx"][0].T,
        "cc": np.moveaxis(features_first(np.stack([a["c_ctx"], a["c"][0]]), 1), 1, 2),
        "w_mod": a["w_mod"], "b_mod": features_first(a["b_mod"], 1),
        "norm1_g": features_first(a["norm1_g"], 1), "norm2_g": features_first(a["norm2_g"], 1),
        "final_g": features_first(a["final_g"], 0),
        "w_in": a["w_in"], "rpb": a["rpb"],
        "hy_conv_w": features_first(a["hy_conv_w"], 2), "hy_conv_b": features_first(a["hy_conv_b"], 1),
        "hy_w1": a["hy_w1"], "hy_w2": a["hy_w2"], "hy_w3": a["hy_w3"],
        "fvec": np.stack([a["hy_b1"], a["hy_freq"][:, 0], a["hy_b2"], a["hy_freq"][:, 1]], axis=-1),
        "hy_bias": features_first(a["hy_bias"], 2),
        "w_opab": np.concatenate([a["w_o"], np.concatenate([a["w_pa"], a["w_pb"]], axis=1)], axis=2),
        "ffn_w1": a["ffn_w1"][0], "ffn_w3": a["ffn_w3"][0], "ffn_w2": a["ffn_w2"][0],
        "moe_router": np.moveaxis(a["moe_router"][0].reshape(DK, P, NE), 1, 0),
        "moe_w1": a["moe_w1"][0].reshape(NE * D, FF), "moe_w3": a["moe_w3"][0].reshape(NE * D, FF),
        "moe_w2": a["moe_w2"][0].reshape(NE * FF, D),
        **tables(),
    }
    arrays = {k: np.ascontiguousarray(v) for k, v in arrays.items()}
    nc = bacc.Bacc("TRN2", target_bir_lowering=False, num_devices=1)
    t = {k: nc.dram_tensor("in_" + k, v.shape, mybir.dt.from_np(v.dtype), kind="ExternalInput").ap() for k, v in arrays.items()}
    out = nc.dram_tensor("out_features", (D, L), F32, kind="ExternalOutput").ap()
    build(nc, t, out)
    r = run(nc, [{"in_" + k: v for k, v in arrays.items()}], core_ids=[0])
    return np.ascontiguousarray(r.results[0]["out_features"].T)[None]
```

```python
import math
from contextlib import ExitStack

import numpy as np
import concourse.bass as bass
from concourse import mybir

F32 = mybir.dt.float32
R32 = mybir.dt.float32r
U32 = mybir.dt.uint32
ALU = mybir.AluOpType
ACT = mybir.ActivationFunctionType
AX = mybir.AxisListType.X

P = 128
D = 1024
DK = D // P
L = 256
TOK = 2 * L
PROJ = 5120
ATT_W, HY_W = 512, 512
OFF_U, OFF_GA, OFF_GB = 1536, 3072, 4096
HEADS, HD = 8, 64
GRID, WIN = 64, 16
RPB_R, RPB_C = 15, 31
FF = 2816
FK = FF // P
NE = 8
BLK = 256
NB = FF // BLK
NFFT = 384
BINS = 96
EPS = 1e-6
SCALE = HD ** -0.5
NEG = -1e30
MAGIC = 1.5 * 2.0 ** 23
TWO_PI_PARTS = (6.28125, 0.0019350051879882812, 3.0199157663446036e-07)
PI_CLIP = 3.1415925
TAPB = (0, 4)
SCB = (7, 0, 1, 2)
N_SMALL, N_FILT = 11, 9

MOD_U, U_U, QKV_U, MERGE_U, WO_U, UP_U, DOWN_U = 24, 6, 6, 12, 4, 22, 16
MRING = 3
MCH = 48
MTRIPS = MOD_U // MRING
MODB, MTB = 4, 5
SHIFT1, SCALE1, GATE1, SHIFT2, SCALE2, GATE2 = range(6)


RAW, SPLIT = 6, 4
ORDER = [(0, 0), (1, 0)] + [u for b in range(1, NB) for u in ((0, b), (1, b), (2, b - 1))] + [(2, NB - 1)]
NU = len(ORDER)
POS = {u: j for j, u in enumerate(ORDER)}


def slot_before(j, slots):
    return j - slots if j >= slots else max(q for q in range(NU) if q % slots == j % slots) - NU


def unit_bases():
    base, n = [{}, {}], 0
    for l in range(2):
        stages = [("u", U_U), ("qkv", QKV_U), ("merge", MERGE_U), ("wo", WO_U)]
        if l == 0:
            stages += [("up", UP_U), ("down", DOWN_U)]
        for name, count in stages:
            base[l][name] = n
            n += count
    return base, n


def build(nc, t, out):
    base, n_units = unit_bases()
    top = ExitStack()
    with top:
        def sem(name):
            return top.enter_context(nc.semaphore(name))

        def sb(stack, name, shape, dt=F32):
            return stack.enter_context(nc.sbuf_tensor(name, shape, dt))

        X = sb(top, "x_residual", [P, DK, TOK])
        ident = sb(top, "ident", [P, P])
        flip = sb(top, "flip", [P, P])
        ones = sb(top, "ones", [P, P])
        eps = sb(top, "eps", [P, 1])
        cvec = sb(top, "cvec", [P, DK, 2])
        svec = sb(top, "svec", [P, DK, MRING, 2 * MRING])
        mrow = sb(top, "modulation_rows", [2 * MRING, BLK])
        bmod = sb(top, "b_mod", [P, 2 * MCH])
        g1 = sb(top, "norm1_g", [P, 2, DK])
        g2 = sb(top, "norm2_g", [P, 2, DK])
        gf = sb(top, "final_g", [P, DK])
        cw = sb(top, "conv_w", [P, 2, 3, 12])
        cb = sb(top, "conv_b", [P, 2, 12])
        hyb = sb(top, "hyena_bias", [P, 2, 2, 4])
        mod = sb(top, "modulation", [P, 2 * MCH, 2])
        na1 = sb(top, "norm1_scale", [P, DK, 2])
        na2 = sb(top, "norm2_scale", [P, DK, 2])
        rs = sb(top, "rms", [P, TOK])
        sq = sb(top, "squares", [P, 2, TOK])
        router = sb(top, "router", [P, DK, NE])
        RTH = sb(top, "router_hi", [P, DK, NE], R32)
        RTL = sb(top, "router_lo", [P, DK, NE], R32)

        PS = top.enter_context(nc.psum_tensor("psum", [P, 8, 512], F32))

        st = ExitStack()
        raw = sb(st, "raw_units", [P, 2, 2048])
        WH = sb(st, "units_hi", [P, 2, 2048], R32)
        WL = sb(st, "units_lo", [P, 2, 2048], R32)
        m1 = ExitStack()
        mraw1 = sb(m1, "mod1_units", [P, MRING, 2048])
        m1.close()
        HH = sb(st, "h_hi", [P, DK, TOK], R32)
        HL = sb(st, "h_lo", [P, DK, TOK], R32)
        mix = ExitStack()
        fi = ExitStack()
        decay = sb(fi, "decay", [P, 2, 2, HY_W])
        fw3 = sb(fi, "filter_w3", [64, 2, HY_W])
        fi.close()
        OHH = sb(mix, "hyena_out_hi", [P, 4, TOK], R32)
        OHL = sb(mix, "hyena_out_lo", [P, 4, TOK], R32)
        hy = ExitStack()
        spec = sb(hy, "filter_spectra", [BINS, 2, 5, HY_W])
        dftf = sb(hy, "dft_forward", [P, 2, 4 * BINS])
        dftk = sb(hy, "dft_filter", [P, 2, 5 * BINS])
        dfti = sb(hy, "dft_inverse", [BINS, 4, L])
        m0 = ExitStack()
        mraw0 = sb(m0, "mod0_units", [P, MRING, 2048])
        m0.close()
        U = sb(hy, "hyena_u", [P, 12, TOK])
        fl = ExitStack()
        posT = sb(fl, "positions", [33, L])
        fw1 = sb(fl, "filter_w1", [33, 64])
        fw2 = sb(fl, "filter_w2", [64, 64])
        fb = sb(fl, "filter_vectors", [64, 4])
        arg = sb(fl, "sine_argument", [64, 2, L])
        turns = sb(fl, "sine_turns", [64, L])
        part = sb(fl, "sine_part", [64, L])
        act1 = sb(fl, "filter_act", [64, 2, L])
        taps = sb(fl, "filter_taps", [P, 2, 2, HY_W])
        fl.close()
        cv = ExitStack()
        VT = sb(cv, "tokens_major", [P, 2, HY_W])
        Y = sb(cv, "product_spectrum", [BINS, 4, HY_W])
        pt = sb(cv, "product_terms", [BINS, 2, HY_W])
        zt = sb(cv, "conv_sum", [P, 4, L])
        cv.close()
        hy.close()
        OAH = sb(mix, "att_out_hi", [P, 4, TOK], R32)
        OAL = sb(mix, "att_out_lo", [P, 4, TOK], R32)
        at = ExitStack()
        QK = sb(at, "qk", [P, 8, TOK])
        V = sb(at, "v", [P, 4, ATT_W])
        bias = sb(at, "att_bias", [P, HEADS, 6 * GRID])
        mask = sb(at, "att_mask", [P, 6 * GRID])
        S = sb(at, "scores", [P, 2, TOK])
        nmax = sb(at, "neg_max", [P, 32])
        psums = sb(at, "prob_sums", [P, 32])
        rsum = sb(at, "recip_sums", [P, 32])
        PT = sb(at, "probs_T", [P, 2, TOK])
        OT = sb(at, "att_tokens_major", [P, 4, ATT_W])
        at.close()
        mg = ExitStack()
        MH = sb(mg, "merged_hi", [P, DK, TOK], R32)
        ML = sb(mg, "merged_lo", [P, DK, TOK], R32)
        sga = sb(mg, "sig_a", [P, 2, TOK])
        sgb = sb(mg, "sig_b", [P, 2, TOK])
        mg.close()
        mix.close()
        ff = ExitStack()
        MDH = sb(ff, "mid_hi", [P, FK, TOK], R32)
        MDL = sb(ff, "mid_lo", [P, FK, TOK], R32)
        ff.close()
        st.close()
        mo = ExitStack()
        eraw = sb(mo, "expert_raw", [P, RAW, 2048])
        EH = sb(mo, "expert_hi", [P, SPLIT, 2048], R32)
        EL = sb(mo, "expert_lo", [P, SPLIT, 2048], R32)
        rt = ExitStack()
        RH = sb(rt, "moe_h_hi", [P, DK, L], R32)
        RL = sb(rt, "moe_h_lo", [P, DK, L], R32)
        rt.close()
        selw = sb(mo, "select_weighted", [P, 2, NE, P])
        sel = sb(mo, "select", [P, 2, NE, P])
        mt = ExitStack()
        mo_h = sb(mt, "moe_h", [P, DK, L])
        mt.close()
        GH = sb(mo, "gathered_hi", [P, DK, P], R32)
        GL = sb(mo, "gathered_lo", [P, DK, P], R32)
        mo_ht = sb(mo, "moe_h_tokens", [P, 2, D])
        selT = sb(mo, "scatter", [P, NE, L])
        sil = sb(mo, "silu_block", [P, BLK])
        mid = sb(mo, "mid_block", [P, BLK])
        TH = sb(mo, "midT_hi", [P, 2, P], R32)
        TL = sb(mo, "midT_lo", [P, 2, P], R32)
        yexp = sb(mo, "expert_out", [P, D])
        logits = sb(mo, "logits", [P, 2, NE])
        tv = sb(mo, "top_values", [P, 2, 8])
        ti = sb(mo, "top_index", [P, 2, 8], U32)
        tif = sb(mo, "top_index_f", [P, 2, 8])
        gt = sb(mo, "top_gates", [P, 2, 4])
        oh = sb(mo, "one_hot", [P, 2, 4, NE])
        msk = sb(mo, "chosen", [P, 2, NE])
        wex = sb(mo, "expert_weight", [P, 2, NE])
        over = sb(mo, "overflow", [P, NE])
        overi = sb(mo, "overflow_flag", [P, NE], mybir.dt.int32)
        rank = sb(mo, "rank", [P, 2, NE])
        tri = sb(mo, "before", [P, P])
        iot = sb(mo, "iota", [P, L])
        mo.close()

        consts_in = sem("consts_in")
        x_in = sem("x_in")
        filt_in = sem("filt_in")
        bias_in = sem("bias_in")
        raw_in = [sem("raw_in0"), sem("raw_in1")]
        hi_done = sem("hi_done")
        lo_done = sem("lo_done")
        unit_done = sem("unit_done")
        evac = sem("evac")
        dve_chain = sem("dve_chain")
        pool_chain = sem("pool_chain")
        s_ready = sem("s_ready")
        m_in = [sem(f"m_in{n_}") for n_ in range(MRING)]
        md_pe = sem("md_pe")
        md_row, md_tr, md_out = sem("md_row"), sem("md_turn"), sem("md_out")
        setup_done = sem("setup_done")
        f_pe, f_po, f_ac, f_dv = (sem("f_" + s) for s in ("pe", "po", "ac", "dv"))
        n_sq, n_pe, n_rt = sem("n_sq"), sem("n_pe"), sem("n_rt")
        n_t, n_hi, n_lo = sem("n_t"), sem("n_hi"), sem("n_lo")
        c_ac = sem("c_ac")
        y_t, y_vt, y_d, y_y, y_i, y_z = (sem("y_" + s) for s in ("t", "vt", "d", "y", "i", "z"))
        y_hi, y_lo = sem("y_hi"), sem("y_lo")
        a_s, a_sc, a_ex, a_t, a_pt, a_o = (sem("a_" + s) for s in ("s", "sc", "ex", "t", "pt", "o"))
        a_on, a_ot, a_hi, a_lo = (sem("a_" + s) for s in ("on", "ot", "hi", "lo"))
        a_flip, a_bias = sem("a_flip"), sem("a_bias")
        m_sig, m_sum, m_hi, m_lo = (sem("m_" + s) for s in ("sig", "sum", "hi", "lo"))
        up_silu, up_mid, up_hi, up_lo = (sem("up_" + s) for s in ("silu", "mid", "hi", "lo"))
        out_done = sem("out_done")
        o_ready = sem("o_ready")
        r_split, r_pe, r_mask, r_rank, r_ev, h_tr, h_ev = (sem("r_" + s) for s in
            ("split", "pe", "mask", "rank", "ev", "htr", "hev"))
        flag_ready = sem("flag_ready")
        r_cnt = sem("r_cnt")
        p_sel, p_tr, p_selT = sem("p_sel"), sem("p_tr"), sem("p_selT")
        e_in = [sem(f"e_in{n}") for n in range(RAW)]
        e_hi, e_lo, e_use = sem("e_hi"), sem("e_lo"), sem("e_use")
        e_silu, e_mid, e_tr, e_th, e_tl = (sem("e_" + s) for s in ("silu", "mid", "tr", "th", "tl"))
        g_pe, g_hi, g_lo, y_ev, sc_pe, sc_ev = (sem("g_" + s) for s in
            ("pe", "hi", "lo", "yev", "scpe", "scev"))

        evb, n = [{}, {}], 0
        for l in range(2):
            n += 2 * (l == 0)
            for name, count in (("u", U_U), ("qkv", QKV_U), ("merge", 0), ("wo", WO_U)) + \
                    ((("up", 0), ("down", DK)) if l == 0 else ()):
                evb[l][name] = n
                n += count

        norm_c0 = [0, 0, 0, L, L]
        items_before = [0, 16, 32, 48, 56]

        block = top.enter_context(nc.Block())

        @block.sync
        def _(sp):
            def load(u, s, dst, src):
                sp.dma_start(dst, src).then_inc(raw_in[s], 16)

            def free(u):
                if not isinstance(u, int) or u >= 2:
                    sp.wait_ge(lo_done, u - 1)

            def std(w, col):
                return w[:, bass.ds(col, BLK)].rearrange("(k p) c -> p k c", p=P)

            def raw_std(s):
                return raw[:, s, :].rearrange("p (k c) -> p k c", k=DK)

            def mod_load(l, u, n):
                dst = (mraw0, mraw1)[l][:, n, :].rearrange("p (k c) -> p k c", k=DK)
                sp.dma_start(dst, std(t["w_mod"][l], u * BLK)).then_inc(m_in[n], 16)

            for l in range(2):
                b = base[l]
                if l == 0:
                    for n in range(MRING):
                        mod_load(0, n, n)
                    for s in range(2):
                        load(0, s, raw_std(s), std(t["w_in"][l], OFF_U + s * BLK))
                    with sp.Fori(1, MOD_U // MRING) as i:
                        for n in range(MRING):
                            sp.wait_ge(md_pe, MRING * i + n - MRING + 1)
                            mod_load(0, MRING * i + n, n)
                with sp.Fori(1 - l, U_U // 2) as i:
                    for s in range(2):
                        free(b["u"] + 2 * i + s)
                        load(0, s, raw_std(s), std(t["w_in"][l], OFF_U + (2 * i + s) * BLK))
                with sp.Fori(0, QKV_U // 2) as i:
                    for s in range(2):
                        free(b["qkv"] + 2 * i + s)
                        load(0, s, raw_std(s), std(t["w_in"][l], (2 * i + s) * BLK))
                with sp.Fori(0, 2) as i:
                    for n in range(6):
                        free(b["merge"] + 6 * i + n)
                        pair, kind = n // 3, n % 3
                        col = (2 * i + pair) * BLK
                        w = t["w_opab"][l] if kind == 2 else t["w_in"][l]
                        load(0, n % 2, raw_std(n % 2), std(w, (OFF_GA, OFF_GB, D)[kind] + col))
                with sp.Fori(0, WO_U // 2) as i:
                    for s in range(2):
                        free(b["wo"] + 2 * i + s)
                        load(0, s, raw_std(s), std(t["w_opab"][l], (2 * i + s) * BLK))
                if l == 0:
                    with sp.Fori(0, NB) as i:
                        for s, w in enumerate(("ffn_w1", "ffn_w3")):
                            free(b["up"] + 2 * i + s)
                            load(0, s, raw_std(s), std(t[w], i * BLK))
                    def down_loads(i):
                        for s in range(2):
                            free(b["down"] + 2 * i + s)
                            load(0, s, raw[:, s, 0:11 * P].rearrange("p (k c) -> p k c", k=11),
                                 t["ffn_w2"][s * 11 * P:(s + 1) * 11 * P, bass.ds(i * P, P)]
                                 .rearrange("(k p) c -> p k c", p=P))

                    def next_mod_loads(i):
                        for n in range(MRING):
                            sp.wait_ge(md_pe, MOD_U + MRING * i + n - MRING + 1)
                            mod_load(1, MRING * i + n, n)

                    down_loads(0)
                    sp.wait_ge(unit_done, b["down"])
                    with sp.Fori(0, DK - 1) as i:
                        down_loads(i + 1)
                        next_mod_loads(i)
                    next_mod_loads(DK - 1)
            sp.wait_ge(lo_done, n_units)
            sp.wait_ge(unit_done, n_units)
            def experts(g):
                with sp.Fori(0, NE) as e:
                    E0 = g * NE + e
                    for j, (kind, b) in enumerate(ORDER):
                        sp.wait_ge(e_lo, NU + NU * E0 + slot_before(j, RAW) + 1)
                        dst = eraw[:, j % RAW, :]
                        if kind < 2:
                            w = t["moe_w1"] if kind == 0 else t["moe_w3"]
                            src = w[bass.ds(e * D, D), b * BLK:(b + 1) * BLK].rearrange("(k p) c -> p k c", p=P)
                            dst = dst.rearrange("p (k c) -> p k c", k=DK)
                        else:
                            src = t["moe_w2"][bass.ds(e * FF + b * BLK, BLK), :].rearrange("(k p) c -> p k c", p=P)
                            dst = dst.rearrange("p (k c) -> p k c", k=2)
                        sp.dma_start(dst, src).then_inc(e_in[j % RAW], 16)

            experts(0)
            sp.wait_ge(flag_ready, 1)
            with sp.If(sp.value_load(overi[0:1, 0:1], min_val=0, max_val=1) == 1):
                experts(1)
            sp.wait_ge(o_ready, DK)
            sp.dma_start(out.rearrange("(k p) t -> p k t", p=P), X[:, :, L:TOK]).then_inc(out_done, 16)
            sp.wait_ge(out_done, 16)

        @block.gpsimd
        def _(pool):
            def load(dst, src, s):
                pool.dma_start(dst, src).then_inc(s, 16)
            small = [(cvec[:], t["cc"]), (ident[:], t["ident"]), (flip[:], t["flip"]), (bmod[:], t["b_mod"]),
                     (g1[:], t["norm1_g"]), (g2[:], t["norm2_g"]), (gf[:], t["final_g"]),
                     (cw[:], t["hy_conv_w"]), (cb[:], t["hy_conv_b"]), (hyb[:], t["hy_bias"]),
                     (router[:], t["moe_router"])]
            assert len(small) == N_SMALL
            def filter_inputs(l):
                return [(posT[:], t["posT"]), (fw1[:], t["hy_w1"][l]), (fw2[:], t["hy_w2"][l]), (fb[:], t["fvec"][l]),
                        (fw3[:], t["hy_w3"][l].rearrange("f (o c) -> f o c", o=2)),
                        (decay[:], t["decay"]), (dftk[:], t["dftk"]), (dftf[:], t["dftf"]), (dfti[:], t["dfti"])]

            for dst, src in small[:1]:
                load(dst, src, consts_in)
            for dst, src in filter_inputs(0)[:4]:
                load(dst, src, filt_in)
            for dst, src in small[1:]:
                load(dst, src, consts_in)
            chain = Chain(pool, pool_chain)
            link = chain.link
            TS = nc.gpsimd.tensor_scalar

            def sine_argument(l, j):
                pool.wait_ge(f_ac, 14 * l + 2 * j + 1)
                a = arg[:, j, :]
                link(TS(a, a, fb[:, 2 * j + 1:2 * j + 2], None, ALU.mult))
                link(TS(turns[:], a, 1.0 / (2 * math.pi), MAGIC, ALU.mult, ALU.add))
                link(TS(turns[:], turns[:], MAGIC, None, ALU.subtract))
                for c in TWO_PI_PARTS:
                    link(TS(part[:], turns[:], -c, None, ALU.mult))
                    link(nc.gpsimd.tensor_tensor(a, a, part[:], ALU.add))
                TS(a, a, PI_CLIP, -PI_CLIP, ALU.min, ALU.max).then_inc(f_po, 1)

            for l in range(2):
                if l == 1:
                    pool.wait_ge(unit_done, base[1]["u"])
                    pool.wait_ge(evac, evb[0]["down"] + DK)
                filt = filter_inputs(l)
                assert len(filt) == N_FILT
                for dst, src in (filt if l else filt[4:]):
                    load(dst, src, filt_in)
                if l == 0:
                    load(X[:, :, 0:L], t["ctxT"].rearrange("(k p) t -> p k t", p=P), x_in)
                    load(X[:, :, L:TOK], t["xT"].rearrange("(k p) t -> p k t", p=P), x_in)
                pool.wait_ge(filt_in, 16 * N_FILT * (l + 1))
                for j in range(2):
                    sine_argument(l, j)
                pool.wait_ge(y_z, (4 if l == 0 else 6))
                pool.wait_ge(y_lo, (2 if l == 0 else 3))
                load(mask[:], t["mask"], bias_in)
                rp = t["rpb"]
                for h in range(HEADS):
                    for half in range(2):
                        first = ((l * HEADS + h) * RPB_R + 5 - half) * RPB_C + WIN - GRID
                        src = bass.AP(rp.tensor, first, [[1, GRID], [RPB_C, 6], [1, GRID]])
                        load(bias[half * GRID:(half + 1) * GRID, h, :].rearrange("p (r c) -> p r c", r=6), src, bias_in)
            pool.wait_ge(unit_done, n_units)
            load(tri[:], t["tri"], bias_in)
            load(iot[:], t["iota"], bias_in)

        @block.scalar
        def _(act):
            A = nc.scalar.activation

            def hi(u, s, half):
                act.wait_ge(raw_in[s], 16 * half + 16)
                if not isinstance(u, int) or u >= 2:
                    act.wait_ge(unit_done, u - 1)
                A(WH[:, s, :], raw[:, s, :], ACT.Copy).then_inc(hi_done, 1)

            def ahead(b, n, s):
                u = b + n + 2
                half = (u - s) // 2 if isinstance(u, int) else None
                hi(u, s, half)

            def ahead_loop(b, i, stride, n):
                u0 = b + n + 2
                hi(u0 + stride * i, n % 2, u0 // 2 + (stride // 2) * i)

            def norm_roots(q):
                c0 = norm_c0[q]
                if q == 0:
                    act.wait_ge(x_in, 32)
                elif q < 4:
                    act.wait_ge(evac, (None, evb[0]["wo"] + WO_U, evb[0]["down"] + DK, evb[1]["wo"] + WO_U)[q])
                for k in range(DK):
                    if 8 * q + k >= 2:
                        act.wait_ge(n_pe, 8 * q + k - 1)
                    if q and k < 2:
                        act.wait_ge(n_lo, items_before[q])
                    A(sq[:, k % 2, c0:TOK], X[:, k, c0:TOK], ACT.Square).then_inc(n_sq, 1)
                act.wait_ge(n_pe, 8 * q + 8)
                A(rs[:, c0:TOK], PS[:, 7, c0:TOK], ACT.Sqrt, bias=eps[:, 0:1], scale=1.0 / D).then_inc(n_rt, 1)

            def norm_hi(q, shift, hh):
                mb = MCH * (q // 2) + shift * DK
                streams = range(1 if q == 3 else 0, 2)
                it = items_before[q]
                for k in range(DK):
                    for s in streams:
                        act.wait_ge(n_t, it + 1)
                        dst = hh[:, k, 0:L] if q == 3 else hh[:, k, s * L:(s + 1) * L]
                        A(dst, sq[:, it % 2, 0:L], ACT.Identity,
                          bias=mod[:, mb + k, s:s + 1]).then_inc(n_hi, 1)
                        if q == 3:
                            A(mo_h[:, k, :], sq[:, it % 2, 0:L], ACT.Identity,
                              bias=mod[:, mb + k, s:s + 1]).then_inc(n_hi, 1)
                        it += 1

            act.wait_ge(consts_in, 16 * N_SMALL)
            act.wait_ge(setup_done, 3)
            for n in range(MRING):
                A(svec[:, :, n, 2 * n:2 * n + 2], cvec[:], ACT.Silu).then_inc(s_ready, 1)
            A(RTH[:], router[:], ACT.Copy).then_inc(r_split, 1)
            for s in range(2):
                hi(s, s, 0)

            def spectra_out(l):
                for q in range(10):
                    act.wait_ge(f_pe, 13 * l + 4 + q)
                    A(spec[:, q // 5, q % 5, :], PS[0:BINS, q % 8, :], ACT.Copy).then_inc(f_ac, 1)

            conv_items = 0
            att_n = att_q = 0
            for l in range(2):
                b = base[l]
                c0 = 0 if l == 0 else L
                if l == 1:
                    norm_roots(2)
                for j in range(2):
                    act.wait_ge(f_pe, 13 * l + j + 1)
                    A(arg[:, j, :], PS[0:64, 6, 0:L], ACT.Identity, bias=fb[:, 2 * j:2 * j + 1]).then_inc(f_ac, 1)
                    act.wait_ge(f_po, 2 * l + j + 1)
                    A(act1[:, j, :], arg[:, j, :], ACT.Sin).then_inc(f_ac, 1)
                if l == 0:
                    norm_roots(0)
                    spectra_out(0)
                norm_hi(2 * l, SHIFT1, HH)
                with act.Fori(0, U_U // 2) as i:
                    for n in range(2):
                        ahead_loop(b["u"], i, 2, n)
                        act.wait_ge(unit_done, b["u"] + 2 * i + n + 1)
                        for j in range(2):
                            m = 4 * i + 2 * n + j
                            A(U[:, m, c0:TOK], PS[:, 2 * n + j, c0:TOK], ACT.Identity,
                              bias=cb[:, l, bass.ds(m, 1)], scale=cw[:, l, 1, bass.ds(m, 1)]).then_inc(c_ac, 1)
                if l == 1:
                    spectra_out(1)
                for o in range(2):
                    for s in range(1 if l else 0, 2):
                        n = conv_items
                        act.wait_ge(y_t, n + 1)
                        if n:
                            act.wait_ge(y_d, n)
                        for c in range(2):
                            last = A(VT[:, c, :], PS[:, 4 + c, :], ACT.Copy)
                        last.then_inc(y_vt, 1)
                        if o == 1:
                            act.wait_ge(y_z, n + 1)
                            A(OHH[:, :, s * L:(s + 1) * L], zt[:, :, :], ACT.Copy).then_inc(y_hi, 1)
                        conv_items += 1
                with act.Fori(0, QKV_U // 2) as i:
                    for n in range(2):
                        ahead_loop(b["qkv"], i, 2, n)
                def probs_out(n, width):
                    act.wait_ge(a_t, n + 1)
                    if n >= 2:
                        act.wait_ge(a_o, n - 1)
                    A(PT[:, n % 2, 0:width], PS[:, 2 + n % 2, 0:width], ACT.Copy).then_inc(a_pt, 1)
                for qc in range(0 if l == 0 else 2, 4):
                    width = TOK if qc >= 2 else L
                    for h in range(HEADS):
                        n = att_n
                        act.wait_ge(a_sc, n + 1)
                        A(S[:, n % 2, 0:width], S[:, n % 2, 0:width], ACT.Exp, bias=nmax[:, n % 32:n % 32 + 1],
                          accum_out=psums[:, n % 32:n % 32 + 1]).then_inc(a_ex, 1)
                        if h:
                            probs_out(n - 1, width)
                        att_n += 1
                    probs_out(att_n - 1, width)
                    act.wait_ge(a_ot, att_q + 1)
                    A(OAH[:, :, qc * P:(qc + 1) * P], PS[:, 6 + qc % 2, :].rearrange("p (c q) -> p c q", c=4),
                      ACT.Copy).then_inc(a_hi, 1)
                    att_q += 1
                mb = 4 * l
                if l == 0:
                    act.nop().then_inc(m_sig, 1)
                with act.Fori(0, 2) as i:
                    for n in range(6):
                        pair, kind = n // 3, n % 3
                        ahead_loop(b["merge"], i, 6, n)
                        act.wait_ge(unit_done, b["merge"] + 6 * i + n + 1)
                        if kind < 2:
                            act.wait_ge(m_lo, mb + 2 * i + pair + 1)
                            dst = sga if kind == 0 else sgb
                            A(dst[:, :, c0:TOK], PS[:, 2 * kind:2 * kind + 2, c0:TOK], ACT.Sigmoid).then_inc(m_sig, 1)
                        else:
                            act.wait_ge(m_sum, mb + 2 * i + pair + 2)
                            A(MH[:, bass.ds(2 * (2 * i + pair), 2), c0:TOK], sga[:, :, c0:TOK], ACT.Copy).then_inc(m_hi, 1)
                for n in range(WO_U):
                    if l == 0 or n < 2:
                        hi(b["wo"] + n + 2, n % 2, b["wo"] // 2 + (n + 2) // 2)
                norm_roots(2 * l + 1)
                if l == 0:
                    norm_hi(1, SHIFT2, HH)
                    act.nop().then_inc(up_silu, 1)
                    with act.Fori(0, NB) as i:
                        ahead_loop(b["up"], i, 2, 0)
                        act.wait_ge(unit_done, b["up"] + 2 * i + 1)
                        act.wait_ge(up_lo, i + 1)
                        A(sq[:, :, :], PS[:, 0:2, :], ACT.Silu).then_inc(up_silu, 1)
                        ahead_loop(b["up"], i, 2, 1)
                        act.wait_ge(up_mid, i + 2)
                        A(MDH[:, bass.ds(2 * i, 2), :], sq[:, :, :], ACT.Copy).then_inc(up_hi, 1)
                    with act.Fori(0, DK) as i:
                        for n in range(2):
                            ahead_loop(b["down"], i, 2, n)
                else:
                    act.wait_ge(unit_done, n_units)
                    norm_hi(3, SHIFT2, RH)
            for c in range(2):
                act.wait_ge(r_mask, c + 1)
                A(gt[:, c, 1:2], gt[:, c, 0:1], ACT.Exp).then_inc(r_ev, 1)
            for c in range(2):
                for hf in range(2):
                    act.wait_ge(h_tr, 2 * c + hf + 1)
                    A(mo_ht[:, c, hf * 512:(hf + 1) * 512], PS[:, 2 * c + hf, :], ACT.Copy).then_inc(h_ev, 1)
            def experts(g):
                for q in range(4):
                    act.wait_ge(p_tr, 4 * g + q + 1)
                    A(selT[:, 2 * q:2 * q + 2, :], PS[:, q, :].rearrange("p (e t) -> p e t", e=2), ACT.Copy).then_inc(p_selT, 1)

                def gathered(E0):
                    for q in range(2):
                        act.wait_ge(g_pe, 2 * E0 + q + 1)
                        A(GH[:, 4 * q:4 * q + 4, :], PS[:, 5 + q, :].rearrange("p (k j) -> p k j", k=4), ACT.Copy).then_inc(g_hi, 1)

                def ehi(E0, j):
                    r = j % RAW
                    loads = len(range(r, NU, RAW))
                    act.wait_ge(e_in[r], 16 * loads * E0 + 16 * (j // RAW + 1))
                    act.wait_ge(e_use, NU + NU * E0 + slot_before(j, SPLIT) + 1)
                    A(EH[:, j % SPLIT, :], eraw[:, r, :], ACT.Copy).then_inc(e_hi, 1)

                def turned(E0, b):
                    act.wait_ge(e_tr, NB * E0 + b + 1)
                    if b:
                        act.wait_ge(e_use, NU + NU * E0 + POS[(2, b - 1)] + 1)
                    A(TH[:], PS[:, 2, 0:2 * P].rearrange("p (k j) -> p k j", k=2), ACT.Copy).then_inc(e_th, 1)

                def expert(e, last):
                    E0 = g * NE + e
                    for j, (kind, b) in enumerate(ORDER):
                        if kind == 0:
                            act.wait_ge(e_use, NU + NU * E0 + j + 1)
                            act.wait_ge(e_mid, NB * E0 + b + 1)
                            A(sil[:], PS[:, 0, 0:BLK], ACT.Silu).then_inc(e_silu, 1)
                            if b:
                                turned(E0, b - 1)
                        if j + SPLIT < NU:
                            ehi(E0, j + SPLIT)
                        if j == NU - 2:
                            turned(E0, NB - 1)
                    act.wait_ge(e_use, NU + NU * E0 + NU)
                    act.wait_ge(sc_pe, 4 * E0 + 4)
                    A(yexp[:, 0:512], PS[:, 3, :], ACT.Copy).then_inc(y_ev, 1)
                    if not last:
                        ehi(E0 + 1, 0)
                        gathered(E0 + 1)
                        for j in range(1, SPLIT):
                            ehi(E0 + 1, j)

                for j in range(SPLIT):
                    ehi(g * NE, j)
                gathered(g * NE)
                with act.Fori(0, NE - 1) as e:
                    expert(e, False)
                expert(NE - 1, True)
                act.wait_ge(sc_ev, 4 + 4 * NE * (g + 1))

            experts(0)
            act.wait_ge(flag_ready, 1)
            with act.If(act.value_load(overi[0:1, 0:1], min_val=0, max_val=1) == 1):
                experts(1)
            norm_roots(4)

        @block.vector
        def _(dve):
            V_ = nc.vector
            TT, TS, STT = V_.tensor_tensor, V_.tensor_scalar, V_.scalar_tensor_tensor
            chain = Chain(dve, dve_chain)
            link = chain.link

            def lo(u, s):
                dve.wait_ge(hi_done, u + 1)
                TT(WL[:, s, :], raw[:, s, :], WH[:, s, :].bitcast(F32), ALU.subtract).then_inc(lo_done, 1)

            def mod_row(l, i):
                dve.wait_ge(md_pe, MOD_U * l + MRING * i + MRING)
                V_.tensor_copy(mrow[:], PS[0:2 * MRING, MODB, 0:BLK]).then_inc(md_row, 1)

            def mod_out(l, i):
                dve.wait_ge(md_tr, MTRIPS * l + i + 1)
                m = bass.ds(MCH * l + 2 * MRING * i, 2 * MRING)
                TT(mod[:, m, :], PS[:, MTB, 0:4 * MRING].rearrange("p (m s) -> p m s", s=2),
                   bmod[:, m].unsqueeze(2).to_broadcast([P, 2 * MRING, 2]), ALU.add).then_inc(md_out, 1)

            def mod_both(l, i):
                mod_row(l, i)
                mod_out(l, i)

            def norm_lo(q, shift, scale, hh, hl, between=None):
                mb = MCH * (q // 2) + shift * DK
                c0 = norm_c0[q]
                streams = range(1 if q == 3 else 0, 2)
                dve.wait_ge(n_rt, q + 1)
                link(V_.reciprocal(rs[:, c0:TOK], rs[:, c0:TOK]))
                todo = [(k, s) for k in range(DK) for s in streams]
                first = items_before[q]

                def low(j):
                    k, s = todo[j]
                    it = first + j
                    dve.wait_ge(n_hi, it + 1 if q < 3 else first + 2 * (j + 1))
                    dst = slice(0, L) if q == 3 else slice(s * L, (s + 1) * L)
                    STT(hl[:, k, dst], sq[:, it % 2, 0:L], mod[:, mb + k, s:s + 1],
                        hh[:, k, dst].bitcast(F32), ALU.add, ALU.subtract).then_inc(n_lo, 1)

                for j, (k, s) in enumerate(todo):
                    it = first + j
                    if j >= 2:
                        dve.wait_ge(n_lo, it - 1)
                    STT(sq[:, it % 2, 0:L], X[:, k, s * L:(s + 1) * L], scale[:, k, s:s + 1],
                        rs[:, s * L:(s + 1) * L], ALU.mult, ALU.mult).then_inc(n_t, 1)
                    if j:
                        low(j - 1)
                    if between:
                        between(j)
                low(len(todo) - 1)

            V_.memset(ones[:], 1.0).then_inc(setup_done, 1)
            V_.memset(svec[:], 0.0).then_inc(setup_done, 1)
            V_.memset(eps[:], EPS).then_inc(setup_done, 1)
            dve.sem_inc(evac, 2)
            dve.wait_ge(setup_done, 3)
            dve.wait_ge(r_split, 1)
            TT(RTL[:], router[:], RTH[:].bitcast(F32), ALU.subtract).then_inc(r_split, 1)
            for s in range(2):
                lo(s, s)
            dve.wait_ge(consts_in, 16 * N_SMALL)
            dve.wait_ge(x_in, 32)
            conv_items = conv_c = 0
            att_n = att_q = 0
            for l in range(2):
                b = base[l]
                c0 = 0 if l == 0 else L
                ns = 2 - l
                def decayed(l):
                    dve.wait_ge(f_pe, 13 * l + 3)
                    for o in range(2):
                        for pc in range(2):
                            TT(taps[:, o, pc, :], PS[:, TAPB[l] + 2 * o + pc, :], decay[:, pc, o, :],
                               ALU.mult).then_inc(f_dv, 1)

                def norm_scale(scale, which, g):
                    for s in range(2):
                        link(STT(scale[:, :, s], mod[:, MCH * l + which * DK:MCH * l + (which + 1) * DK, s], 1.0,
                                 g[:, l, :], ALU.add, ALU.mult))

                if l == 0:
                    for i in range(3):
                        mod_both(0, i)
                    decayed(0)
                    dve.wait_ge(md_out, 3)
                norm_scale(na1, SCALE1, g1)
                norm_lo(2 * l, SHIFT1, na1, HH, HL, 
                        (lambda j: mod_both(0, 3 + j // 3) if j % 3 == 2 else None) if l == 0 else None)
                if l == 0:
                    dve.wait_ge(md_out, MTRIPS)
                if l == 1:
                    decayed(1)
                norm_scale(na2, SCALE2, g2)
                Ust = U[:, :, :].rearrange("p m (s t) -> p m s t", s=2)
                with dve.Fori(0, U_U // 2) as i:
                    chain.enter(i, 4, U_U // 2)
                    for n in range(2):
                        lo(b["u"] + 2 * i + n + 2, n)
                        for j in range(2):
                            m = 4 * i + 2 * n + j
                            dve.wait_ge(c_ac, 12 * l + 1 + m)
                            pv = PS[:, 2 * n + j, :].rearrange("p (s t) -> p s t", s=2)
                            row = U[:, bass.ds(m, 1), :].rearrange("p m (s t) -> p (m s) t", s=2)
                            sl = slice(l, 2)
                            link(STT(row[:, sl, 1:L], pv[:, sl, 0:L - 1], cw[:, l, 0, bass.ds(m, 1)],
                                     row[:, sl, 1:L], ALU.mult, ALU.add))
                            last = STT(row[:, sl, 0:L - 1], pv[:, sl, 1:L], cw[:, l, 2, bass.ds(m, 1)],
                                       row[:, sl, 0:L - 1], ALU.mult, ALU.add)
                        last.then_inc(evac, 1)
                    chain.exit()
                dve.wait_ge(evac, evb[l]["qkv"])
                for o in range(2):
                    for s in range(l, 2):
                        n = conv_items
                        dve.wait_ge(y_d, n + 1)
                        if n:
                            dve.wait_ge(y_i, n)
                        F = spec[:, o]
                        for j in range(2):
                            are, aim = PS[0:BINS, j, :], PS[0:BINS, 2 + j, :]
                            fre, fim, fren = F[:, j], F[:, 2 + j], (F[:, 4] if j == 0 else F[:, 1])
                            TT(Y[:, j, :], are, fre, ALU.mult)
                            TT(pt[:, 0, :], aim, fim, ALU.mult)
                            TT(Y[:, 2 + j, :], are, fim, ALU.mult)
                            link(TT(pt[:, 1, :], aim, fren, ALU.mult))
                            TT(Y[:, j, :], Y[:, j, :], pt[:, 0, :], ALU.subtract)
                            last = TT(Y[:, 2 + j, :], Y[:, 2 + j, :], pt[:, 1, :], ALU.add)
                            link(last) if j == 0 else last.then_inc(y_y, 1)
                        dve.wait_ge(y_i, n + 1)
                        if conv_c:
                            dve.wait_ge(y_lo, conv_c)
                        cols = slice(s * L, (s + 1) * L)
                        for c in range(4):
                            last = STT(zt[:, c, :], U[:, c, cols], hyb[:, l, o, c:c + 1], PS[:, 6 + c // 2, (c % 2) * L:(c % 2 + 1) * L],
                                       ALU.mult, ALU.add)
                        link(last)
                        dst = zt[:, :, :] if o else U[:, 0:4, cols]
                        TT(dst, zt[:, :, :], U[:, 4 + 4 * o:8 + 4 * o, cols], ALU.mult).then_inc(y_z, 1)
                        if o:
                            dve.wait_ge(y_hi, conv_c + 1)
                            TT(OHL[:, :, cols], zt[:, :, :], OHH[:, :, cols].bitcast(F32), ALU.subtract).then_inc(y_lo, 1)
                            conv_c += 1
                        conv_items += 1
                for n in range(QKV_U):
                    lo(b["qkv"] + n + 2, n % 2)
                    dve.wait_ge(unit_done, b["qkv"] + n + 1)
                    if n == 0:
                        dve.wait_ge(y_lo, conv_c)
                    if n < 4:
                        first = c0 if n < 2 else 0
                        last = V_.tensor_copy(QK[:, 2 * n:2 * n + 2, first:TOK],
                                              PS[:, 2 * (n % 2):2 * (n % 2) + 2, first:TOK])
                    else:
                        src = PS[:, 2 * (n % 2):2 * (n % 2) + 2, :].rearrange("p a (b c) -> p (a b) c", b=2)
                        last = V_.tensor_copy(V[:, :, (n - 4) * BLK:(n - 3) * BLK], src)
                    last.then_inc(evac, 1)
                dve.wait_ge(bias_in, 16 * 17 * (l + 1))
                for h in range(HEADS):
                    dve.wait_ge(a_flip, HEADS * l + h + 1)
                    TT(bias[:, h, :], PS[:, 4 + h % 4, 0:6 * GRID], mask[:, :], ALU.add).then_inc(a_bias, 1)
                dve.wait_ge(a_bias, HEADS * (l + 1))
                for qc in range(2 * l, 4):
                    width = TOK if qc >= 2 else L
                    n0 = att_n
                    for h in range(HEADS):
                        n = att_n
                        dve.wait_ge(a_s, n + 1)
                        if n >= 2:
                            dve.wait_ge(a_t, n - 1)
                        last = TS(S[:, n % 2, 0:L], PS[:, n % 2, 0:L], SCALE, None, ALU.mult)
                        if qc >= 2:
                            bs = bias[:, h, (3 - qc) * P:(3 - qc) * P + L]
                            last = STT(S[:, n % 2, L:TOK], PS[:, n % 2, L:TOK], SCALE, bs, ALU.mult, ALU.add)
                        link(last)
                        V_.tensor_reduce(nmax[:, n % 32:n % 32 + 1], S[:, n % 2, 0:width], AX, ALU.max,
                                         negate=True).then_inc(a_sc, 1)
                        att_n += 1
                    dve.wait_ge(a_ex, att_n)
                    r0 = n0 % 32
                    link(V_.reciprocal(rsum[:, r0:r0 + HEADS], psums[:, r0:r0 + HEADS]))
                    dve.wait_ge(a_o, att_n)
                    src = PS[:, 4 + qc % 2, :].rearrange("p (h d) -> p h d", h=HEADS)
                    TT(OT[:, qc, :].rearrange("p (h d) -> p h d", h=HEADS), src,
                       rsum[:, r0:r0 + HEADS].unsqueeze(2).to_broadcast([P, HEADS, HD]), ALU.mult).then_inc(a_on, 1)
                    dve.wait_ge(a_hi, att_q + 1)
                    TT(OAL[:, :, qc * P:(qc + 1) * P], PS[:, 6 + qc % 2, :].rearrange("p (c q) -> p c q", c=4),
                       OAH[:, :, qc * P:(qc + 1) * P].bitcast(F32), ALU.subtract).then_inc(a_lo, 1)
                    att_q += 1
                if l == 0:
                    for credit in (m_sum, m_lo):
                        dve.nop().then_inc(credit, 1)
                with dve.Fori(0, 2) as i:
                    chain.enter(i, 2, 2)
                    for n in range(6):
                        pair, kind = n // 3, n % 3
                        lo(b["merge"] + 6 * i + n + 2, n % 2)
                        if kind == 2:
                            q = 4 * l + 2 * i + pair
                            dve.wait_ge(unit_done, b["merge"] + 6 * i + n + 1)
                            dve.wait_ge(m_sig, 2 * q + 3)
                            TT(sga[:, :, c0:TOK], sga[:, :, c0:TOK], PS[:, 4:6, c0:TOK], ALU.mult)
                            link(TT(sgb[:, :, c0:TOK], sgb[:, :, c0:TOK], PS[:, 6:8, c0:TOK], ALU.mult))
                            TT(sga[:, :, c0:TOK], sga[:, :, c0:TOK], sgb[:, :, c0:TOK], ALU.add).then_inc(m_sum, 1)
                            dve.wait_ge(m_hi, q + 1)
                            mm = bass.ds(2 * (2 * i + pair), 2)
                            TT(ML[:, mm, c0:TOK], sga[:, :, c0:TOK], MH[:, mm, c0:TOK].bitcast(F32), ALU.subtract).then_inc(m_lo, 1)
                    chain.exit()
                for n in range(WO_U):
                    if l == 0 or n < 2:
                        lo(b["wo"] + n + 2, n % 2)
                    dve.wait_ge(unit_done, b["wo"] + n + 1)
                    for j in range(2):
                        for s in range(l, 2):
                            m = 2 * n + j
                            cols = slice(s * L, (s + 1) * L)
                            last = STT(X[:, m, cols], PS[:, 2 * (n % 2) + j, cols], mod[:, MCH * l + GATE1 * DK + m, s:s + 1],
                                       X[:, m, cols], ALU.mult, ALU.add)
                    last.then_inc(evac, 1)
                if l == 0:
                    norm_lo(1, SHIFT2, na2, HH, HL)
                    for credit in (up_mid, up_lo):
                        dve.nop().then_inc(credit, 1)
                    with dve.Fori(0, NB) as i:
                        lo(b["up"] + 2 * i + 2, 0)
                        lo(b["up"] + 2 * i + 3, 1)
                        dve.wait_ge(up_silu, i + 2)
                        dve.wait_ge(unit_done, b["up"] + 2 * i + 2)
                        TT(sq[:, :, :], sq[:, :, :], PS[:, 2:4, :], ALU.mult).then_inc(up_mid, 1)
                        dve.wait_ge(up_hi, i + 1)
                        TT(MDL[:, bass.ds(2 * i, 2), :], sq[:, :, :], MDH[:, bass.ds(2 * i, 2), :].bitcast(F32),
                           ALU.subtract).then_inc(up_lo, 1)
                    with dve.Fori(0, DK // 2) as i:
                        for mm in range(2):
                            for s in range(2):
                                lo(b["down"] + 4 * i + 2 * mm + s + 2, s)
                            mod_row(1, 2 * i + mm)
                            dve.wait_ge(unit_done, b["down"] + 4 * i + 2 * mm + 2)
                            for s in range(2):
                                cols = slice(s * L, (s + 1) * L)
                                xm = X[:, bass.ds(2 * i + mm, 1), cols].rearrange("p m t -> p (m t)")
                                last = STT(xm, PS[:, mm, cols], mod[:, bass.ds(GATE2 * DK + 2 * i + mm, 1), s],
                                           xm, ALU.mult, ALU.add)
                            last.then_inc(evac, 1)
                            mod_out(1, 2 * i + mm)
                    dve.wait_ge(md_out, 2 * MTRIPS)
                else:
                    norm_lo(3, SHIFT2, na2, RH, RL)
            for c in range(2):
                dve.wait_ge(r_pe, c + 1)
                link(V_.tensor_copy(logits[:, c, :], PS[:, c, 0:NE]))
                link(V_.max(tv[:, c, :], logits[:, c, :]))
                link(V_.max_index(ti[:, c, :], tv[:, c, :], logits[:, c, :]))
                V_.tensor_copy(tif[:, c, :], ti[:, c, :])
                TT(gt[:, c, 0:1], tv[:, c, 1:2], tv[:, c, 0:1], ALU.subtract).then_inc(r_mask, 1)
            dve.wait_ge(bias_in, 16 * 36)
            for c in range(2):
                dve.wait_ge(r_ev, c + 1)
                link(TS(gt[:, c, 2:3], gt[:, c, 1:2], 1.0, None, ALU.add))
                link(V_.reciprocal(gt[:, c, 2:3], gt[:, c, 2:3]))
                link(TT(gt[:, c, 3:4], gt[:, c, 1:2], gt[:, c, 2:3], ALU.mult))
                for j in range(2):
                    link(TS(oh[:, c, j, :], iot[:, 0:NE], tif[:, c, j:j + 1], None, ALU.is_equal))
                    link(TS(oh[:, c, 2 + j, :], oh[:, c, j, :], gt[:, c, 2 + j:3 + j], None, ALU.mult))
                link(TT(wex[:, c, :], oh[:, c, 2, :], oh[:, c, 3, :], ALU.add))
                TT(msk[:, c, :], oh[:, c, 0, :], oh[:, c, 1, :], ALU.add).then_inc(r_mask, 1)
            dve.wait_ge(r_mask, 4)
            dve.wait_ge(r_rank, 1)
            for c in range(2):
                link(TS(rank[:, c, :], msk[:, c, :], -1000.0, 1000.0, ALU.mult, ALU.add))
                link(TT(rank[:, c, :], rank[:, c, :], PS[:, 4 + c, 0:NE], ALU.add))
            V_.tensor_reduce(over[:, 0:1], PS[:, 6, 0:NE], AX, ALU.max).then_inc(r_cnt, 1)
            dve.wait_ge(r_cnt, 1)
            TS(overi[:, 0:1], over[:, 0:1], P + 0.5, None, ALU.is_gt).then_inc(flag_ready, 1)
            dve.wait_ge(flag_ready, 1)
            dve.sem_inc(e_lo, NU)
            dve.sem_inc(e_mid, 1)
            dve.sem_inc(sc_ev, 4)

            def experts(g):
                if g:
                    dve.wait_ge(sc_pe, 4 + 4 * NE)
                    dve.wait_ge(g_pe, 2 * NE)
                for e in range(NE):
                    for c in range(2):
                        TS(sel[:, c, e, :], iot[:, g * P:(g + 1) * P], rank[:, c, e:e + 1], None, ALU.is_equal)
                        last = TS(selw[:, c, e, :], iot[:, g * P:(g + 1) * P], rank[:, c, e:e + 1],
                                  wex[:, c, e:e + 1], ALU.is_equal, ALU.mult)
                    last.then_inc(p_sel, 1)

                def gathered(E0):
                    for q in range(2):
                        dve.wait_ge(g_hi, 2 * E0 + q + 1)
                        TT(GL[:, 4 * q:4 * q + 4, :], PS[:, 5 + q, :].rearrange("p (k j) -> p k j", k=4),
                           GH[:, 4 * q:4 * q + 4, :].bitcast(F32), ALU.subtract).then_inc(g_lo, 1)

                def elo(E0, j):
                    dve.wait_ge(e_hi, NU * E0 + j + 1)
                    TT(EL[:, j % SPLIT, :], eraw[:, j % RAW, :], EH[:, j % SPLIT, :].bitcast(F32),
                       ALU.subtract).then_inc(e_lo, 1)

                def turned(E0, b):
                    dve.wait_ge(e_th, NB * E0 + b + 1)
                    TT(TL[:], PS[:, 2, 0:2 * P].rearrange("p (k j) -> p k j", k=2), TH[:].bitcast(F32),
                       ALU.subtract).then_inc(e_tl, 1)

                def expert(e, last):
                    E0 = g * NE + e
                    for j, (kind, b) in enumerate(ORDER):
                        if kind == 0 and b:
                            turned(E0, b - 1)
                        if kind == 1:
                            dve.wait_ge(e_silu, NB * E0 + b + 1)
                            dve.wait_ge(e_use, NU + NU * E0 + j + 1)
                            TT(mid[:], sil[:], PS[:, 1, 0:BLK], ALU.mult).then_inc(e_mid, 1)
                        if j + SPLIT < NU:
                            elo(E0, j + SPLIT)
                        if j == NU - 2:
                            turned(E0, NB - 1)
                    dve.wait_ge(e_use, NU + NU * E0 + NU)
                    dve.wait_ge(sc_pe, 4 * E0 + 4)
                    V_.tensor_copy(yexp[:, 512:D], PS[:, 4, :]).then_inc(y_ev, 1)
                    if not last:
                        elo(E0 + 1, 0)
                        gathered(E0 + 1)
                    for r in range(4):
                        if r == 2 and not last:
                            elo(E0 + 1, 1)
                        dve.wait_ge(sc_pe, 4 * E0 + r + 5)
                        for j in range(2):
                            f = 2 * r + j
                            ins = STT(X[:, f, L:TOK], PS[:, SCB[r], j * L:(j + 1) * L], mod[:, MCH + GATE2 * DK + f, 1:2],
                                      X[:, f, L:TOK], ALU.mult, ALU.add)
                        ins.then_inc(sc_ev, 1)
                    if not last:
                        for j in range(2, SPLIT):
                            elo(E0 + 1, j)

                for j in range(SPLIT):
                    elo(g * NE, j)
                gathered(g * NE)
                with dve.Fori(0, NE - 1) as e:
                    expert(e, False)
                expert(NE - 1, True)

            experts(0)
            with dve.If(dve.value_load(overi[0:1, 0:1], min_val=0, max_val=1) == 1):
                experts(1)
            dve.wait_ge(n_rt, 5)
            link(V_.reciprocal(rs[:, L:TOK], rs[:, L:TOK]))
            for k in range(DK):
                STT(X[:, k, L:TOK], X[:, k, L:TOK], gf[:, k:k + 1], rs[:, L:TOK], ALU.mult, ALU.mult).then_inc(o_ready, 1)

        @block.tensor
        def _(pe):
            MM, TR = nc.tensor.matmul, nc.tensor.transpose

            def mm3(o, wh, wl, xh, xl, first, last):
                MM(o, wh, xh, start=first, stop=False)
                MM(o, wh, xl, start=False, stop=False)
                return MM(o, wl, xh, start=False, stop=last)

            def ready(u):
                pe.wait_ge(lo_done, u + 1)

            def cols(s, k, j):
                a = k * BLK + j * P
                return slice(a, a + P)

            def features(s, banks, c0, xh, xl, ks=range(DK), wk=None):
                for j in range(2):
                    for n, k in enumerate(ks):
                        w = n if wk is None else wk + n
                        last = mm3(PS[:, banks + j, c0:TOK], WH[:, s, cols(s, w, j)], WL[:, s, cols(s, w, j)],
                                   xh[:, k, c0:TOK], xl[:, k, c0:TOK], n == 0, n == len(ks) - 1)
                return last

            def norm_sums(q):
                c0 = norm_c0[q]
                for k in range(DK):
                    pe.wait_ge(n_sq, 8 * q + k + 1)
                    MM(PS[:, 7, c0:TOK], ones[:], sq[:, k % 2, c0:TOK], start=k == 0, stop=k == DK - 1).then_inc(n_pe, 1)

            def mod_units(l, i):
                if l or not isinstance(i, int) or i:
                    pe.wait_ge(md_row, MTRIPS * l + i)
                for n in range(MRING):
                    pe.wait_ge(m_in[n], 16 * (MTRIPS * l + i + 1))
                    for k in range(DK):
                        last = MM(PS[0:2 * MRING, MODB, 0:BLK], svec[:, k, n, :], (mraw0, mraw1)[l][:, n, k * BLK:(k + 1) * BLK],
                                  start=n == 0 and k == 0, stop=n == MRING - 1 and k == DK - 1)
                    last.then_inc(md_pe, 1)

            def mod_turn(l, i):
                pe.wait_ge(md_row, MTRIPS * l + i + 1)
                if l or not isinstance(i, int) or i:
                    pe.wait_ge(md_out, MTRIPS * l + i)
                for j in range(2):
                    o = PS[:, MTB, 0:4 * MRING].rearrange("p (n j s) -> p n j s", n=MRING, j=2)[:, :, j, :]
                    last = MM(o, mrow[:, j * P:(j + 1) * P], ident[0:2 * MRING, 0:2 * MRING], start=True, stop=True)
                last.then_inc(md_tr, 1)

            def hyena_inputs(l):
                with pe.Fori(0, U_U // 2) as i:
                    for n in range(2):
                        ready(base[l]["u"] + 2 * i + n)
                        pe.wait_ge(evac, evb[l]["u"] + 2 * i + n - 1)
                        features(n, 2 * n, L * l, HH, HL).then_inc(unit_done, 1)
                pe.wait_ge(evac, evb[l]["qkv"])

            pe.wait_ge(setup_done, 3)
            pe.wait_ge(s_ready, MRING)
            conv_items = 0
            att_n = att_q = 0
            for l in range(2):
                b = base[l]
                c0 = 0 if l == 0 else L
                if l == 1:
                    pe.wait_ge(md_out, 2 * MTRIPS)
                    norm_sums(2)
                else:
                    mod_units(0, 0)
                pe.wait_ge(filt_in, 16 * N_FILT * (l + 1))
                MM(PS[0:64, 6, 0:L], fw1[:], posT[:], start=True, stop=True).then_inc(f_pe, 1)
                if l == 0:
                    mod_turn(0, 0)
                    mod_units(0, 1)
                pe.wait_ge(f_ac, 14 * l + 2)
                MM(PS[0:64, 6, 0:L], fw2[:], act1[:, 0, :], start=True, stop=True).then_inc(f_pe, 1)
                if l == 0:
                    mod_turn(0, 1)
                    mod_units(0, 2)
                pe.wait_ge(f_ac, 14 * l + 4)
                if l == 1:
                    pe.wait_ge(n_rt, 3)
                for o in range(2):
                    for pc in range(2):
                        last = MM(PS[:, TAPB[l] + 2 * o + pc, :], act1[:, 1, pc * P:(pc + 1) * P], fw3[:, o, :],
                                  start=True, stop=True)
                last.then_inc(f_pe, 1)
                if l == 0:
                    mod_turn(0, 2)
                    norm_sums(0)
                    pe.wait_ge(n_rt, 1)
                    pe.wait_ge(md_out, 3)
                else:
                    pe.wait_ge(n_lo, items_before[2] + 16)
                    hyena_inputs(1)
                pe.wait_ge(f_dv, 4 * l + 4)
                for q in range(10):
                    if q >= 8:
                        pe.wait_ge(f_ac, 14 * l + 4 + q - 7)
                    o, g = q // 5, q % 5
                    for c in range(2):
                        last = MM(PS[0:BINS, q % 8, :], dftk[:, c, g * BINS:(g + 1) * BINS], taps[:, o, c, :],
                                  start=c == 0, stop=c == 1)
                    last.then_inc(f_pe, 1)
                if l == 0:
                    pe.wait_ge(f_ac, 10)
                    with pe.Fori(3, MTRIPS) as i:
                        mod_units(0, i)
                        mod_turn(0, i)
                    pe.wait_ge(n_lo, 16)
                pe.wait_ge(f_ac, 14 * l + 14)
                if l == 0:
                    hyena_inputs(0)
                for o in range(2):
                    for s in range(l, 2):
                        n = conv_items
                        if o:
                            pe.wait_ge(y_z, n - (2 - l) + 1)
                        if n:
                            pe.wait_ge(y_vt, n)
                        for c in range(2):
                            for ch in range(4):
                                last = TR(PS[:, 4 + c, ch * P:(ch + 1) * P], U[:, ch, s * L + c * P:s * L + (c + 1) * P], ident[:])
                        last.then_inc(y_t, 1)
                        pe.wait_ge(y_vt, n + 1)
                        if n:
                            pe.wait_ge(y_y, n)
                        for g in range(4):
                            for c in range(2):
                                last = MM(PS[0:BINS, g, :], dftf[:, c, g * BINS:(g + 1) * BINS], VT[:, c, :], start=c == 0, stop=c == 1)
                        last.then_inc(y_d, 1)
                        pe.wait_ge(y_y, n + 1)
                        if n:
                            pe.wait_ge(y_z, n)
                        for ch in range(4):
                            for g in range(4):
                                last = MM(PS[:, 6 + ch // 2, (ch % 2) * L:(ch % 2 + 1) * L], Y[:, g, ch * P:(ch + 1) * P], dfti[:, g, :],
                                          start=g == 0, stop=g == 3)
                        last.then_inc(y_i, 1)
                        conv_items += 1
                for n in range(QKV_U):
                    ready(b["qkv"] + n)
                    pe.wait_ge(evac, evb[l]["qkv"] + n - 1)
                    if n == 0:
                        pe.wait_ge(y_z, conv_items)
                    if n < 4:
                        last = features(n % 2, 2 * (n % 2), c0 if n < 2 else 0, HH, HL)
                    else:
                        for tc in range(4):
                            o = PS[:, 2 * (n % 2) + tc // 2, (tc % 2) * BLK:(tc % 2 + 1) * BLK]
                            for k in range(DK):
                                w = slice(k * BLK, (k + 1) * BLK)
                                x_ = slice(tc * P, (tc + 1) * P)
                                MM(o, HH[:, k, x_], WH[:, n % 2, w], start=k == 0, stop=False)
                                MM(o, HL[:, k, x_], WH[:, n % 2, w], start=False, stop=False)
                                last = MM(o, HH[:, k, x_], WL[:, n % 2, w], start=False, stop=k == DK - 1)
                    last.then_inc(unit_done, 1)
                pe.wait_ge(bias_in, 16 * 17 * (l + 1))
                for h in range(HEADS):
                    if h >= 4:
                        pe.wait_ge(a_bias, HEADS * l + h - 3)
                    MM(PS[:, 4 + h % 4, 0:6 * GRID], flip[:], bias[:, h, :], start=True, stop=True).then_inc(a_flip, 1)
                pe.wait_ge(evac, evb[l]["merge"])
                pe.wait_ge(a_bias, HEADS * (l + 1))

                def scores(n, qc, h):
                    r = slice(HD * (h % 2), HD * (h % 2) + HD)
                    width = TOK if qc >= 2 else L
                    if n >= 2:
                        pe.wait_ge(a_sc, n - 1)
                    MM(PS[:, n % 2, 0:width], QK[r, h // 2, qc * P:(qc + 1) * P], QK[r, 4 + h // 2, 0:width],
                       start=True, stop=True).then_inc(a_s, 1)

                def turn(n, qc):
                    pe.wait_ge(a_ex, n + 1)
                    if n >= 2:
                        pe.wait_ge(a_pt, n - 1)
                    for kc in range(4 if qc >= 2 else 2):
                        last = TR(PS[:, 2 + n % 2, kc * P:(kc + 1) * P], S[:, n % 2, kc * P:(kc + 1) * P], ident[:])
                    last.then_inc(a_t, 1)

                def attend(n, qc, h):
                    pe.wait_ge(a_pt, n + 1)
                    nk = 4 if qc >= 2 else 2
                    for kc in range(nk):
                        last = MM(PS[:, 4 + qc % 2, h * HD:(h + 1) * HD], PT[:, n % 2, kc * P:(kc + 1) * P],
                                  V[:, kc, h * HD:(h + 1) * HD], start=kc == 0, stop=kc == nk - 1)
                    last.then_inc(a_o, 1)

                for qc in range(2 * l, 4):
                    n0 = att_n
                    for h in range(HEADS + 2):
                        if h < HEADS:
                            scores(n0 + h, qc, h)
                        if 1 <= h <= HEADS:
                            turn(n0 + h - 1, qc)
                        if h >= 2:
                            attend(n0 + h - 2, qc, h - 2)
                    att_n += HEADS
                    pe.wait_ge(a_on, att_q + 1)
                    for c in range(4):
                        last = TR(PS[:, 6 + qc % 2, c * P:(c + 1) * P], OT[:, qc, c * P:(c + 1) * P], ident[:])
                    last.then_inc(a_ot, 1)
                    att_q += 1
                pe.wait_ge(a_lo, att_q)
                with pe.Fori(0, 2) as i:
                    for n in range(6):
                        pair, kind = n // 3, n % 3
                        ready(b["merge"] + 6 * i + n)
                        if kind == 0:
                            pe.wait_ge(m_sig, 2 * (4 * l + 2 * i + pair) + 1)
                        if kind == 2:
                            pe.wait_ge(m_sum, 4 * l + 2 * i + pair + 1)
                        if kind < 2:
                            last = features(n % 2, 2 * kind, c0, HH, HL)
                        else:
                            features(n % 2, 4, c0, OAH, OAL, range(4), 0)
                            last = features(n % 2, 6, c0, OHH, OHL, range(4), 4)
                        last.then_inc(unit_done, 1)
                pe.wait_ge(m_lo, 4 * l + 5)
                for n in range(WO_U):
                    ready(b["wo"] + n)
                    pe.wait_ge(evac, evb[l]["wo"] + n - 1)
                    features(n % 2, 2 * (n % 2), c0, MH, ML).then_inc(unit_done, 1)
                norm_sums(2 * l + 1)
                if l == 0:
                    pe.wait_ge(n_lo, items_before[1] + 16)
                    with pe.Fori(0, NB) as i:
                        ready(b["up"] + 2 * i)
                        pe.wait_ge(up_silu, i + 1)
                        features(0, 0, 0, HH, HL).then_inc(unit_done, 1)
                        ready(b["up"] + 2 * i + 1)
                        pe.wait_ge(up_mid, i + 1)
                        features(1, 2, 0, HH, HL).then_inc(unit_done, 1)
                    pe.wait_ge(up_lo, NB + 1)
                    with pe.Fori(0, DK // 2) as i:
                        for mm in range(2):
                            pe.wait_ge(evac, evb[l]["down"] + 2 * i + mm - 1)
                            for s in range(2):
                                ready(b["down"] + 4 * i + 2 * mm + s)
                                for n in range(11):
                                    w = slice(n * P, (n + 1) * P)
                                    k = 11 * s + n
                                    last = mm3(PS[:, mm, :], WH[:, s, w], WL[:, s, w], MDH[:, k, :], MDL[:, k, :],
                                               k == 0, k == FK - 1)
                                last.then_inc(unit_done, 1)
                                if s == 0:
                                    mod_units(1, 2 * i + mm)
                            mod_turn(1, 2 * i + mm)
            pe.wait_ge(n_lo, 56)
            pe.wait_ge(r_split, 2)
            for c in range(2):
                x_ = slice(c * P, (c + 1) * P)
                for k in range(DK):
                    MM(PS[:, c, 0:NE], RH[:, k, x_], RTH[:, k, :], start=k == 0, stop=False)
                    MM(PS[:, c, 0:NE], RL[:, k, x_], RTH[:, k, :], start=False, stop=False)
                    last = MM(PS[:, c, 0:NE], RH[:, k, x_], RTL[:, k, :], start=False, stop=k == DK - 1)
                last.then_inc(r_pe, 1)
            pe.wait_ge(r_mask, 4)
            MM(PS[:, 4, 0:NE], tri[:], msk[:, 0, :], start=True, stop=True)
            MM(PS[:, 5, 0:NE], tri[:], msk[:, 1, :], start=True, stop=False)
            MM(PS[:, 5, 0:NE], ones[:], msk[:, 0, :], start=False, stop=True)
            MM(PS[:, 6, 0:NE], ones[:], msk[:, 0, :], start=True, stop=False)
            MM(PS[:, 6, 0:NE], ones[:], msk[:, 1, :], start=False, stop=True).then_inc(r_rank, 1)
            for c in range(2):
                for hf in range(2):
                    for k in range(4):
                        last = TR(PS[:, 2 * c + hf, k * P:(k + 1) * P], mo_h[:, 4 * hf + k, c * P:(c + 1) * P], ident[:])
                    last.then_inc(h_tr, 1)
            pe.wait_ge(h_ev, 4)

            def experts(g):
                if g:
                    pe.wait_ge(sc_ev, 4 + 4 * NE)
                for q in range(4):
                    pe.wait_ge(p_sel, NE * g + 2 * q + 2)
                    for j in range(2):
                        for c in range(2):
                            last = TR(PS[:, q, j * L + c * P:j * L + (c + 1) * P], selw[:, c, 2 * q + j, :], ident[:])
                    last.then_inc(p_tr, 1)
                pe.wait_ge(p_selT, 4 * g + 4)
                if g == 0:
                    pe.sem_inc(e_use, NU)
                    pe.sem_inc(sc_pe, 4)

                def gather(e):
                    for q in range(2):
                        for k in range(4):
                            for c in range(2):
                                ins = MM(PS[:, 5 + q, k * P:(k + 1) * P], mo_ht[:, c, (4 * q + k) * P:(4 * q + k + 1) * P],
                                         of_expert(sel[:, c], e), start=c == 0, stop=c == 1)
                        ins.then_inc(g_pe, 1)

                def of_expert(ap, e):
                    return ap[:, e, :] if isinstance(e, int) else ap[:, bass.ds(e, 1), :].rearrange("p e j -> p (e j)")

                def up(E0, kind, b):
                    j = POS[(kind, b)]
                    pe.wait_ge(e_lo, NU + NU * E0 + j + 1)
                    for k in range(DK):
                        w = slice(k * BLK, (k + 1) * BLK)
                        o = PS[:, kind, 0:BLK]
                        MM(o, GH[:, k, :], EH[:, j % SPLIT, w], start=k == 0, stop=False)
                        MM(o, GH[:, k, :], EL[:, j % SPLIT, w], start=False, stop=False)
                        ins = MM(o, GL[:, k, :], EH[:, j % SPLIT, w], start=False, stop=k == DK - 1)
                    ins.then_inc(e_use, 1)

                def turn_mid(E0, b):
                    pe.wait_ge(e_mid, NB * E0 + b + 2)
                    for k in range(2):
                        ins = TR(PS[:, 2, k * P:(k + 1) * P], mid[:, k * P:(k + 1) * P], ident[:])
                    ins.then_inc(e_tr, 1)

                def down(E0, b):
                    j = POS[(2, b)]
                    pe.wait_ge(e_tl, NB * E0 + b + 1)
                    pe.wait_ge(e_lo, NU + NU * E0 + j + 1)
                    for hf in range(2):
                        for k in range(2):
                            w = slice(k * D + hf * 512, k * D + (hf + 1) * 512)
                            o = PS[:, 3 + hf, :]
                            MM(o, TH[:, k, :], EH[:, j % SPLIT, w], start=b == 0 and k == 0, stop=False)
                            MM(o, TH[:, k, :], EL[:, j % SPLIT, w], start=False, stop=False)
                            ins = MM(o, TL[:, k, :], EH[:, j % SPLIT, w], start=False, stop=b == NB - 1 and k == 1)
                    ins.then_inc(e_use, 1)

                def expert(e, last):
                    E0 = g * NE + e
                    pe.wait_ge(g_lo, 2 * E0 + 2)
                    for b in range(NB):
                        if b:
                            pe.wait_ge(e_silu, NB * E0 + b)
                        else:
                            pe.wait_ge(sc_ev, 4 * E0 + 2)
                        up(E0, 0, b)
                        if b == 0:
                            pe.wait_ge(sc_ev, 4 * E0 + 4)
                        else:
                            turn_mid(E0, b - 1)
                            pe.wait_ge(e_mid, NB * E0 + b + 1)
                        up(E0, 1, b)
                        if b:
                            down(E0, b - 1)
                    turn_mid(E0, NB - 1)
                    down(E0, NB - 1)
                    if not last:
                        gather(e + 1)
                    pe.wait_ge(y_ev, 2 * E0 + 2)
                    for r in range(4):
                        for j in range(2):
                            f = 2 * r + j
                            ins = MM(PS[:, SCB[r], j * L:(j + 1) * L], yexp[:, f * P:(f + 1) * P],
                                     of_expert(selT, e), start=True, stop=True)
                        ins.then_inc(sc_pe, 1)

                pe.wait_ge(sc_ev, 4)
                gather(0)
                with pe.Fori(0, NE - 1) as e:
                    expert(e, False)
                expert(NE - 1, True)

            experts(0)
            pe.wait_ge(flag_ready, 1)
            with pe.If(pe.value_load(overi[0:1, 0:1], min_val=0, max_val=1) == 1):
                experts(1)
            norm_sums(4)


class Chain:

    def __init__(self, eng, sem):
        self.eng, self.sem, self.n, self.i, self.per = eng, sem, 0, None, 0

    def enter(self, i, per, trips):
        self.i, self.per, self.trips, self.start = i, per, trips, self.n

    def exit(self):
        assert self.n - self.start == self.per, (self.n - self.start, self.per)
        self.i, self.n = None, self.start + self.per * self.trips

    def link(self, ins):
        ins.then_inc(self.sem, 1)
        self.n += 1
        self.eng.wait_ge(self.sem, self.n if self.i is None else self.n + self.per * self.i)


def tables():
    pos = np.arange(L, dtype=np.float32)
    bands = np.linspace(1e-4, 15.0, 16, dtype=np.float32)
    ang = (np.float32(2.0 * math.pi / L) * pos[:, None] * bands[None, :]).astype(np.float32)
    feats = np.concatenate([(pos / (L - 1))[:, None], np.cos(ang), -np.sin(ang)], axis=-1)
    dist = np.abs(pos - L // 2) * np.float32(2.0 / L)
    rates = np.abs(np.linspace(math.log(1e-2) / 1.5, math.log(1e-2) / 0.3, 2 * HY_W, dtype=np.float32))
    decay = np.exp(-dist[:, None] * rates[None, :]) + 0.05
    j = np.arange(L)[:, None].astype(np.float64)
    k = np.arange(2 * BINS)[None, :]
    w = 2 * np.pi / NFFT
    re, im = np.cos(w * j * k), -np.sin(w * j * k)
    nyq = np.cos(np.pi * j[:, 0])
    imn = im.copy()
    imn[:, 0] = nyq
    ren = re[:, :BINS].copy()
    ren[:, 0] = nyq
    fwd = np.concatenate([re, imn], axis=1)
    fil = np.concatenate([re, im * (k > 0), ren], axis=1)
    n = (np.arange(L) + L // 2)[None, :]
    kk = np.arange(2 * BINS)[:, None]
    ire = np.where(kk == 0, 1.0, 2 * np.cos(w * kk * n)) / NFFT
    iim = np.where(kk == 0, np.cos(np.pi * n), -2 * np.sin(w * kk * n)) / NFFT
    inv = np.concatenate([ire, iim], axis=0).reshape(4, BINS, L)
    c = np.arange(P) % GRID
    start = np.clip(c - WIN // 2, 0, GRID - WIN)[:, None]
    col = np.arange(GRID)[None, :]
    mask = np.where((col >= start) & (col < start + WIN), 0.0, NEG)
    f = np.float32
    chunks = lambda a: np.ascontiguousarray(a.reshape(2, P, -1).transpose(1, 0, 2)).astype(f)
    return {
        "posT": np.ascontiguousarray(feats.T).astype(f),
        "decay": np.ascontiguousarray(decay.reshape(2, P, 2, HY_W).transpose(1, 0, 2, 3)).astype(f),
        "dftf": chunks(fwd), "dftk": chunks(fil),
        "dfti": np.ascontiguousarray(inv.transpose(1, 0, 2)).astype(f),
        "mask": np.tile(mask, (1, 6)).astype(f),
        "ident": np.eye(P, dtype=f),
        "flip": np.kron(np.eye(2), np.eye(GRID)[::-1]).astype(f),
        "tri": np.triu(np.ones((P, P), f), 1),
        "iota": np.tile(np.arange(L, dtype=f), (P, 1)),
    }


def kernel(**inputs):
    import concourse.bacc as bacc
    from concourse.bass_utils import run_bass_kernel_spmd as run

    a = {k: np.asarray(v) for k, v in inputs.items()}

    def features_first(v, lead):
        v = v.reshape(*v.shape[:-1], v.shape[-1] // P, P)
        return np.moveaxis(v, -1, 0)

    arrays = {
        "xT": a["x"][0].T, "ctxT": a["ctx"][0].T,
        "cc": np.moveaxis(features_first(np.stack([a["c_ctx"], a["c"][0]]), 1), 1, 2),
        "w_mod": a["w_mod"], "b_mod": features_first(a["b_mod"], 1),
        "norm1_g": features_first(a["norm1_g"], 1), "norm2_g": features_first(a["norm2_g"], 1),
        "final_g": features_first(a["final_g"], 0),
        "w_in": a["w_in"], "rpb": a["rpb"],
        "hy_conv_w": features_first(a["hy_conv_w"], 2), "hy_conv_b": features_first(a["hy_conv_b"], 1),
        "hy_w1": a["hy_w1"], "hy_w2": a["hy_w2"], "hy_w3": a["hy_w3"],
        "fvec": np.stack([a["hy_b1"], a["hy_freq"][:, 0], a["hy_b2"], a["hy_freq"][:, 1]], axis=-1),
        "hy_bias": features_first(a["hy_bias"], 2),
        "w_opab": np.concatenate([a["w_o"], np.concatenate([a["w_pa"], a["w_pb"]], axis=1)], axis=2),
        "ffn_w1": a["ffn_w1"][0], "ffn_w3": a["ffn_w3"][0], "ffn_w2": a["ffn_w2"][0],
        "moe_router": np.moveaxis(a["moe_router"][0].reshape(DK, P, NE), 1, 0),
        "moe_w1": a["moe_w1"][0].reshape(NE * D, FF), "moe_w3": a["moe_w3"][0].reshape(NE * D, FF),
        "moe_w2": a["moe_w2"][0].reshape(NE * FF, D),
        **tables(),
    }
    arrays = {k: np.ascontiguousarray(v) for k, v in arrays.items()}
    nc = bacc.Bacc("TRN2", target_bir_lowering=False, num_devices=1)
    t = {k: nc.dram_tensor("in_" + k, v.shape, mybir.dt.from_np(v.dtype), kind="ExternalInput").ap() for k, v in arrays.items()}
    out = nc.dram_tensor("out_features", (D, L), F32, kind="ExternalOutput").ap()
    build(nc, t, out)
    r = run(nc, [{"in_" + k: v for k, v in arrays.items()}], core_ids=[0])
    return np.ascontiguousarray(r.results[0]["out_features"].T)[None]
```
